# Optimizing a Trainium2 kernel written in Bass

```python
import math
import jax
import jax.numpy as jnp
from jax import lax
import numpy as np

D_MODEL = 1024
BATCH = 1
SEQ = 256
DEPTH = 2

N_EVEN = (DEPTH + 1) // 2
N_ODD = DEPTH // 2
NORM_EPS = 1e-6

HG_DK = 128
HG_HEADS = D_MODEL // HG_DK
HG_WIDTH = HG_HEADS * HG_DK
HG_CHUNK = 64

SSM_HEADDIM = 64
SSM_HEADS = D_MODEL // SSM_HEADDIM
SSM_WIDTH = SSM_HEADS * SSM_HEADDIM
SSM_GROUPS = 2
SSM_STATE = 128
SSM_CONV = 4
SSM_CHUNK = 64
SSM_XBC = SSM_WIDTH + 2 * SSM_GROUPS * SSM_STATE

IN_SIZES = (HG_WIDTH, HG_WIDTH, HG_WIDTH, HG_WIDTH, SSM_WIDTH, SSM_XBC, SSM_HEADS)
IN_COLS = 4 * HG_WIDTH + SSM_WIDTH + SSM_XBC + SSM_HEADS
MIX_WIDTH = HG_WIDTH + SSM_WIDTH

RW_HEADSIZE = 64
RW_HEADS = D_MODEL // RW_HEADSIZE
RW_DECAY_LORA = 64
RW_AAA_LORA = 64
RW_GATE_LORA = 128
RW_GN_EPS = 64e-5

N_EXPERTS = 16
N_EXPERT_GROUPS = 4
EXPERTS_PER_GROUP = N_EXPERTS // N_EXPERT_GROUPS
TOP_K = 2
D_EXPERT = D_MODEL // 2

kernel_name = "hybrid_hgrn2_ssd_rwkv7_grouped_moe"

def group_rms_norm(x, w, n_groups):
    shp = x.shape
    xg = x.astype(jnp.float32).reshape(shp[:-1] + (n_groups, shp[-1] // n_groups))
    y = xg * lax.rsqrt(jnp.mean(xg * xg, axis=-1, keepdims=True) + NORM_EPS)
    return (y.reshape(shp) * w.astype(jnp.float32)).astype(x.dtype)

def rms_norm(x, w):
    return group_rms_norm(x, w, 1)

def modulate(h, shift, scale):
    return h * (1.0 + scale[:, None, :]) + shift[:, None, :]

def causal_dwconv(x, w, b):
    k = w.shape[0]
    y = lax.conv_general_dilated(x, w[:, None, :].astype(x.dtype), window_strides=(1,),
                                 padding=[(k - 1, 0)], dimension_numbers=('NWC', 'WIO', 'NWC'),
                                 feature_group_count=x.shape[-1])
    return y + b

def segsum(x):
    t = x.shape[-1]
    idx = jnp.arange(t)
    xe = jnp.broadcast_to(x[..., :, None], x.shape + (t,))
    cs = jnp.cumsum(jnp.where(idx[:, None] > idx[None, :], xe, 0.0), axis=-2)
    return jnp.where(idx[:, None] >= idx[None, :], cs, -jnp.inf)

def hgrn2_chunk_scan(q, k, v, log_f):
    bsz, s_len, h, dk = q.shape
    dv = v.shape[-1]
    nc = s_len // HG_CHUNK

    def to_chunks(t):
        return t.reshape(bsz, nc, HG_CHUNK, h, t.shape[-1]).transpose(1, 0, 3, 2, 4)

    causal = jnp.tril(jnp.ones((HG_CHUNK, HG_CHUNK), dtype=bool))

    def step(state, inp):
        qi, ki, vi, gi = inp
        b = jnp.cumsum(gi, axis=2)
        b_last = b[:, :, -1:, :]
        o_inter = jnp.einsum('bhtk,bhkv->bhtv', qi * jnp.exp(b), state)
        diff = b[:, :, :, None, :] - b[:, :, None, :, :]
        decay = jnp.exp(jnp.where(causal[:, :, None], diff, -jnp.inf))
        scores = jnp.einsum('bhtk,bhtsk,bhsk->bhts', qi, decay, ki)
        o_intra = jnp.einsum('bhts,bhsv->bhtv', scores, vi)
        new_state = (jnp.exp(b_last[:, :, 0, :])[..., None] * state
                     + jnp.einsum('bhsk,bhsv->bhkv', ki * jnp.exp(b_last - b), vi))
        return new_state, o_inter + o_intra

    s0 = jnp.zeros((bsz, h, dk, dv), jnp.float32)
    _, o = lax.scan(step, s0, (to_chunks(q), to_chunks(k), to_chunks(v), to_chunks(log_f)))
    return o.transpose(1, 0, 3, 2, 4).reshape(bsz, s_len, h, dv)

def ssd_chunk_scan(x, dt, a, bm, cm):
    bsz, s_len, h, p = x.shape
    g, n = bm.shape[-2:]
    j = h // g
    nc = s_len // SSM_CHUNK
    l = SSM_CHUNK
    xc = (x * dt[..., None]).reshape(bsz, nc, l, g, j, p)
    da = (dt * a).reshape(bsz, nc, l, g, j).transpose(0, 3, 4, 1, 2)
    bc = bm.reshape(bsz, nc, l, g, n)
    cc = cm.reshape(bsz, nc, l, g, n)
    a_cs = jnp.cumsum(da, axis=-1)
    lmat = jnp.exp(segsum(da))
    cb = jnp.einsum('bclgn,bcsgn->bgcls', cc, bc)
    y_diag = jnp.einsum('bgjcls,bcsgjp->bclgjp', cb[:, :, None] * lmat, xc)
    decay_states = jnp.exp(a_cs[..., -1:] - a_cs).transpose(0, 3, 4, 1, 2)
    states = jnp.einsum('bclgn,bclgjp->bcgjpn', bc, xc * decay_states[..., None])
    chunk_decay = jnp.exp(segsum(jnp.pad(a_cs[..., -1], ((0, 0), (0, 0), (0, 0), (1, 0)))))
    states = jnp.concatenate([jnp.zeros_like(states[:, :1]), states], axis=1)
    states = jnp.einsum('bgjzc,bcgjpn->bzgjpn', chunk_decay, states)[:, :-1]
    state_decay_out = jnp.exp(a_cs).transpose(0, 3, 4, 1, 2)
    y_off = jnp.einsum('bclgn,bcgjpn->bclgjp', cc, states) * state_decay_out[..., None]
    return (y_diag + y_off).reshape(bsz, s_len, h, p)

def hgrn2_ssd_mixer(h, lb, w_in, hg_norm, conv_w, conv_b, dt_bias, a_log, d_skip, ssm_norm, w_out):
    bsz, s_len, _ = h.shape
    f32 = jnp.float32
    proj = jnp.einsum('bsd,de->bse', h, w_in)
    bounds = [sum(IN_SIZES[:m]) for m in range(1, len(IN_SIZES))]
    q, f_raw, i_val, g_out, z, xbc, dt_raw = jnp.split(proj, bounds, axis=-1)
    f = lb + (1.0 - lb) * jax.nn.sigmoid(f_raw.astype(f32))
    hg = lambda t: t.astype(f32).reshape(bsz, s_len, HG_HEADS, HG_DK)
    o_a = hgrn2_chunk_scan(hg(q), hg(1.0 - f), hg(i_val), hg(jnp.log(f)))
    o_a = group_rms_norm(o_a.reshape(bsz, s_len, HG_WIDTH), hg_norm, HG_HEADS) * jax.nn.silu(g_out.astype(f32))
    xbc = jax.nn.silu(causal_dwconv(xbc, conv_w, conv_b))
    xs, bm, cm = jnp.split(xbc, [SSM_WIDTH, SSM_WIDTH + SSM_GROUPS * SSM_STATE], axis=-1)
    dt = jax.nn.softplus(dt_raw.astype(f32) + dt_bias.astype(f32))
    a = -jnp.exp(a_log.astype(f32))
    xs_h = xs.astype(f32).reshape(bsz, s_len, SSM_HEADS, SSM_HEADDIM)
    y = ssd_chunk_scan(xs_h, dt, a,
                       bm.astype(f32).reshape(bsz, s_len, SSM_GROUPS, SSM_STATE),
                       cm.astype(f32).reshape(bsz, s_len, SSM_GROUPS, SSM_STATE))
    y = y + d_skip.astype(f32)[:, None] * xs_h
    o_b = group_rms_norm(y.reshape(bsz, s_len, SSM_WIDTH) * jax.nn.silu(z.astype(f32)), ssm_norm, SSM_GROUPS)
    o = jnp.concatenate([o_a, o_b], axis=-1).astype(h.dtype)
    return jnp.einsum('bse,ed->bsd', o, w_out).astype(h.dtype)

def rwkv7_scan(r, w, k, v, kk, a):
    def step(state, inp):
        r_t, w_t, k_t, v_t, kk_t, a_t = inp
        sa = jnp.einsum('bhvk,bhk->bhv', state, -kk_t)
        state = (state * w_t[:, :, None, :] + sa[..., None] * (kk_t * a_t)[:, :, None, :]
                 + v_t[..., None] * k_t[:, :, None, :])
        return state, jnp.einsum('bhvk,bhk->bhv', state, r_t)

    bsz, _, h, n = r.shape
    seq_first = tuple(t.transpose(1, 0, 2, 3) for t in (r, w, k, v, kk, a))
    s0 = jnp.zeros((bsz, h, n, n), jnp.float32)
    _, y = lax.scan(step, s0, seq_first)
    return y.transpose(1, 0, 2, 3)

def rwkv7_mixer(h, mu, w_rkv, w_dec0, w_dec1, w_dec2, a0, a1, a2, g1, g2, k_k, k_a, r_k, ln_w, ln_b, w_o):
    bsz, s_len, d = h.shape
    f32 = jnp.float32
    xx = jnp.pad(h[:, :-1], ((0, 0), (1, 0), (0, 0))) - h
    mixed = h[None] + xx[None] * mu[:, None, None, :]
    r, k, v = jnp.einsum('ibsd,ide->ibse', mixed[:3], w_rkv)
    xw, xa, xg = mixed[3], mixed[4], mixed[5]
    w_log = -jax.nn.softplus(-(w_dec0 + jnp.tanh(xw @ w_dec1) @ w_dec2).astype(f32)) - 0.5
    decay = jnp.exp(-jnp.exp(w_log))
    a = jax.nn.sigmoid((a0 + (xa @ a1) @ a2).astype(f32))
    g = jax.nn.sigmoid(xg @ g1) @ g2
    heads = lambda t: t.astype(f32).reshape(bsz, s_len, RW_HEADS, RW_HEADSIZE)
    r_h, v_h, w_h, a_h = heads(r), heads(v), heads(decay), heads(a)
    kk = heads(k * k_k)
    kk = kk / jnp.maximum(jnp.sqrt(jnp.sum(kk * kk, axis=-1, keepdims=True)), 1e-12)
    k_h = heads(k) * (1.0 + (a_h - 1.0) * k_a.astype(f32).reshape(RW_HEADS, RW_HEADSIZE))
    o = rwkv7_scan(r_h, w_h, k_h, v_h, kk, a_h)
    mean = jnp.mean(o, axis=-1, keepdims=True)
    var = jnp.mean(jnp.square(o - mean), axis=-1, keepdims=True)
    o = ((o - mean) * lax.rsqrt(var + RW_GN_EPS) * ln_w.astype(f32).reshape(RW_HEADS, RW_HEADSIZE)
         + ln_b.astype(f32).reshape(RW_HEADS, RW_HEADSIZE))
    o = o + jnp.sum(r_h * k_h * r_k.astype(f32), axis=-1, keepdims=True) * v_h
    o = (o.reshape(bsz, s_len, d) * g).astype(h.dtype)
    return (o @ w_o).astype(h.dtype)

def grouped_moe(h, router_w, router_b, w1, w3, w2):
    bsz, s_len, _ = h.shape
    logits = jnp.einsum('bsd,de->bse', h, router_w).astype(jnp.float32) + router_b.astype(jnp.float32)
    probs = jax.nn.softmax(logits, axis=-1)
    grouped = probs.reshape(bsz, s_len, N_EXPERT_GROUPS, EXPERTS_PER_GROUP)
    group_score = jnp.sum(lax.top_k(grouped, TOP_K)[0], axis=-1)
    group_mask = jax.nn.one_hot(jnp.argmax(group_score, axis=-1), N_EXPERT_GROUPS, dtype=bool)
    masked = jnp.where(group_mask[..., None], grouped, -1.0).reshape(bsz, s_len, N_EXPERTS)
    top_w, top_i = lax.top_k(masked, TOP_K)
    top_w = top_w / jnp.sum(top_w, axis=-1, keepdims=True)
    gates = jnp.sum(jax.nn.one_hot(top_i, N_EXPERTS, dtype=jnp.float32) * top_w[..., None], axis=-2)
    hidden = jax.nn.silu(jnp.einsum('bsd,edf->bsef', h, w1)) * jnp.einsum('bsd,edf->bsef', h, w3)
    hidden = hidden * gates.astype(hidden.dtype)[..., None]
    return jnp.einsum('bsef,efd->bsd', hidden, w2).astype(h.dtype)

def setup_inputs(seed: int = 0) -> dict:
    key = jax.random.key(seed)
    ks = iter(jax.random.split(key, 64))
    f32 = jnp.float32
    nrm = lambda shape, scale: jax.random.normal(next(ks), shape, f32) * scale
    uni = lambda shape, lo, hi: jax.random.uniform(next(ks), shape, f32, lo, hi)
    d = D_MODEL
    x = nrm((BATCH, SEQ, d), 1.0)
    c = nrm((BATCH, d), 1.0)
    mod_w = nrm((DEPTH, d, 6 * d), 0.5 * d ** -0.5)
    mod_b = nrm((DEPTH, 6 * d), 0.02)
    norm_w = 1.0 + nrm((DEPTH, 2, d), 0.02)
    hg_lb_logits = nrm((DEPTH + 1, HG_WIDTH), 1.0)
    ev_w_in = nrm((N_EVEN, d, IN_COLS), d ** -0.5)
    ev_hg_norm = 1.0 + nrm((N_EVEN, HG_WIDTH), 0.02)
    ev_conv_w = nrm((N_EVEN, SSM_CONV, SSM_XBC), SSM_CONV ** -0.5)
    ev_conv_b = nrm((N_EVEN, SSM_XBC), 0.02)
    dt0 = jnp.exp(uni((N_EVEN, SSM_HEADS), math.log(1e-3), math.log(1e-1)))
    ev_dt_bias = dt0 + jnp.log(-jnp.expm1(-dt0))
    ev_a_log = jnp.log(uni((N_EVEN, SSM_HEADS), 1.0, 16.0))
    ev_d_skip = 1.0 + nrm((N_EVEN, SSM_HEADS), 0.1)
    ev_ssm_norm = 1.0 + nrm((N_EVEN, SSM_WIDTH), 0.02)
    ev_w_out = nrm((N_EVEN, MIX_WIDTH, d), MIX_WIDTH ** -0.5)
    od_mu = uni((N_ODD, 6, d), 0.0, 1.0)
    od_w_rkv = nrm((N_ODD, 3, d, d), d ** -0.5)
    od_w_dec0 = uni((N_ODD, d), -6.0, 0.0)
    od_w_dec1 = nrm((N_ODD, d, RW_DECAY_LORA), d ** -0.5)
    od_w_dec2 = nrm((N_ODD, RW_DECAY_LORA, d), 0.5 * RW_DECAY_LORA ** -0.5)
    od_a0 = nrm((N_ODD, d), 0.5)
    od_a1 = nrm((N_ODD, d, RW_AAA_LORA), d ** -0.5)
    od_a2 = nrm((N_ODD, RW_AAA_LORA, d), 0.5 * RW_AAA_LORA ** -0.5)
    od_g1 = nrm((N_ODD, d, RW_GATE_LORA), d ** -0.5)
    od_g2 = nrm((N_ODD, RW_GATE_LORA, d), RW_GATE_LORA ** -0.5)
    od_k_k = 0.85 + nrm((N_ODD, d), 0.05)
    od_k_a = 1.0 + nrm((N_ODD, d), 0.05)
    od_r_k = nrm((N_ODD, RW_HEADS, RW_HEADSIZE), 0.1)
    od_ln_w = 1.0 + nrm((N_ODD, d), 0.02)
    od_ln_b = nrm((N_ODD, d), 0.02)
    od_w_o = nrm((N_ODD, d, d), d ** -0.5)
    router_w = nrm((d, N_EXPERTS), d ** -0.5)
    router_b = nrm((N_EXPERTS,), 0.01)
    moe_w1 = nrm((DEPTH, N_EXPERTS, d, D_EXPERT), d ** -0.5)
    moe_w3 = nrm((DEPTH, N_EXPERTS, d, D_EXPERT), d ** -0.5)
    moe_w2 = nrm((DEPTH, N_EXPERTS, D_EXPERT, d), D_EXPERT ** -0.5)
    final_norm_w = 1.0 + nrm((d,), 0.02)
    return {"x": x, "c": c, "mod_w": mod_w, "mod_b": mod_b, "norm_w": norm_w,
            "hg_lb_logits": hg_lb_logits, "ev_w_in": ev_w_in, "ev_hg_norm": ev_hg_norm,
            "ev_conv_w": ev_conv_w, "ev_conv_b": ev_conv_b, "ev_dt_bias": ev_dt_bias,
            "ev_a_log": ev_a_log, "ev_d_skip": ev_d_skip, "ev_ssm_norm": ev_ssm_norm,
            "ev_w_out": ev_w_out, "od_mu": od_mu, "od_w_rkv": od_w_rkv, "od_w_dec0": od_w_dec0,
            "od_w_dec1": od_w_dec1, "od_w_dec2": od_w_dec2, "od_a0": od_a0, "od_a1": od_a1,
            "od_a2": od_a2, "od_g1": od_g1, "od_g2": od_g2, "od_k_k": od_k_k, "od_k_a": od_k_a,
            "od_r_k": od_r_k, "od_ln_w": od_ln_w, "od_ln_b": od_ln_b, "od_w_o": od_w_o,
            "router_w": router_w, "router_b": router_b, "moe_w1": moe_w1, "moe_w3": moe_w3,
            "moe_w2": moe_w2, "final_norm_w": final_norm_w}

def reference(x, c, mod_w, mod_b, norm_w, hg_lb_logits, ev_w_in, ev_hg_norm, ev_conv_w, ev_conv_b,
              ev_dt_bias, ev_a_log, ev_d_skip, ev_ssm_norm, ev_w_out, od_mu, od_w_rkv, od_w_dec0,
              od_w_dec1, od_w_dec2, od_a0, od_a1, od_a2, od_g1, od_g2, od_k_k, od_k_a, od_r_k,
              od_ln_w, od_ln_b, od_w_o, router_w, router_b, moe_w1, moe_w3, moe_w2, final_norm_w):
    mod = jnp.einsum('bd,lde->lbe', jax.nn.silu(c), mod_w) + mod_b[:, None, :]
    gamma = jax.nn.softmax(hg_lb_logits.astype(jnp.float32), axis=0)
    lower_bounds = jnp.cumsum(gamma, axis=0) - gamma[0]
    for l in range(DEPTH):
        sh_m, sc_m, gt_m, sh_f, sc_f, gt_f = jnp.split(mod[l], 6, axis=-1)
        h = modulate(rms_norm(x, norm_w[l, 0]), sh_m, sc_m)
        j = l // 2
        if l % 2 == 0:
            y = hgrn2_ssd_mixer(h, lower_bounds[l + 1], ev_w_in[j], ev_hg_norm[j], ev_conv_w[j],
                                ev_conv_b[j], ev_dt_bias[j], ev_a_log[j], ev_d_skip[j],
                                ev_ssm_norm[j], ev_w_out[j])
        else:
            y = rwkv7_mixer(h, od_mu[j], od_w_rkv[j], od_w_dec0[j], od_w_dec1[j], od_w_dec2[j],
                            od_a0[j], od_a1[j], od_a2[j], od_g1[j], od_g2[j], od_k_k[j], od_k_a[j],
                            od_r_k[j], od_ln_w[j], od_ln_b[j], od_w_o[j])
        x = x + gt_m[:, None, :] * y
        h = modulate(rms_norm(x, norm_w[l, 1]), sh_f, sc_f)
        x = x + gt_f[:, None, :] * grouped_moe(h, router_w, router_b, moe_w1[l], moe_w3[l], moe_w2[l])
    return rms_norm(x, final_norm_w)


_drawn_inputs = setup_inputs


def setup_inputs(seed=0):
    import zlib

    import numpy as np

    out = dict(_drawn_inputs(seed))
    spreads = {}
    factors = {'ev_hg_norm': 6.197,
     'ev_ssm_norm': 3.789,
     'od_w_dec1': 4.258,
     'od_w_dec2': 6.121,
     'od_k_k': 4.076,
     'od_ln_w': 8.0,
     'od_ln_b': 8.0,
     'final_norm_w': 2.694}
    for name, (base, spread) in spreads.items():
        noise = np.random.default_rng([zlib.crc32(name.encode()), seed]).standard_normal(out[name].shape)
        drawn = base * np.exp(spread * noise) if base else spread * noise
        out[name] = jnp.asarray(drawn.astype(out[name].dtype))
    for name, factor in factors.items():
        out[name] = (out[name] * factor).astype(out[name].dtype)
    return out
```

```python
from contextlib import ExitStack

import concourse.bass as bass
from concourse import mybir

F32 = mybir.dt.float32
I32 = mybir.dt.int32
ALU = mybir.AluOpType
ACT = mybir.ActivationFunctionType
AX = mybir.AxisListType

P = 128
D = 1024
S = 256
KB = D // P
NT = S // P
LAYERS = 2
EPS = 1e-6
GN_EPS = 64e-5
HEAD = 64
NH = D // HEAD
GROUPS = 2
TAPS = 4
XBC = D + 2 * GROUPS * P
XBLK = XBC // P
IN_COLS = 4 * D + D + XBC + NH
NE = 16
FF = D // 2
FB = FF // P
MID = P // 2
C = 64
SLOTS = 6
TILE = 4096
W = 512
E05 = 0.6065306597126334
HALVES = [1, 2, 4, 8, 16, 32, 64]
NSUB = 4


def layout_vectors():
    groups = [
        [("mod_b", 96), ("norm_w", 32)],
        [("c", 8), ("final_norm_w", 8), ("hg_lb_logits", 24), ("ev_hg_norm", 8), ("ev_conv_w", 48),
         ("ev_conv_b", 12), ("ev_ssm_norm", 8)],
        [("od_mu", 48), ("od_w_dec0", 8), ("od_a0", 8), ("od_k_k", 8), ("od_k_a", 8), ("od_r_k", 8),
         ("od_ln_w", 8), ("od_ln_b", 8)],
    ]
    at = {}
    for g, rows in enumerate(groups):
        r = 0
        for name, n in rows:
            at[name] = (g, r, n)
            r += n
    return at


VEC = layout_vectors()


def weight_tiles():
    first = [("mod", 0, j) for j in range(12)]
    first += [("in", 0, j) for j in (2, 3, 0, 1, 4, 5, 12, 10, 11, 8, 9, 6, 7)]
    first += [("out", 0, j) for j in range(4)]
    second = [("mod", 1, j) for j in range(12)] + [("la", 0, 0), ("lb", 0, 0)]
    second += [("rkv", i, j) for i in (1, 0, 2) for j in range(2)]
    second += [("wo", 0, j) for j in range(2)]
    return [first, second]


def trunk(nc, t, out):
    tiles = weight_tiles()

    landed = [0] * SLOTS
    plan = []
    moe_base = []
    n_dma = {"la": 3, "lb": 3}
    for stage in tiles:
        rows = []
        for n, tile in enumerate(stage):
            slot = n % SLOTS
            landed[slot] += n_dma.get(tile[0], 1)
            rows.append((tile, slot, landed[slot]))
        plan.append(rows)
        moe_base.append(list(landed))
        landed = [x + NE // 2 for x in landed]

    FULL_IN = 2 * 13
    FULL_LORA = FULL_IN + 12
    USED = [16, 30]

    with ExitStack() as ctx:
        def sb(name, shape, dt=F32):
            return ctx.enter_context(nc.sbuf_tensor(name, shape, dt))

        def sem(name):
            return ctx.enter_context(nc.semaphore(name))

        ctx.enter_context(nc.allow_non_contiguous_dma(reason="a few small vectors"))

        bank = [ctx.enter_context(nc.psum_tensor(f"bank{i}", [P, W], F32)) for i in range(8)]

        ring = sb("ring", [P, SLOTS * TILE])
        BUF = KB * S
        XPAD = XBLK * (S + TAPS - 1)
        arena = sb("arena", [P, 12 * BUF + XPAD])

        def buf(i, n=1):
            return arena[:, i * BUF:(i + n) * BUF]

        def blocks(i):
            return buf(i).rearrange("p (k s) -> p k s", k=KB)

        def by_tile(i):
            return buf(i).rearrange("p (k t s) -> p k t s", k=KB, t=NT)

        xpad = arena[:, 12 * BUF:12 * BUF + XPAD].rearrange("p (k s) -> p k s", k=XBLK)

        xT = blocks(0)
        hT = blocks(1)
        xN = buf(8).rearrange("p (t d) -> p t d", t=NT)
        squares = blocks(11)

        ident = sb("ident", [P, P])
        ones = sb("ones", [P, S])
        halves = sb("halves", [P, 2])
        causal = sb("causal", [P, P])
        strict = sb("strict", [P, P])
        tri = buf(7)[:, 0:6 * P].rearrange("p (i s) -> p i s", i=6)
        level = sb("level", [P, 7, P])
        iota64 = sb("iota64", [P, C])
        pcol0 = sb("pcol0", [P, 1])
        tie4 = sb("tie4", [P, 4])

        vrows = buf(9)[:, 0:3 * P].rearrange("p (g r) -> p g r", g=3)
        vcols = sb("vcols", [P, 3, P])

        def col(name, i):
            g, r, n = VEC[name]
            assert i < n
            return vcols[:, g, r + i:r + i + 1]

        def cols(name, a, b):
            g, r, n = VEC[name]
            return vcols[:, g, r + a:r + b]

        modT = sb("modT", [P, LAYERS, 48])
        gain = sb("gain", [P, LAYERS, 2, KB])
        csilu = sb("csilu", [P, KB])
        rs_root = sb("rs_root", [P, 2 * NH])
        rstd = sb("rstd", [P, 2 * NH])
        gm_mean = sb("gm_mean", [P, 2 * NH])
        beta = sb("beta", [P, 2 * NH])
        lb = sb("lb", [P, KB])
        oml = sb("oml", [P, KB])
        lbe = sb("lbe", [P, 3, KB])
        lbm = sb("lbm", [P, KB])
        dt_bias = sb("dt_bias", [NH, 1])
        a_log = sb("a_log", [NH, 1])
        a_neg = sb("a_neg", [NH, 1])
        dskip = sb("dskip", [P, KB])
        w_dt = sb("w_dt", [P, KB, NH])
        router_w = sb("router_w", [P, KB, NE])
        router_b = sb("router_b", [P, NE])
        eps_col = sb("eps_col", [P, 2])

        tile_landed = [sem(f"tile_landed{i}") for i in range(SLOTS)]
        tile_used = sem("tile_used")
        vec_landed = sem("vec_landed")
        x_landed = sem("x_landed")
        small_landed = sem("small_landed")
        vrows_zeroed = sem("vrows_zeroed")
        consts = sem("consts")
        stored = sem("stored")
        pool_chain = sem("pool_chain")
        dve_chain = sem("dve_chain")
        act_chain = sem("act_chain")

        weight = lambda slot: ring[:, slot * TILE:(slot + 1) * TILE]
        w_cols = lambda slot: weight(slot).rearrange("p (k n) -> p k n", k=KB)
        w_rows = lambda slot: weight(slot).rearrange("p (k n) -> p k n", k=4)
        row_block = lambda ap: ap.rearrange("(k p) n -> p k n", p=P)

        vec_T = sem("vec_T")
        vec_cols = sem("vec_cols")
        xT_psum = sem("xT_psum")
        xT_evac = sem("xT_evac")
        csilu_ready = sem("csilu_ready")
        x_ready = sem("x_ready")
        sq_ready = sem("sq_ready")
        sums_psum = sem("sums_psum")
        root_ready = sem("root_ready")
        rstd_ready = sem("rstd_ready")
        bcast_psum = sem("bcast_psum")
        h_ready = sem("h_ready")
        proj_full = sem("proj_full")
        proj_evac = sem("proj_evac")
        lb_max = sem("lb_max")
        start_exp = sem("start_exp")
        logf_ready = sem("logf_ready")
        k_ready = sem("k_ready")
        b_ready = sem("b_ready")
        dl_ready = sem("dl_ready")
        dr_ready = sem("dr_ready")
        el_exp = sem("el_exp")
        ek_ready = sem("ek_ready")
        eq_ready = sem("eq_ready")
        score_full = sem("score_full")
        score_evac = sem("score_evac")
        o_full = sem("o_full")
        o_evac = sem("o_evac")
        head_sum = sem("head_sum")
        head_root = sem("head_root")
        head_rstd = sem("head_rstd")
        head_bcast = sem("head_bcast")
        bcast_used = sem("bcast_used")
        oa_ready = sem("oa_ready")
        silu_g = sem("silu_g")
        dt_full = sem("dt_full")
        dtz = sem("dtz")
        dtabs = sem("dtabs")
        dtln = sem("dtln")
        dt_ready = sem("dt_ready")
        dtN_full = sem("dtN_full")
        dtN_ready = sem("dtN_ready")
        conv_zero = sem("conv_zero")
        conv_done = sem("conv_done")
        conv_silu = sem("conv_silu")
        xs_full = sem("xs_full")
        xdt_ready = sem("xdt_ready")
        cb_full = sem("cb_full")
        cb_ready = sem("cb_ready")
        row_full = sem("row_full")
        dec_diff = sem("dec_diff")
        dec_exp = sem("dec_exp")
        dec_mat = sem("dec_mat")
        y_full = sem("y_full")
        y_ready = sem("y_ready")
        ysq_ready = sem("ysq_ready")
        yb_full = sem("yb_full")
        ob_ready = sem("ob_ready")
        mix_ready = sem("mix_ready")
        lora_full = sem("lora_full")
        lora_evac = sem("lora_evac")
        cum_ready = sem("cum_ready")
        kk_sq = sem("kk_sq")
        rk_ready = sem("rk_ready")
        rw_diff = sem("rw_diff")
        rw_exp = sem("rw_exp")
        rw_ops = sem("rw_ops")
        kc_ready = sem("kc_ready")
        rsc_full = sem("rsc_full")
        rsc_evac = sem("rsc_evac")
        lt_ready = sem("lt_ready")
        xt1_ready = sem("xt1_ready")
        x1_full = sem("x1_full")
        x1_ready = sem("x1_ready")
        lm_ready = sem("lm_ready")
        tm_full = sem("tm_full")
        tm_ready = sem("tm_ready")
        xm_full = sem("xm_full")
        xm_ready = sem("xm_ready")
        w_full = sem("w_full")
        w_ready = sem("w_ready")
        u_full = sem("u_full")
        u_ready = sem("u_ready")
        ry_full = sem("ry_full")
        ry_ready = sem("ry_ready")
        gn_mean = sem("gn_mean")
        gn_sq = sem("gn_sq")
        bv_ready = sem("bv_ready")
        bvT_full = sem("bvT_full")
        kmid_diff = sem("kmid_diff")
        kmid_ready = sem("kmid_ready")
        og_ready = sem("og_ready")
        moe_names = ["hN_full", "hN_evac", "logit_full", "lmax", "lexp", "sel_ready", "rank_full", "tab_ready", "slots_ready",
                     "slot_full", "rows_ready", "p_ready", "gath_full", "hg_ready", "up_done", "silu_done",
                     "hid_ready", "y0_ready", "y1_ready", "s_ready", "scat_done", "down_half", "chain"]
        M = [{n: sem(f"m{l}_{n}") for n in moe_names} for l in range(LAYERS)]

        qT, kT, bT, zT, gT = blocks(2), blocks(4), blocks(5), blocks(11), blocks(10)
        fT = blocks(3)
        eT = [3, 7]
        vN = buf(6).rearrange("p (t d) -> p t d", t=NT)
        scd = buf(8).rearrange("p (t h s) -> p t h s", t=NT, h=KB)
        scx = buf(9)[:, 0:KB * P].rearrange("p (h s) -> p h s", h=KB)
        oa = blocks(2)
        cbm = buf(9)[:, KB * P:KB * P + 6 * P].rearrange("p (g n) -> p g n", g=GROUPS)
        xdt = buf(4).rearrange("p (t d) -> p t d", t=NT)
        NDEC = 5
        dec = buf(7)[:, 0:NDEC * 3 * P].rearrange("p (r n) -> p r n", r=NDEC)
        yT = blocks(5)
        kmid = sb("kmid", [P, KB])
        scratch = sb("scratch", [P, 7 * S])
        ctmp = scratch[:, 0:2 * S].rearrange("p (u s) -> p u s", u=2)
        dts = scratch[0:NH, 2 * S:7 * S].rearrange("p (u s) -> p u s", u=5)
        dtN = sb("dtN", [P, 2, NT, NH])

        xx = blocks(2)
        mixed = [blocks(3), blocks(4)]
        rT, kkT, aT, ggT = blocks(5), blocks(11), blocks(8), blocks(9)
        k1T = blocks(6)
        vN1 = buf(7).rearrange("p (t h n) -> p t h n", t=NT, h=NH)
        sgT = blocks(10)
        cum = arena[:, 12 * BUF:12 * BUF + KB * (S + 1)].rearrange("p (k s) -> p k s", k=KB)
        AR = buf(1, 2).rearrange("p (k t a s) -> p k t a s", k=KB, t=NT, a=2)
        rwB, rwK = by_tile(8), by_tile(6)
        oR = AR[:, :, :, 0, :]
        lora = [scratch[:, i * S:(i + 1) * S] for i in range(3)]
        bvN = buf(5).rearrange("p (t h n) -> p t h n", t=NT, h=NH)
        pslot = [arena[:, 3 * BUF:6 * BUF], arena[:, 10 * BUF:13 * BUF]]

        def part(pr, off, n):
            return pslot[pr % 2][:, off * P:(off + n) * P]

        def sc(pr, kind, tt, hh):
            return part(pr, kind * 4 + tt * 2 + hh, 1)

        def scro(pr, kind, hh):
            return part(pr, 16 + kind * 2 + hh, 1)

        def kcross(pr, which):
            return part(pr, 24 + which, 1)

        def xinv(pr):
            return part(pr, 26, 4)

        def xinvT(pr):
            return part(pr, 30, 4)

        def tmid(pr):
            return part(pr, 34, 4)

        def lmask(pr, i):
            return part(pr, 38 + 4 * (i % 2), 4)

        def uneg(pr, tt):
            return part(pr, 46 + tt, 1)

        assert 48 * P <= 3 * BUF and 10 * BUF + 48 * P <= 12 * BUF + XPAD

        hN = buf(2).rearrange("p (t d) -> p t d", t=NT)
        m3 = buf(3)
        hgT = m3[:, 0:KB * C].rearrange("p (k c) -> p k c", k=KB)
        hid = m3[:, 512:512 + FB * C].rearrange("p (f c) -> p f c", f=FB)
        hsil = m3[:, 768:768 + FB * C].rearrange("p (f c) -> p f c", f=FB)
        pick = m3[:, 1024:1024 + NT * C].rearrange("p (t c) -> p t c", t=NT)
        pick2 = m3[:, 1152:1152 + NT * C].rearrange("p (t c) -> p t c", t=NT)
        spread = m3[0:C, 1280:1280 + S]
        spread2 = m3[0:C, 1536:1536 + S]
        ymoe = buf(4)[0:C, 0:D]
        rows4 = buf(4)[0:C, D:D + 4 * S].rearrange("p (r s) -> p r s", r=4)
        rt = buf(5)

        def small(i, n=1):
            return rt[:, i * 32:(i + n) * 32]

        tok4 = sb("tok4", [P, NT, 4])
        pcol = sb("pcol", [P, 1])
        tab_f = sb("tab_f", [P, 64])
        tab_i = sb("tab_i", [1, 64], I32)

        block = ctx.enter_context(nc.Block())

        @block.sync
        def _(sp):
            def load(tile, slot):
                kind, l, j = tile
                if kind == "mod":
                    srcs = [(w_cols(slot), row_block(t["mod_w"][l])[:, :, j * W:(j + 1) * W])]
                elif kind == "in":
                    srcs = [(w_cols(slot), row_block(t["ev_w_in"][0])[:, :, j * W:(j + 1) * W])]
                elif kind == "out":
                    srcs = [(w_rows(slot), row_block(t["ev_w_out"][0])[:, 4 * j:4 * j + 4, :])]
                elif kind == "rkv":
                    srcs = [(w_cols(slot), row_block(t["od_w_rkv"][0, l])[:, :, j * W:(j + 1) * W])]
                elif kind == "wo":
                    srcs = [(w_rows(slot), row_block(t["od_w_o"][0])[:, 4 * j:4 * j + 4, :])]
                elif kind == "la":
                    wt = weight(slot)
                    srcs = [(wt[:, 0:512].rearrange("p (k n) -> p k n", k=KB), row_block(t["od_w_dec1"][0])),
                            (wt[:, 512:1024].rearrange("p (k n) -> p k n", k=KB), row_block(t["od_a1"][0])),
                            (wt[:, 1024:2048].rearrange("p (k n) -> p k n", k=KB), row_block(t["od_g1"][0]))]
                elif kind == "lb":
                    wt = weight(slot)
                    srcs = [(wt[0:64, 0:D], t["od_w_dec2"][0]), (wt[0:64, D:2 * D], t["od_a2"][0]),
                            (wt[:, 2 * D:3 * D], t["od_g2"][0])]
                for dst, src in srcs:
                    sp.dma_start(dst, src).then_inc(tile_landed[slot], 16)

            def wait_used(l, n):
                kind = plan[l][n][0][0]
                if kind == "mod":
                    sp.wait_ge(tile_used, (USED[0] if l else 0) + n + 1)
                elif kind == "in":
                    sp.wait_ge(proj_full, 2 * (n - 12) + 2)
                elif kind == "out":
                    sp.wait_ge(tile_used, 12 + n - 25 + 1)
                elif kind == "la":
                    sp.wait_ge(lora_full, 3)
                elif kind == "lb":
                    sp.wait_ge(proj_full, FULL_LORA)
                elif kind == "rkv":
                    sp.wait_ge(proj_full, FULL_LORA + 2 * (n - 14) + 2)
                elif kind == "wo":
                    sp.wait_ge(tile_used, USED[0] + 12 + n - 20 + 1)

            for l in range((NSUB + 1) // 2):
                base = M[l]
                for n, (tile, slot, _) in enumerate(plan[l]):
                    if n >= SLOTS:
                        wait_used(l, n - SLOTS)
                    elif l > 0 and n == 0:
                        g_end = sp.value_load(tab_i[0:1, NE + NE:NE + NE + 1], min_val=NE, max_val=2 * NE)
                        sp.wait_ge(M[l - 1]["down_half"], g_end * 2)
                    load(tile, slot)
                n_stage = len(plan[l])
                if NSUB < 2 * l + 2:
                    break
                for e in range(2):
                    for s, (dst, src) in enumerate([
                            (w_cols(3 * e), row_block(t["moe_w1"][l, e])),
                            (w_cols(3 * e + 1), row_block(t["moe_w3"][l, e])),
                            (w_rows(3 * e + 2), row_block(t["moe_w2"][l, e]))]):
                        slot = 3 * e + s
                        last = max(n for n in range(n_stage) if n % SLOTS == slot)
                        wait_used(l, last)
                        sp.dma_start(dst, src).then_inc(tile_landed[slot], 16)
                sp.wait_ge(base["tab_ready"], 1)
                w1v = t["moe_w1"][l].rearrange("e (k p) n -> p e k n", p=P)
                w3v = t["moe_w3"][l].rearrange("e (k p) n -> p e k n", p=P)
                w2v = t["moe_w2"][l].rearrange("e (k p) n -> p e k n", p=P)
                with sp.Fori(1, NE // 2) as i:
                    for e in range(2):
                        done = sp.value_load(tab_i[0:1, bass.ds(NE + 2 * i + (e - 1), 1)], min_val=1, max_val=2 * NE)
                        sp.wait_ge(base["up_done"], done)
                        sp.dma_start(w_cols(3 * e), w1v[:, bass.ds(2 * i + e, 1)]
                                     .rearrange("p e k n -> p (e k) n")).then_inc(tile_landed[3 * e], 16)
                        sp.dma_start(w_cols(3 * e + 1), w3v[:, bass.ds(2 * i + e, 1)]
                                     .rearrange("p e k n -> p (e k) n")).then_inc(tile_landed[3 * e + 1], 16)
                        sp.wait_ge(base["down_half"], done * 2)
                        sp.dma_start(w_rows(3 * e + 2), w2v[:, bass.ds(2 * i + e, 1)]
                                     .rearrange("p e k n -> p (e k) n")).then_inc(tile_landed[3 * e + 2], 16)
            for tt in range(NT):
                sp.wait_ge(o_evac, 4 + 4 * (tt + 1))
                sp.dma_start(out[0, tt * P:(tt + 1) * P, :], hN[:, tt, :]).then_inc(stored, 16)
            sp.wait_ge(stored, 16 * NT)

        @block.gpsimd
        def _(pool):
            count = [0]

            def link(ins):
                count[0] += 1
                ins.then_inc(pool_chain, 1)
                pool.wait_ge(pool_chain, count[0])

            link(pool.memset(ident[:], 0.0))
            link(pool.affine_select(out=ident[:], in_=ident[:], compare_op=ALU.not_equal, fill=1.0, base=0,
                                    pattern=[[-1, P]], channel_multiplier=1))
            pool.memset(ones[:], 1.0)
            link(pool.memset(halves[:], 0.0))
            for hh in range(2):
                link(pool.memset(halves[hh * HEAD:(hh + 1) * HEAD, hh:hh + 1], 1.0))
            pool.iota(iota64[:], pattern=[[1, C]], base=0, channel_multiplier=0, allow_small_or_imprecise_dtypes=True)
            pool.iota(tie4[:], pattern=[[1, 4]], base=0, channel_multiplier=0, allow_small_or_imprecise_dtypes=True)
            pool.iota(pcol0[:], pattern=[[0, 1]], base=0, channel_multiplier=1, allow_small_or_imprecise_dtypes=True)
            pool.memset(eps_col[:, 0:1], EPS)
            pool.memset(eps_col[:, 1:2], GN_EPS)
            for i in range(6):
                h = 2 << i
                v = tri[:, i, :].rearrange("p (b s) -> p b s", s=h)
                link(pool.memset(tri[:, i, :], 1.0))
                link(pool.affine_select(out=v, in_=v, compare_op=ALU.is_ge, fill=0.0, base=0,
                                        pattern=[[-h, P // h], [0, h]], channel_multiplier=1))
                link(pool.affine_select(out=v, in_=v, compare_op=ALU.is_ge, fill=0.0, base=h - 1,
                                        pattern=[[h, P // h], [0, h]], channel_multiplier=-1))
                link(pool.affine_select(out=tri[:, i, :], in_=tri[:, i, :], compare_op=ALU.is_ge, fill=0.0,
                                        base=0, pattern=[[1, P]], channel_multiplier=-1))
            link(pool.memset(causal[:], 1.0))
            link(pool.affine_select(out=causal[:], in_=causal[:], compare_op=ALU.is_ge, fill=0.0, base=0,
                                    pattern=[[1, P]], channel_multiplier=-1))
            link(pool.tensor_tensor(strict[:], causal[:], ident[:], ALU.subtract))
            inner = [ident[:]] + [tri[:, i, :] for i in range(6)]
            outer = [tri[:, i, :] for i in range(6)] + [causal[:]]
            for i in range(7):
                link(pool.tensor_tensor(level[:, i, :], outer[i], inner[i], ALU.subtract))
            pool.memset(xpad[:, :, 0:TAPS - 1], 0.0).then_inc(conv_zero, 1)
            pool.memset(eps_col[:, 0:1], EPS).then_inc(consts, 1)

            pool.wait_ge(b_ready, 1)
            for i, h in enumerate(HALVES + [P]):
                e = buf(eT[i % 2]).rearrange("p (b two h) -> p b two h", two=2, h=h)
                b = buf(5).rearrange("p (b two h) -> p b two h", two=2, h=h)
                kv = buf(4).rearrange("p (b two h) -> p b two h", two=2, h=h)
                nb = KB * S // (2 * h)
                if i >= 2:
                    pool.wait_ge(score_full, 4 + 2 * (i - 1))
                mid = b[:, :, 0, h - 1:h].to_broadcast([P, nb, h])
                pool.tensor_tensor(e[:, :, 0, :], mid, b[:, :, 0, :], ALU.subtract).then_inc(dl_ready, 1)
                pool.wait_ge(el_exp, i + 1)
                pool.wait_ge(k_ready, 1)
                pool.tensor_tensor(e[:, :, 0, :], e[:, :, 0, :], kv[:, :, 0, :], ALU.mult).then_inc(ek_ready, 1)
            if NSUB < 3:
                return

            for jj in range(KB // 2):
                for i in range(1, 7):
                    for pr in (2 * jj, 2 * jj + 1):
                        pool.wait_ge(lt_ready, pr + 1)
                        if i >= 3:
                            pool.wait_ge(tm_full, jj * 12 + 2 * (i - 3) + pr % 2 + 1)
                        elif jj > 0:
                            pool.wait_ge(tm_full, jj * 12)
                        src = part(pr, 8, 4).rearrange("p (u s) -> p u s", u=4)
                        dst = lmask(pr, i).rearrange("p (u s) -> p u s", u=4)
                        pool.tensor_tensor(dst, src, level[:, i:i + 1, :].to_broadcast([P, 4, P]),
                                           ALU.mult).then_inc(lm_ready, 1)

        @block.tensor
        def _(pe):
            pe.wait_ge(consts, 1)

            def column_sums(dst, src, tt, n):
                for k in range(n):
                    mm = pe.matmul(dst, src(k)[:, tt * P:(tt + 1) * P], ones[:, 0:1], start=(k == 0),
                                   stop=(k == n - 1))
                return mm

            def norm(k):
                pe.wait_ge(sq_ready, k + 1)
                for tt in range(NT):
                    mm = column_sums(bank[7][:, tt:tt + 1], lambda b: squares[:, b, :], tt, KB)
                mm.then_inc(sums_psum, 1)
                pe.wait_ge(rstd_ready, k + 1)
                for tt in range(NT):
                    mm = pe.matmul(bank[6][:, tt * P:(tt + 1) * P], rstd[:, tt:tt + 1].to_broadcast([P, P]),
                                   ident[:], start=True, stop=True)
                mm.then_inc(bcast_psum, 1)

            used = [0]
            full = [0]

            def take(stage, n):
                tile, slot, count = plan[stage][n]
                pe.wait_ge(tile_landed[slot], 16 * count)
                return tile, slot

            def proj_bank():
                n = full[0]
                if n >= 4:
                    pe.wait_ge(proj_evac, n - 3)
                full[0] += 1
                return bank[n % 4]

            def project_T(slot, src):
                for half in range(2):
                    ps = proj_bank()
                    for c in range(2):
                        for k in range(KB):
                            mm = pe.matmul(ps[:, c * S:(c + 1) * S],
                                           w_cols(slot)[:, k, (2 * half + c) * P:(2 * half + c + 1) * P],
                                           src[:, k, :], start=(k == 0), stop=(k == KB - 1))
                    mm.then_inc(proj_full, 1)
                return mm

            def project_N(slot, src):
                for tt in range(NT):
                    ps = proj_bank()
                    for k in range(KB):
                        mm = pe.matmul(ps[:, :], src[:, k, tt * P:(tt + 1) * P], w_cols(slot)[:, k, :],
                                       start=(k == 0), stop=(k == KB - 1))
                    mm.then_inc(proj_full, 1)
                return mm

            def modulation(l):
                for n in range(12):
                    _, slot = take(l, n)
                    for c in range(4):
                        o = 4 * n + c
                        for k in range(KB):
                            mm = pe.matmul(bank[5][:, o:o + 1], w_cols(slot)[:, k, c * P:(c + 1) * P],
                                           csilu[:, k:k + 1], start=(k == 0), stop=(k == KB - 1))
                    mm.then_inc(tile_used, 1)

            def out_projection(stage, first, n, srcs, ready):
                for j in range(n):
                    ready(j)
                    _, slot = take(stage, first + j)
                    for d in range(KB):
                        for kk in range(4):
                            mm = pe.matmul(bank[d // 2][:, (d % 2) * S:(d % 2 + 1) * S],
                                           w_rows(slot)[:, kk, d * P:(d + 1) * P], srcs(4 * j + kk),
                                           start=(j == 0 and kk == 0 and d % 2 == 0),
                                           stop=(j == n - 1 and kk == 3), skip_group_check=True)
                    mm.then_inc(tile_used, 1)

            pe.wait_ge(vec_landed, 16 * len(VEC))
            for g in range(3):
                mm = pe.transpose(bank[4][:, g * P:(g + 1) * P], vrows[:, g, :], ident[:])
            mm.then_inc(vec_T, 1)
            pe.wait_ge(x_landed, 16)
            for k in range(KB):
                for tt in range(NT):
                    mm = pe.transpose(bank[k // 2][:, (k % 2) * S + tt * P:(k % 2) * S + (tt + 1) * P],
                                      xN[:, tt, k * P:(k + 1) * P], ident[:])
                if k % 2:
                    mm.then_inc(xT_psum, 1)
            pe.wait_ge(csilu_ready, 1)
            modulation(0)
            norm(0)
            pe.wait_ge(h_ready, 1)
            pe.wait_ge(xT_evac, 1)

            scores = [0]

            def score_bank():
                m = scores[0]
                if m >= 2:
                    pe.wait_ge(score_evac, m - 1)
                scores[0] += 1
                return bank[4 + m % 2]

            def diagonal():
                pe.wait_ge(proj_evac, 8)
                pe.wait_ge(k_ready, 1)
                for r in range(2):
                    for tt in range(NT):
                        ps = score_bank()
                        for h in range(4):
                            ss = slice(tt * P, (tt + 1) * P)
                            mm = pe.matmul(ps[:, h * P:(h + 1) * P], kT[:, 4 * r + h, ss], qT[:, 4 * r + h, ss],
                                           start=True, stop=True)
                        mm.then_inc(score_full, 1)

            def level_scores(i):
                h = (HALVES + [P])[i]
                pe.wait_ge(ek_ready, i + 1)
                pe.wait_ge(eq_ready, i + 1)
                e = blocks(eT[i % 2])
                if h < P:
                    for tt in range(NT):
                        ps = score_bank()
                        for hh in range(KB):
                            et = e[:, hh, tt * P:(tt + 1) * P]
                            right = et.rearrange("p (b two h) -> p b two h", two=2, h=h)[:, :, 1, :]
                            mm = pe.matmul(ps[:, hh * 64:(hh + 1) * 64], et, right, start=True, stop=True)
                        mm.then_inc(score_full, 1)
                else:
                    for r in range(2):
                        ps = score_bank()
                        for hh in range(4):
                            mm = pe.matmul(ps[:, hh * P:(hh + 1) * P], e[:, 4 * r + hh, 0:P],
                                           e[:, 4 * r + hh, P:S], start=True, stop=True)
                        mm.then_inc(score_full, 1)

            extra = {4: [diagonal, lambda: level_scores(0)], 5: [lambda: level_scores(1)],
                     6: [lambda: level_scores(2)], 7: [lambda: level_scores(3)], 8: [lambda: level_scores(4)],
                     9: [lambda: level_scores(5)], 10: [lambda: level_scores(6)], 11: [lambda: level_scores(7)]}
            for n in range(13):
                (_, _, j), slot = take(0, 12 + n)
                mm = (project_N if j in (4, 5) else project_T)(slot, hT)
                if n == 8:
                    pe.wait_ge(small_landed, 16 * 7)
                    for k in range(KB):
                        mm = pe.matmul(bank[6][0:NH, 0:S], w_dt[:, k, :], hT[:, k, :], start=(k == 0),
                                       stop=(k == KB - 1))
                    mm.then_inc(dt_full, 1)
                for f in extra.get(n, []):
                    f()

            pe.wait_ge(score_evac, 20)
            for u in range(4):
                if u >= 2:
                    pe.wait_ge(o_evac, u - 1)
                elif u == 0:
                    pe.wait_ge(dtz, 1)
                for c in range(2):
                    h = 2 * u + c
                    hs = slice(h * P, (h + 1) * P)
                    o = bank[6 + u % 2]
                    pe.matmul(o[:, c * S:c * S + P], vN[:, 0, hs], scd[:, 0, h, :], start=True, stop=True)
                    pe.matmul(o[:, c * S + P:(c + 1) * S], vN[:, 0, hs], scx[:, h, :], start=True, stop=False)
                    mm = pe.matmul(o[:, c * S + P:(c + 1) * S], vN[:, 1, hs], scd[:, 1, h, :], start=False, stop=True)
                mm.then_inc(o_full, 1)

            pe.wait_ge(dt_ready, 1)
            for a in range(2):
                for tt in range(NT):
                    mm = pe.transpose(bank[4][:, (2 * a + tt) * NH:(2 * a + tt + 1) * NH],
                                      dts[:, 3 + a, tt * P:(tt + 1) * P], ident[0:NH, 0:NH])
            mm.then_inc(dtN_full, 1)
            pe.wait_ge(conv_silu, 1)
            pe.wait_ge(o_evac, 4)
            for u in range(4):
                tt, half = u // 2, u % 2
                if u == 3:
                    pe.wait_ge(xdt_ready, 1)
                ps = bank[[5, 6, 7, 5][u]]
                for c in range(4):
                    mm = pe.transpose(ps[:, c * P:(c + 1) * P],
                                      xpad[:, 4 * half + c, TAPS - 1 + tt * P:TAPS - 1 + (tt + 1) * P], ident[:])
                mm.then_inc(xs_full, 1)
            pe.wait_ge(xdt_ready, 3)
            for g in range(GROUPS):
                ps = bank[6 + g]
                B = xpad[:, KB + g, TAPS - 1:]
                Cq = xpad[:, KB + GROUPS + g, TAPS - 1:]
                pe.matmul(ps[:, 0:S], B[:, 0:P], Cq[:, 0:S], start=True, stop=True)
                mm = pe.matmul(ps[:, S:S + P], B[:, P:S], Cq[:, P:S], start=True, stop=True)
                mm.then_inc(cb_full, 1)
            pe.wait_ge(dtN_ready, 1)
            pe.wait_ge(xdt_ready, 4)
            for h in range(KB):
                for tt in range(NT):
                    mm = pe.matmul(bank[4][:, tt * KB + h:tt * KB + h + 1], fT[:, h, tt * P:(tt + 1) * P],
                                   ones[:, 0:1], start=True, stop=True)
            mm.then_inc(head_sum, 1)
            pe.wait_ge(head_rstd, 1)
            for u in range(4):
                if u >= 2:
                    pe.wait_ge(bcast_used, u - 1)
                for c in range(2):
                    for tt in range(NT):
                        r = tt * KB + 2 * u + c
                        mm = pe.matmul(bank[4 + u % 2][:, c * S + tt * P:c * S + (tt + 1) * P],
                                       rstd[:, r:r + 1].to_broadcast([P, P]), ident[:], start=True, stop=True)
                mm.then_inc(head_bcast, 1)
            pe.wait_ge(cb_ready, 2)
            pe.wait_ge(bcast_used, 4)

            def decay_row(h):
                if h >= 2:
                    pe.wait_ge(dec_diff, h - 1)
                pe.matmul(bank[4 + h % 2][:, 0:S], ident[0:NH, h:h + 1].to_broadcast([NH, P]), dts[:, 4, :],
                          start=True, stop=True).then_inc(row_full, 1)

            def head_out(h):
                pe.wait_ge(dec_mat, h + 1)
                pr, c = h // 2, h % 2
                if pr >= 2 and c == 0:
                    pe.wait_ge(y_ready, pr - 1)
                o = bank[6 + pr % 2][c * HEAD:(c + 1) * HEAD, :]
                m = dec[:, h % NDEC, :]
                hs = slice(h * HEAD, (h + 1) * HEAD)
                pe.matmul(o[:, 0:S], xdt[:, 0, hs], m[:, 0:S], start=True, stop=True)
                pe.matmul(o[:, P:S], xdt[:, 1, hs], m[:, S:S + P], start=False, stop=True,
                          skip_group_check=True).then_inc(y_full, 1)

            for h in range(NH + 2):
                if h < NH:
                    decay_row(h)
                if h >= 2:
                    head_out(h - 2)
            pe.wait_ge(ysq_ready, 1)
            pe.wait_ge(dec_diff, NH)
            for g in range(GROUPS):
                for tt in range(NT):
                    for k in range(4):
                        mm = pe.matmul(bank[4][:, 2 * g + tt:2 * g + tt + 1],
                                       fT[:, 4 * g + k, tt * P:(tt + 1) * P], ones[:, 0:1],
                                       start=(k == 0), stop=(k == 3))
            mm.then_inc(head_sum, 1)
            pe.wait_ge(head_rstd, 2)
            for g in range(GROUPS):
                for tt in range(NT):
                    r = 2 * g + tt
                    mm = pe.matmul(bank[5][:, g * S + tt * P:g * S + (tt + 1) * P],
                                   rstd[:, r:r + 1].to_broadcast([P, P]), ident[:], start=True, stop=True)
            mm.then_inc(yb_full, 1)
            pe.wait_ge(proj_evac, 26)
            out_projection(0, 25, 4, lambda i: oa[:, i, :] if i < KB else yT[:, i - KB, :],
                           lambda j: pe.wait_ge(oa_ready, 1) if j == 0 else pe.wait_ge(ob_ready, 1))

            def moe(l, k):
                m = M[l]
                norm(k)
                pe.wait_ge(h_ready, k + 1)
                for u in range(4):
                    tt, half = u // 2, u % 2
                    for c in range(4):
                        mm = pe.transpose(bank[4 + u][:, c * P:(c + 1) * P],
                                          hT[:, 4 * half + c, tt * P:(tt + 1) * P], ident[:])
                    mm.then_inc(m["hN_full"], 1)
                for tt in range(NT):
                    for kk in range(KB):
                        mm = pe.matmul(bank[0][:, tt * NE:(tt + 1) * NE], hT[:, kk, tt * P:(tt + 1) * P],
                                       router_w[:, kk, :], start=(kk == 0), stop=(kk == KB - 1))
                mm.then_inc(m["logit_full"], 1)
                pe.wait_ge(m["sel_ready"], 1)
                sel = small(8).rearrange("p (t e) -> p t e", t=NT)
                pe.matmul(bank[1][:, 0:NE], strict[:], sel[:, 0, :], start=True, stop=True)
                pe.matmul(bank[1][:, NE:2 * NE], ones[:, 0:P], sel[:, 0, :], start=True, stop=False)
                pe.matmul(bank[1][:, NE:2 * NE], strict[:], sel[:, 1, :], start=False, stop=True)
                pe.matmul(bank[1][:, 2 * NE:3 * NE], ones[:, 0:P], sel[:, 0, :], start=True, stop=False)
                pe.matmul(bank[1][:, 2 * NE:3 * NE], ones[:, 0:P], sel[:, 1, :], start=False,
                          stop=True).then_inc(m["rank_full"], 1)
                pe.wait_ge(m["slots_ready"], 2)
                for r in range(4):
                    for tt in range(NT):
                        mm = pe.matmul(bank[2 + r // 2][0:C, (r % 2) * S + tt * P:(r % 2) * S + (tt + 1) * P],
                                       tok4[:, tt, r:r + 1].to_broadcast([P, C]), ident[:], start=True, stop=True)
                mm.then_inc(m["slot_full"], 1)

                def gather():
                    for kb in range(KB):
                        for tt in range(NT):
                            mm = pe.matmul(bank[4][:, kb * C:(kb + 1) * C], hN[:, tt, kb * P:(kb + 1) * P],
                                           pick[:, tt, :], start=(tt == 0), stop=(tt == NT - 1))
                    mm.then_inc(m["gath_full"], 1)

                def scatter(first=False, last=False):
                    for d in range(KB):
                        mm = pe.matmul(bank[d // 2][:, (d % 2) * S:(d % 2 + 1) * S], ymoe[:, d * P:(d + 1) * P],
                                       spread, start=(first and d % 2 == 0), stop=last, skip_group_check=True)
                    mm.then_inc(m["scat_done"], 1)

                pe.wait_ge(m["hN_evac"], 4)
                pe.wait_ge(m["p_ready"], 1)
                gather()
                pe.wait_ge(m["y0_ready"], 1)
                pe.wait_ge(m["y1_ready"], 1)
                pe.wait_ge(m["s_ready"], 1)
                pe.wait_ge(m["rows_ready"], 1)
                scatter(first=True)
                with pe.Fori(0, NE // 2) as i:
                    for e in range(2):
                        wa, wb, wc = w_cols(3 * e), w_cols(3 * e + 1), w_rows(3 * e + 2)
                        lo = moe_base[l]
                        for s in range(3):
                            pe.wait_ge(tile_landed[3 * e + s], (i + (lo[3 * e + s] + 1)) * 16)
                        n = pe.value_load(tab_i[0:1, bass.ds(2 * i + e, 1)], min_val=1, max_val=4)
                        g0 = pe.value_load(tab_i[0:1, bass.ds(NE + 2 * i + e, 1)], min_val=0, max_val=2 * NE)
                        with pe.Fori(0, n) as j:
                            g = g0 + j
                            pe.wait_ge(m["hg_ready"], g + 1)
                            pe.wait_ge(m["hid_ready"], g + 1)
                            for half, ww in ((0, wa), (1, wb)):
                                for f in range(FB):
                                    for kb in range(KB):
                                        mm = pe.matmul(bank[5][:, (half * FB + f) * C:(half * FB + f + 1) * C],
                                                       ww[:, kb, f * P:(f + 1) * P], hgT[:, kb, :],
                                                       start=(kb == 0), stop=(kb == KB - 1))
                            mm.then_inc(m["up_done"], 1)
                            pe.wait_ge(m["p_ready"], g + 2)
                            gather()
                            pe.wait_ge(m["y0_ready"], g + 1)
                            pe.wait_ge(m["y1_ready"], g + 1)
                            pe.wait_ge(m["s_ready"], g + 1)
                            scatter()
                            pe.wait_ge(m["hid_ready"], g + 2)
                            for half in range(2):
                                for f in range(FB):
                                    mm = pe.matmul(bank[6 + half][0:C, :], hid[:, f, :],
                                                   wc[:, f, half * W:(half + 1) * W],
                                                   start=(f == 0), stop=(f == FB - 1))
                                if half == 0:
                                    mm.then_inc(m["down_half"], 1)
                            mm.then_inc(m["down_half"], 1)
                total = pe.value_load(tab_i[0:1, 2 * NE:2 * NE + 1], min_val=NE, max_val=2 * NE)
                pe.wait_ge(m["y0_ready"], total + 1)
                pe.wait_ge(m["y1_ready"], total + 1)
                pe.wait_ge(m["s_ready"], total + 1)
                scatter(last=True)

            if NSUB >= 2:
                moe(0, 1)
            if NSUB >= 3:
                modulation(1)
                norm(2)
                pe.wait_ge(h_ready, 3)
                _, sa = take(1, 12)
                _, sl = take(1, 13)
                wa, wl = weight(sa), weight(sl)
                first = [wa[:, 0:512].rearrange("p (k n) -> p k n", k=KB),
                         wa[:, 512:1024].rearrange("p (k n) -> p k n", k=KB),
                         wa[:, 1024:2048].rearrange("p (k n) -> p k n", k=KB)]
                second = [wl[0:64, 0:D], wl[0:64, D:2 * D], wl[:, 2 * D:3 * D]]
                rank = [64, 64, P]
                for i in range(3):
                    pe.wait_ge(mix_ready, i + 1)
                    for k in range(KB):
                        mm = pe.matmul(bank[4][0:rank[i], 0:S], first[i][:, k, :], mixed[i % 2][:, k, :],
                                       start=(k == 0), stop=(k == KB - 1))
                    mm.then_inc(lora_full, 1)
                    pe.wait_ge(lora_evac, i + 1)
                    for u in range(4):
                        ps = proj_bank()
                        for c in range(2):
                            d = 2 * u + c
                            mm = pe.matmul(ps[:, c * S:(c + 1) * S], second[i][:, d * P:(d + 1) * P],
                                           lora[i][0:rank[i], :], start=True, stop=True)
                        mm.then_inc(proj_full, 1)
                for n, i in enumerate((1, 0, 2)):
                    pe.wait_ge(mix_ready, 4 + n)
                    for j in range(2):
                        _, slot = take(1, 14 + 2 * n + j)
                        (project_N if i == 2 else project_T)(slot, mixed[(3 + n) % 2])

                def head_sums(ps, src):
                    for pr in range(KB):
                        for tt in range(NT):
                            r = tt * NH + 2 * pr
                            mm = pe.matmul(ps[:, r:r + 2], src[:, pr, tt, :], halves[:], start=True, stop=True)
                    return mm

                def head_rows(ps, colsrc, pr):
                    for tt in range(NT):
                        for hh in range(2):
                            r = tt * NH + 2 * pr + hh
                            mm = pe.matmul(ps[hh * HEAD:(hh + 1) * HEAD, tt * P:(tt + 1) * P],
                                           colsrc[:, r:r + 1].to_broadcast([P, HEAD]), ident[:],
                                           start=True, stop=True)
                    return mm

                def head_rows_ring(colsrc, base):
                    for u in range(4):
                        if u >= 2:
                            pe.wait_ge(bcast_used, base + u - 1)
                        for c in range(2):
                            mm = head_rows(bank[6 + u % 2][:, c * S:(c + 1) * S], colsrc, 2 * u + c)
                        mm.then_inc(head_bcast, 1)

                pe.wait_ge(kk_sq, 1)
                head_sums(bank[4], by_tile(3)).then_inc(head_sum, 1)
                pe.wait_ge(rk_ready, 1)
                head_sums(bank[5], by_tile(4)).then_inc(head_sum, 1)
                pe.wait_ge(head_rstd, 3)
                head_rows_ring(rstd, 4)
                pe.wait_ge(rw_ops, 4)

                nsc = [0]

                def rscore_bank():
                    m = nsc[0]
                    if m >= 2:
                        pe.wait_ge(rsc_evac, m - 1)
                    nsc[0] += 1
                    return bank[m % 2]

                def pair_scores(pr):
                    for kind, keys in ((0, rwK), (1, rwB)):
                        for hh in range(2):
                            ps = rscore_bank()
                            fs = slice(hh * HEAD, (hh + 1) * HEAD)
                            for tt in range(NT):
                                mm = pe.matmul(ps[:, tt * S:(tt + 1) * S], keys[fs, pr, tt, :],
                                               AR[fs, pr, tt, :, :], start=True, stop=True)
                            mm.then_inc(rsc_full, 1)
                    pe.wait_ge(kc_ready, pr + 1)
                    for hh in range(2):
                        ps = rscore_bank()
                        fs = slice(hh * HEAD, (hh + 1) * HEAD)
                        for kind in range(2):
                            mm = pe.matmul(ps[:, kind * S:(kind + 1) * S], kcross(pr, kind)[fs, :],
                                           AR[fs, pr, 1, :, :], start=True, stop=True)
                        mm.then_inc(rsc_full, 1)

                def invert(jj):
                    prs = (2 * jj, 2 * jj + 1)
                    for pr in prs:
                        pe.wait_ge(xt1_ready, pr + 1)
                        for u in range(4):
                            mm = pe.transpose(bank[4 + 2 * (pr % 2)][:, u * P:(u + 1) * P],
                                              xinvT(pr)[:, u * P:(u + 1) * P], ident[:])
                        mm.then_inc(x1_full, 1)
                    for i in range(1, 7):
                        for pr in prs:
                            n = jj * 12 + 2 * (i - 1) + pr % 2
                            pe.wait_ge(lm_ready, n + 1)
                            if i == 1:
                                pe.wait_ge(x1_ready, pr + 1)
                            else:
                                pe.wait_ge(xm_ready, n - 1)
                            for u in range(4):
                                us = slice(u * P, (u + 1) * P)
                                mm = pe.matmul(bank[2 + pr % 2][:, us], lmask(pr, i)[:, us], xinv(pr)[:, us],
                                               start=True, stop=True)
                            mm.then_inc(tm_full, 1)
                        for pr in prs:
                            n = jj * 12 + 2 * (i - 1) + pr % 2
                            pe.wait_ge(tm_ready, n + 1)
                            for u in range(4):
                                us = slice(u * P, (u + 1) * P)
                                mm = pe.matmul(bank[5 + 2 * (pr % 2)][:, us], tmid(pr)[:, us], xinvT(pr)[:, us],
                                               start=True, stop=True)
                            if i < 6:
                                for u in range(4):
                                    us = slice(u * P, (u + 1) * P)
                                    mm = pe.matmul(bank[4 + 2 * (pr % 2)][:, us], xinvT(pr)[:, us],
                                                   tmid(pr)[:, us], start=True, stop=True)
                            mm.then_inc(xm_full, 1)

                def solve(pr):
                    n = (pr // 2) * 12 + 10 + pr % 2
                    pe.wait_ge(xm_ready, n + 1)
                    bw = bank[2 + pr % 2]
                    for tt in range(NT):
                        for hh in range(2):
                            o = bw[:, hh * HEAD:(hh + 1) * HEAD]
                            h = 2 * pr + hh
                            mm = pe.matmul(o, sc(pr, 0, tt, hh), vN1[:, tt, h, :], start=True, stop=(tt == 0))
                            if tt:
                                pe.matmul(o, scro(pr, 0, hh), vN1[:, 0, h, :], start=False, stop=False)
                                mm = pe.matmul(o, scro(pr, 2, hh), uneg(pr, 0)[:, hh * HEAD:(hh + 1) * HEAD],
                                               start=False, stop=True)
                        mm.then_inc(w_full, 1)
                        pe.wait_ge(w_ready, 2 * pr + tt + 1)
                        for hh in range(2):
                            mm = pe.matmul(bw[:, P + hh * HEAD:P + (hh + 1) * HEAD],
                                           xinvT(pr)[:, (2 * tt + hh) * P:(2 * tt + hh + 1) * P],
                                           tmid(pr)[:, (2 * tt + hh) * HEAD:(2 * tt + hh + 1) * HEAD],
                                           start=True, stop=True)
                        mm.then_inc(u_full, 1)
                        pe.wait_ge(u_ready, 2 * pr + tt + 1)
                    for hh in range(2):
                        h = 2 * pr + hh
                        o = bank[4 + 2 * (pr % 2)][hh * HEAD:(hh + 1) * HEAD, :]
                        un = lambda tt: uneg(pr, tt)[:, hh * HEAD:(hh + 1) * HEAD]
                        pe.matmul(o[:, 0:P], vN1[:, 0, h, :], sc(pr, 1, 0, hh), start=True, stop=False)
                        pe.matmul(o[:, 0:P], un(0), sc(pr, 3, 0, hh), start=False, stop=True)
                        pe.matmul(o[:, P:S], vN1[:, 1, h, :], sc(pr, 1, 1, hh), start=True, stop=False)
                        pe.matmul(o[:, P:S], un(1), sc(pr, 3, 1, hh), start=False, stop=False)
                        pe.matmul(o[:, P:S], vN1[:, 0, h, :], scro(pr, 1, hh), start=False, stop=False)
                        mm = pe.matmul(o[:, P:S], un(0), scro(pr, 3, hh), start=False, stop=True)
                    mm.then_inc(ry_full, 1)

                pe.wait_ge(proj_evac, 26 + 12 + 12)
                pe.wait_ge(bcast_used, 8)
                for jj in range(KB // 2):
                    for pr in (2 * jj, 2 * jj + 1):
                        pair_scores(pr)
                    if jj > 0:
                        pe.wait_ge(ry_ready, 2 * jj)
                    invert(jj)
                    for pr in (2 * jj, 2 * jj + 1):
                        solve(pr)

                pe.wait_ge(ry_ready, KB)

                head_sums(bank[4], oR).then_inc(head_sum, 1)
                pe.wait_ge(gn_mean, 1)
                head_rows_ring(gm_mean, 8)
                pe.wait_ge(gn_sq, 1)
                head_sums(bank[4], by_tile(3)).then_inc(head_sum, 1)
                pe.wait_ge(head_rstd, 4)
                pe.wait_ge(bcast_used, 12)
                head_rows_ring(rstd, 12)
                pe.wait_ge(bv_ready, 1)
                pe.wait_ge(ry_ready, KB)
                for pr in range(KB):
                    for tt in range(NT):
                        mm = pe.transpose(bank[pr // 2][:, (pr % 2) * S + tt * P:(pr % 2) * S + (tt + 1) * P],
                                          bvN[:, tt, 2 * pr:2 * pr + 2, :].rearrange("p h n -> p (h n)"), ident[:])
                mm.then_inc(bvT_full, 1)
                pe.wait_ge(og_ready, 1)
                og = blocks(4)
                out_projection(1, 20, 2, lambda i: og[:, i, :], lambda j: None)
            if NSUB >= 4:
                moe(1, 3)
            norm(NSUB)
            pe.wait_ge(h_ready, NSUB + 1)
            for u in range(8):
                tt, q = u // 4, u % 4
                for c in range(2):
                    mm = pe.transpose(bank[u][:, c * P:(c + 1) * P],
                                      hT[:, 2 * q + c, tt * P:(tt + 1) * P], ident[:])
                mm.then_inc(o_full, 1)

        @block.scalar
        def _(act):
            count = [0]

            def link(ins):
                count[0] += 1
                ins.then_inc(act_chain, 1)
                act.wait_ge(act_chain, count[0])

            act.wait_ge(vrows_zeroed, 1)
            for name, (g, r, n) in VEC.items():
                src = t[name]
                flat = src.rearrange({1: "a -> a", 2: "a b -> (a b)", 3: "a b c -> (a b c)"}[len(src.shape)])
                act.dma_start(vrows[r:r + n, g, :], flat.rearrange("(n p) -> n p", p=P)).then_inc(vec_landed, 16)
            act.dma_start(xN[:, :, :], t["x"][0].rearrange("(t p) d -> p t d", p=P)).then_inc(x_landed, 16)
            act.dma_start(dt_bias[:], t["ev_dt_bias"].rearrange("a h -> h a")).then_inc(small_landed, 16)
            act.dma_start(a_log[:], t["ev_a_log"].rearrange("a h -> h a")).then_inc(small_landed, 16)
            skip = t["ev_d_skip"].rearrange("a (j two) -> two (a j)", two=2)
            for hh in range(2):
                act.dma_start(dskip[hh * HEAD:(hh + 1) * HEAD, :],
                              skip[hh:hh + 1, :].to_broadcast([HEAD, KB])).then_inc(small_landed, 16)
            act.dma_start(w_dt[:], row_block(t["ev_w_in"][0])[:, :, IN_COLS - NH:IN_COLS]).then_inc(small_landed, 16)
            act.dma_start(router_w[:], row_block(t["router_w"])).then_inc(small_landed, 16)
            act.dma_start(router_b[:], t["router_b"].rearrange("(a e) -> a e", a=1).to_broadcast([P, NE])
                          ).then_inc(small_landed, 16)

            act.wait_ge(vec_cols, 1)
            act.activation(csilu[:], cols("c", 0, KB), ACT.Silu).then_inc(csilu_ready, 1)
            for u in range(4):
                act.wait_ge(xT_psum, u + 1)
                ins = act.activation(xT[:, 2 * u:2 * u + 2, :].rearrange("p k s -> p (k s)"), bank[u][:], ACT.Copy)
            ins.then_inc(xT_evac, 1)
            act.wait_ge(consts, 1)

            def norm(k):
                if k == 0:
                    act.wait_ge(xT_evac, 1)
                else:
                    act.wait_ge(x_ready, k)
                act.activation(squares[:, :, :], xT[:, :, :], ACT.Square).then_inc(sq_ready, 1)
                act.wait_ge(sums_psum, k + 1)
                act.activation(rs_root[:, 0:NT], bank[7][:, 0:NT], ACT.Sqrt, bias=eps_col[:, 0:1],
                               scale=1.0 / D).then_inc(root_ready, 1)

            norm(0)
            evac = [0]

            def evacuate(dst, func=ACT.Copy, **kw):
                n = evac[0]
                act.wait_ge(proj_full, n + 1)
                act.activation(dst, bank[n % 4][:], func, **kw).then_inc(proj_evac, 1)
                evac[0] += 1

            def evac_T(dst, first):
                for u in range(2):
                    b = first + 2 * u
                    evacuate(dst[:, b:b + 2, :].rearrange("p k s -> p (k s)"), ACT.Copy)

            act.wait_ge(lb_max, 1)
            act.activation(lbe[:], lbe[:], ACT.Exp).then_inc(start_exp, 1)
            act.wait_ge(small_landed, 16 * 7)
            act.activation(a_neg[:], a_log[:], ACT.Exp).then_inc(start_exp, 1)
            for u in range(4):
                n = evac[0]
                act.wait_ge(proj_full, n + 1)
                act.activation(fT[:, 2 * u:2 * u + 2, :].rearrange("p k s -> p (k s)"), bank[n % 4][:],
                               ACT.Sigmoid).then_inc(proj_evac, 1)
                evac[0] += 1
            act.wait_ge(k_ready, 1)
            act.activation(fT[:, :, :], fT[:, :, :], ACT.Ln).then_inc(logf_ready, 1)
            evac_T(qT, 0)
            evac_T(qT, 4)

            def level_exp(i):
                act.wait_ge(dl_ready, i + 1)
                act.wait_ge(dr_ready, i + 1)
                act.activation(buf(eT[i % 2]), buf(eT[i % 2]), ACT.Exp).then_inc(el_exp, 1)

            def evac_v(j):
                for tt in range(NT):
                    evacuate(vN[:, tt, j * W:(j + 1) * W])

            def evac_xbc(first):
                for u in range(2):
                    n = evac[0]
                    b = first + 2 * u
                    act.wait_ge(conv_zero, 1)
                    act.wait_ge(proj_full, n + 1)
                    act.activation(xpad[:, b:b + 2, TAPS - 1:],
                                   bank[n % 4][:].rearrange("p (k s) -> p k s", k=2), ACT.Copy).then_inc(proj_evac, 1)
                    evac[0] += 1

            level_exp(0)
            evac_v(0)
            level_exp(1)
            evac_v(1)
            level_exp(2)
            evac_xbc(8)
            level_exp(3)
            evac_xbc(0)
            level_exp(4)
            evac_xbc(4)
            level_exp(5)
            act.wait_ge(dtz, 1)
            act.activation(dts[:, 1, :], dts[:, 0, :], ACT.Abs).then_inc(dtabs, 1)
            act.wait_ge(dtabs, 1)
            link(act.activation(dts[:, 1, :], dts[:, 1, :], ACT.Exp, scale=-1.0))
            act.activation(dts[:, 2, :], dts[:, 1, :], ACT.Ln, bias=1.0).then_inc(dtln, 1)
            evac_T(zT, 0)
            level_exp(6)
            evac_T(zT, 4)
            level_exp(7)
            evac_T(gT, 0)
            evac_T(gT, 4)
            act.wait_ge(proj_evac, 26)
            act.wait_ge(conv_done, XBLK)
            act.activation(xpad[:, :, TAPS - 1:], xpad[:, :, TAPS - 1:], ACT.Silu).then_inc(conv_silu, 1)
            act.activation(buf(10), buf(10), ACT.Silu)
            act.activation(buf(11), buf(11), ACT.Silu).then_inc(silu_g, 1)
            for u in range(4):
                act.wait_ge(o_full, u + 1)
                dst = lambda x: x[:, 2 * u:2 * u + 2, :].rearrange("p k s -> p (k s)")
                act.activation(dst(oa), bank[6 + u % 2][:], ACT.Copy)
                act.activation(dst(fT), bank[6 + u % 2][:], ACT.Square).then_inc(o_evac, 1)
            act.wait_ge(head_sum, 1)
            act.activation(rs_root[:, 0:2 * KB], bank[4][:, 0:2 * KB], ACT.Sqrt, bias=eps_col[:, 0:1],
                           scale=1.0 / P).then_inc(head_root, 1)
            for h in range(NH):
                act.wait_ge(dec_diff, h + 1)
                act.activation(dec[:, h % NDEC, :], dec[:, h % NDEC, :], ACT.Exp).then_inc(dec_exp, 1)
            act.wait_ge(y_ready, KB)
            act.wait_ge(head_sum, 1)
            act.activation(fT[:, :, :], yT[:, :, :], ACT.Square).then_inc(ysq_ready, 1)
            act.wait_ge(head_sum, 2)
            act.activation(rs_root[:, 0:4], bank[4][:, 0:4], ACT.Sqrt, bias=eps_col[:, 0:1],
                           scale=1.0 / (4 * P)).then_inc(head_root, 1)

            def moe(l, k):
                m = M[l]
                norm(k)
                for u in range(4):
                    tt, half = u // 2, u % 2
                    act.wait_ge(m["hN_full"], u + 1)
                    act.activation(hN[:, tt, half * W:(half + 1) * W], bank[4 + u][:], ACT.Copy).then_inc(m["hN_evac"], 1)
                act.wait_ge(m["lmax"], 1)
                act.activation(small(1), small(1), ACT.Exp).then_inc(m["lexp"], 1)
                act.wait_ge(m["slot_full"], 1)
                for r in range(2):
                    ins = act.activation(rows4[:, 2 * r:2 * r + 2, :].rearrange("p r s -> p (r s)"),
                                         bank[2 + r][0:C, :], ACT.Copy)
                ins.then_inc(m["rows_ready"], 1)
                act.wait_ge(m["gath_full"], 1)
                act.activation(hgT[:, :, :].rearrange("p k c -> p (k c)"), bank[4][:], ACT.Copy).then_inc(m["hg_ready"], 1)
                total = act.value_load(tab_i[0:1, 2 * NE:2 * NE + 1], min_val=NE, max_val=2 * NE)
                with act.Fori(0, total) as g:
                    act.wait_ge(m["up_done"], g + 1)
                    act.wait_ge(m["hid_ready"], g + 1)
                    act.activation(hsil[:, :, :].rearrange("p f c -> p (f c)"), bank[5][:, 0:FB * C],
                                   ACT.Silu).then_inc(m["silu_done"], 1)
                    act.wait_ge(m["gath_full"], g + 2)
                    act.activation(hgT[:, :, :].rearrange("p k c -> p (k c)"), bank[4][:],
                                   ACT.Copy).then_inc(m["hg_ready"], 1)
                    act.wait_ge(m["down_half"], g * 2 + 1)
                    act.wait_ge(m["scat_done"], g + 2)
                    act.activation(ymoe[:, 0:W], bank[6][0:C, :], ACT.Copy).then_inc(m["y0_ready"], 1)

            if NSUB >= 2:
                moe(0, 1)
            if NSUB >= 3:
                norm(2)
                lora_func = [ACT.Tanh, ACT.Copy, ACT.Sigmoid]
                for i, (dst, bias) in enumerate(((sgT, "od_w_dec0"), (aT, "od_a0"), (ggT, None))):
                    r = P if i == 2 else 64
                    act.wait_ge(lora_full, i + 1)
                    act.activation(lora[i][0:r, :], bank[4][0:r, 0:S], lora_func[i]).then_inc(lora_evac, 1)
                    for u in range(4):
                        n = evac[0]
                        act.wait_ge(proj_full, n + 1)
                        if bias is None:
                            ins = act.activation(dst[:, 2 * u:2 * u + 2, :].rearrange("p k s -> p (k s)"),
                                                 bank[n % 4][:], ACT.Copy)
                        else:
                            for c in range(2):
                                b = 2 * u + c
                                ins = act.activation(dst[:, b, :], bank[n % 4][:, c * S:(c + 1) * S], ACT.Sigmoid,
                                                     bias=col(bias, b))
                        ins.then_inc(proj_evac, 1)
                        evac[0] += 1
                evac_T(k1T, 0)
                evac_T(k1T, 4)
                evac_T(rT, 0)
                evac_T(rT, 4)
                for j in range(2):
                    for tt in range(NT):
                        evacuate(vN1[:, tt, 8 * j:8 * j + 8, :].rearrange("p h n -> p (h n)"))
                act.wait_ge(head_sum, 3)
                act.activation(rs_root[:], bank[4][:, 0:2 * NH], ACT.Sqrt).then_inc(head_root, 1)
                act.wait_ge(rw_diff, 2)
                act.activation(buf(3), buf(4), ACT.Exp, scale=-E05).then_inc(rw_exp, 1)
                act.activation(buf(10), buf(10), ACT.Exp, scale=-E05).then_inc(rw_exp, 1)
                act.wait_ge(rw_exp, 1)
                act.activation(buf(4), buf(4), ACT.Exp, scale=E05).then_inc(rw_exp, 1)
                act.wait_ge(kmid_diff, 1)
                act.activation(kmid[:], kmid[:], ACT.Exp, scale=E05).then_inc(kmid_ready, 1)
                for i in range(KB // 2 * 12):
                    jj, r = i // 12, i % 12
                    pr = 2 * jj + r % 2
                    act.wait_ge(tm_full, i + 1)
                    act.activation(tmid(pr), bank[2 + pr % 2][:], ACT.Copy).then_inc(tm_ready, 1)
                    if r == 11:
                        for q in (2 * jj, 2 * jj + 1):
                            for tt in range(NT):
                                act.wait_ge(w_full, 2 * q + tt + 1)
                                act.activation(tmid(q)[:, tt * P:(tt + 1) * P], bank[2 + q % 2][:, 0:P],
                                               ACT.Copy).then_inc(w_ready, 1)
                                act.wait_ge(u_full, 2 * q + tt + 1)
                                act.activation(uneg(q, tt), bank[2 + q % 2][:, P:2 * P], ACT.Copy,
                                               scale=-1.0).then_inc(u_ready, 1)
                act.wait_ge(bcast_used, 12)
                act.activation(buf(3).rearrange("p (k t s) -> p k t s", k=KB, t=NT), oR, ACT.Square).then_inc(gn_sq, 1)
                act.wait_ge(head_sum, 6)
                act.activation(rs_root[:], bank[4][:, 0:2 * NH], ACT.Sqrt, bias=eps_col[:, 1:2],
                               scale=1.0 / HEAD).then_inc(head_root, 1)
            if NSUB >= 4:
                moe(1, 3)
            norm(NSUB)
            for u in range(8):
                tt, q = u // 4, u % 4
                act.wait_ge(o_full, 4 + u + 1)
                act.activation(hN[:, tt, 2 * q * P:(2 * q + 2) * P], bank[u][:, 0:S],
                               ACT.Copy).then_inc(o_evac, 1)

        @block.vector
        def _(dve):
            count = [0]

            def link(ins):
                count[0] += 1
                ins.then_inc(dve_chain, 1)
                dve.wait_ge(dve_chain, count[0])

            tt_ = dve.tensor_tensor
            ts_ = dve.tensor_scalar
            stt = dve.scalar_tensor_tensor

            dve.memset(vrows[:], 0.0).then_inc(vrows_zeroed, 1)
            dve.wait_ge(vec_T, 1)
            dve.tensor_copy(vcols[:].rearrange("p g r -> p (g r)"), bank[4][:, 0:3 * P]).then_inc(vec_cols, 1)
            dve.wait_ge(vec_cols, 1)
            lg = cols("hg_lb_logits", 0, 3 * KB).rearrange("p (r k) -> p r k", r=3)
            link(tt_(lbm[:], lg[:, 0, :], lg[:, 1, :], ALU.max))
            link(tt_(lbm[:], lbm[:], lg[:, 2, :], ALU.max))
            tt_(lbe[:], lg, lbm[:].unsqueeze(1).to_broadcast([P, 3, KB]), ALU.subtract).then_inc(lb_max, 1)
            dve.wait_ge(start_exp, 1)
            link(tt_(lbm[:], lbe[:, 0, :], lbe[:, 1, :], ALU.add))
            link(tt_(lbm[:], lbm[:], lbe[:, 2, :], ALU.add))
            link(dve.reciprocal(lbm[:], lbm[:]))
            link(tt_(lb[:], lbe[:, 1, :], lbm[:], ALU.mult))
            link(ts_(oml[:], lb[:], -1.0, 1.0, ALU.mult, ALU.add))

            def modulation(l):
                dve.wait_ge(tile_used, (USED[0] if l else 0) + 12)
                link(tt_(modT[:, l, :], bank[5][:, 0:48], cols("mod_b", 48 * l, 48 * l + 48), ALU.add))
                for f in range(2):
                    link(ts_(gain[:, l, f, :], modT[:, l, (3 * f + 1) * KB:(3 * f + 2) * KB], 1.0, None, ALU.add))
                    link(tt_(gain[:, l, f, :], gain[:, l, f, :], cols("norm_w", (2 * l + f) * KB, (2 * l + f + 1) * KB),
                             ALU.mult))

            def norm(k):
                dve.wait_ge(root_ready, k + 1)
                dve.reciprocal(rstd[:, 0:NT], rs_root[:, 0:NT]).then_inc(rstd_ready, 1)
                dve.wait_ge(bcast_psum, k + 1)
                link(tt_(hT[:, :, :], xT[:, :, :], bank[6][:, 0:S].unsqueeze(1).to_broadcast([P, KB, S]), ALU.mult))
                for b in range(KB):
                    if k == NSUB:
                        ins = ts_(hT[:, b, :], hT[:, b, :], col("final_norm_w", b), None, ALU.mult)
                    else:
                        l, f = k // 2, k % 2
                        sh = modT[:, l, 3 * f * KB + b:3 * f * KB + b + 1]
                        ins = ts_(hT[:, b, :], hT[:, b, :], gain[:, l, f, b:b + 1], sh, ALU.mult, ALU.add)
                ins.then_inc(h_ready, 1)

            def residual(k):
                l, f = k // 2, k % 2
                for b in range(KB):
                    gt = modT[:, l, (3 * f + 2) * KB + b:(3 * f + 2) * KB + b + 1]
                    ins = stt(xT[:, b, :], bank[b // 2][:, (b % 2) * S:(b % 2 + 1) * S], gt, xT[:, b, :],
                              ALU.mult, ALU.add)
                ins.then_inc(x_ready, 1)

            modulation(0)
            dve.wait_ge(xT_evac, 1)
            norm(0)

            dve.wait_ge(proj_evac, 4)
            for b in range(KB):
                ins = ts_(fT[:, b, :], fT[:, b, :], oml[:, b:b + 1], lb[:, b:b + 1], ALU.mult, ALU.add)
            link(ins)
            ts_(kT[:, :, :], fT[:, :, :], -1.0, 1.0, ALU.mult, ALU.add).then_inc(k_ready, 1)
            dve.wait_ge(consts, 1)
            dve.wait_ge(logf_ready, 1)
            for b in range(KB):
                ins = dve.tensor_tensor_scan(bT[:, b, :], ones[:, 0:S], fT[:, b, :], 0.0, ALU.mult, ALU.add)
            ins.then_inc(b_ready, 1)
            dve.wait_ge(b_ready, 1)

            def level_diff(i):
                h = (HALVES + [P])[i]
                e = buf(eT[i % 2]).rearrange("p (b two h) -> p b two h", two=2, h=h)
                b = buf(5).rearrange("p (b two h) -> p b two h", two=2, h=h)
                if i >= 2:
                    dve.wait_ge(score_full, 4 + 2 * (i - 1))
                mid = b[:, :, 0, h - 1:h].to_broadcast([P, KB * S // (2 * h), h])
                tt_(e[:, :, 1, :], b[:, :, 1, :], mid, ALU.subtract).then_inc(dr_ready, 1)

            def level_mult(i):
                h = (HALVES + [P])[i]
                e = buf(eT[i % 2]).rearrange("p (b two h) -> p b two h", two=2, h=h)
                q = buf(2).rearrange("p (b two h) -> p b two h", two=2, h=h)
                dve.wait_ge(el_exp, i + 1)
                dve.wait_ge(proj_evac, 8)
                tt_(e[:, :, 1, :], e[:, :, 1, :], q[:, :, 1, :], ALU.mult).then_inc(eq_ready, 1)

            def level_take(i):
                h = HALVES[i]
                for tt in range(NT):
                    m = 4 + 2 * i + tt
                    dve.wait_ge(score_full, m + 1)
                    src = bank[4 + m % 2][:].rearrange("p (u s) -> p u s", s=64)
                    dst = scd[:, tt, :, :].rearrange("p u (b two h) -> p u b two h", two=2, h=h)[:, :, :, 1, :]
                    mk = level[:, i, :].rearrange("p (b two h) -> p b two h", two=2, h=h)[:, :, 1, :]
                    ins = dve.copy_predicated(dst, mk.unsqueeze(1).to_broadcast([P, KB, 64 // h, h]).bitcast(I32),
                                              src.rearrange("p u (b h) -> p u b h", h=h))
                    ins.then_inc(score_evac, 1)

            level_diff(0)
            level_diff(1)
            for r in range(2):
                for tt in range(NT):
                    m = 2 * r + tt
                    dve.wait_ge(score_full, m + 1)
                    tt_(scd[:, tt, 4 * r:4 * r + 4, :], bank[4 + m % 2][:].rearrange("p (u s) -> p u s", u=4),
                        ident[:].unsqueeze(1).to_broadcast([P, 4, P]), ALU.mult).then_inc(score_evac, 1)
            dve.wait_ge(score_evac, 4)
            for i in range(8):
                level_mult(i)
                if i < 7:
                    level_take(i)
                if i + 2 < 8:
                    level_diff(i + 2)
                if i == 5:
                    dve.wait_ge(dt_full, 1)
                    dve.wait_ge(small_landed, 16 * 7)
                    ts_(dts[:, 0, :], bank[6][0:NH, 0:S], dt_bias[:], None, ALU.add).then_inc(dtz, 1)
                if i == 6:
                    dve.wait_ge(start_exp, 2)
                    dve.wait_ge(dtln, 1)
                    link(stt(dts[:, 3, :], dts[:, 0, :], 0.0, dts[:, 2, :], ALU.max, ALU.add))
                    link(ts_(dts[:, 2, :], dts[:, 3, :], a_neg[:], -1.0, ALU.mult, ALU.mult))
                    dve.tensor_tensor_scan(dts[:, 4, :], ones[0:NH, 0:S], dts[:, 2, :], 0.0, ALU.mult,
                                           ALU.add).then_inc(dt_ready, 1)
            for r in range(2):
                m = 18 + r
                dve.wait_ge(score_full, m + 1)
                dve.tensor_copy(scx[:, 4 * r:4 * r + 4, :].rearrange("p u s -> p (u s)"),
                                bank[4 + m % 2][:]).then_inc(score_evac, 1)
            dve.wait_ge(proj_evac, 18)
            for b in range(XBLK):
                tmp = ctmp[:, b % 2, :]
                wt = lambda j: col("ev_conv_w", j * XBLK + b)
                link(ts_(tmp, xpad[:, b, 0:S], wt(0), col("ev_conv_b", b), ALU.mult, ALU.add))
                for j in range(1, TAPS - 1):
                    link(stt(tmp, xpad[:, b, j:j + S], wt(j), tmp, ALU.mult, ALU.add))
                stt(xpad[:, b, TAPS - 1:], xpad[:, b, TAPS - 1:], wt(TAPS - 1), tmp, ALU.mult,
                    ALU.add).then_inc(conv_done, 1)
            dve.wait_ge(dtN_full, 1)
            dve.tensor_copy(dtN[:].rearrange("p a t h -> p (a t h)"), bank[4][:, 0:4 * NH]).then_inc(dtN_ready, 1)
            dve.wait_ge(dtN_ready, 1)
            for u in range(4):
                tt, half = u // 2, u % 2
                dve.wait_ge(xs_full, u + 1)
                tt_(xdt[:, tt, half * W:(half + 1) * W].rearrange("p (h n) -> p h n", n=HEAD),
                    bank[[5, 6, 7, 5][u]][:].rearrange("p (h n) -> p h n", n=HEAD),
                    dtN[:, 0, tt, 8 * half:8 * half + 8].unsqueeze(2).to_broadcast([P, 8, HEAD]),
                    ALU.mult).then_inc(xdt_ready, 1)
            for g in range(GROUPS):
                dve.wait_ge(cb_full, g + 1)
                ps = bank[6 + g]
                tt_(cbm[:, g, 0:P], ps[:, 0:P], causal[:], ALU.mult)
                tt_(cbm[:, g, 2 * P:3 * P], ps[:, S:S + P], causal[:], ALU.mult)
                dve.tensor_copy(cbm[:, g, P:S], ps[:, P:S]).then_inc(cb_ready, 1)
            dve.wait_ge(head_root, 1)
            dve.reciprocal(rstd[:, 0:2 * KB], rs_root[:, 0:2 * KB]).then_inc(head_rstd, 1)
            dve.wait_ge(silu_g, 1)
            for u in range(4):
                dve.wait_ge(head_bcast, u + 1)
                o = oa[:, 2 * u:2 * u + 2, :].rearrange("p k s -> p (k s)")
                ins = tt_(o, o, bank[4 + u % 2][:], ALU.mult)
                ins.then_inc(bcast_used, 1)
            dve.wait_ge(bcast_used, 4)
            for h in range(KB):
                ins = stt(oa[:, h, :], oa[:, h, :], col("ev_hg_norm", h), gT[:, h, :], ALU.mult, ALU.mult)
            ins.then_inc(oa_ready, 1)

            def decay_diff(h):
                dve.wait_ge(row_full, h + 1)
                if h >= NDEC:
                    dve.wait_ge(y_full, h - NDEC + 1)
                row = bank[4 + h % 2]
                dd = dec[:, h % NDEC, :]
                ts_(dd[:, 0:S], row[:, 0:S], dtN[:, 1, 0, h:h + 1], 0.0, ALU.subtract, ALU.min)
                ts_(dd[:, S:S + P], row[:, P:S], dtN[:, 1, 1, h:h + 1], 0.0, ALU.subtract,
                    ALU.min).then_inc(dec_diff, 1)

            def decay_mult(h):
                dve.wait_ge(dec_exp, h + 1)
                dd = dec[:, h % NDEC, :]
                tt_(dd, dd, cbm[:, h // 8, :], ALU.mult).then_inc(dec_mat, 1)

            def ssd_out(pr):
                dve.wait_ge(y_full, 2 * pr + 2)
                link(stt(yT[:, pr, :], xpad[:, pr, TAPS - 1:], dskip[:, pr:pr + 1], bank[6 + pr % 2][:, 0:S],
                         ALU.mult, ALU.add))
                tt_(yT[:, pr, :], yT[:, pr, :], zT[:, pr, :], ALU.mult).then_inc(y_ready, 1)

            dve.wait_ge(cb_ready, 2)
            for h in range(NH + 4):
                if h < NH:
                    decay_diff(h)
                if 1 <= h <= NH:
                    decay_mult(h - 1)
                if h >= 4 and h % 2 == 1:
                    ssd_out((h - 4) // 2)
            dve.wait_ge(head_root, 2)
            dve.reciprocal(rstd[:, 0:4], rs_root[:, 0:4]).then_inc(head_rstd, 1)
            dve.wait_ge(yb_full, 1)
            for b in range(KB):
                g = b // 4
                ins = stt(yT[:, b, :], yT[:, b, :], col("ev_ssm_norm", b), bank[5][:, g * S:(g + 1) * S],
                          ALU.mult, ALU.mult)
            ins.then_inc(ob_ready, 1)
            dve.wait_ge(tile_used, USED[0])
            residual(0)

            def first_of(dst, vals, top, shape, scratch):
                link(tt_(dst, vals, top, ALU.is_equal))
                link(ts_(scratch[0], dst, -4.0, 4.0, ALU.mult, ALU.add))
                link(tt_(scratch[0], scratch[0], shape[0], ALU.add))
                link(dve.tensor_reduce(scratch[1], scratch[0], AX.X, ALU.min))
                link(tt_(dst, shape[0], scratch[1].unsqueeze(len(scratch[1].shape)).to_broadcast(shape[1]),
                         ALU.is_equal))

            def moe(l, k):
                m = M[l]
                norm(k)
                v3 = lambda i: small(i).rearrange("p (t e) -> p t e", t=NT)
                v8 = lambda i: small(i).rearrange("p (a e) -> p a e", e=4)
                dve.wait_ge(m["logit_full"], 1)
                dve.wait_ge(small_landed, 16 * 7)
                link(tt_(v3(0), bank[0][:, 0:2 * NE].rearrange("p (t e) -> p t e", t=NT),
                         router_b[:].unsqueeze(1).to_broadcast([P, NT, NE]), ALU.add))
                mx = small(20)[:, 0:2]
                link(dve.tensor_reduce(mx, v3(0), AX.X, ALU.max))
                tt_(v3(1), v3(0), mx.unsqueeze(2).to_broadcast([P, NT, NE]), ALU.subtract).then_inc(m["lmax"], 1)
                dve.wait_ge(m["lexp"], 1)
                sm = small(20)[:, 2:4]
                link(dve.tensor_reduce(sm, v3(1), AX.X, ALU.add))
                link(dve.reciprocal(sm, sm))
                link(tt_(v3(2), v3(1), sm.unsqueeze(2).to_broadcast([P, NT, NE]), ALU.mult))
                p8 = v8(2)
                pos = tie4[:].unsqueeze(1).to_broadcast([P, 8, 4])
                t1, t2 = small(20)[:, 8:16], small(20)[:, 16:24]
                scr = (v8(5), small(20)[:, 24:32])
                b8 = lambda x: x.unsqueeze(2).to_broadcast([P, 8, 4])
                link(dve.tensor_reduce(t1, p8, AX.X, ALU.max))
                first_of(v8(3), p8, b8(t1), (pos, [P, 8, 4]), scr)
                link(stt(v8(6), v8(3), -2.0, p8, ALU.mult, ALU.add))
                link(dve.tensor_reduce(t2, v8(6), AX.X, ALU.max))
                first_of(v8(4), v8(6), b8(t2), (pos, [P, 8, 4]), scr)
                gs = small(21)[:, 0:8].rearrange("p (t g) -> p t g", t=NT)
                gm = small(21)[:, 8:16].rearrange("p (t g) -> p t g", t=NT)
                gx = small(21)[:, 16:18]
                pos2 = tie4[:].unsqueeze(1).to_broadcast([P, NT, 4])
                scr2 = (small(21)[:, 20:28].rearrange("p (t g) -> p t g", t=NT), small(21)[:, 28:30])
                link(tt_(small(21)[:, 0:8], t1, t2, ALU.add))
                link(dve.tensor_reduce(gx, gs, AX.X, ALU.max))
                first_of(gm, gs, gx.unsqueeze(2).to_broadcast([P, NT, 4]), (pos2, [P, NT, 4]), scr2)
                gmb = b8(small(21)[:, 8:16])
                link(tt_(v8(3), v8(3), gmb, ALU.mult))
                link(tt_(v8(4), v8(4), gmb, ALU.mult))
                tt_(small(8), small(3), small(4), ALU.add).then_inc(m["sel_ready"], 1)
                ga, gb_ = small(22)[:, 0:2], small(22)[:, 2:4]
                link(tt_(small(6), small(3), small(2), ALU.mult))
                link(dve.tensor_reduce(ga, v3(6), AX.X, ALU.add))
                link(tt_(small(6), small(4), small(2), ALU.mult))
                link(dve.tensor_reduce(gb_, v3(6), AX.X, ALU.add))
                gsum = small(22)[:, 4:6]
                link(tt_(gsum, ga, gb_, ALU.add))
                link(dve.reciprocal(gsum, gsum))
                link(tt_(tok4[:, :, 2], ga, gsum, ALU.mult))
                link(tt_(tok4[:, :, 3], gb_, gsum, ALU.mult))
                dve.wait_ge(m["rank_full"], 1)
                cnt = bank[1][:, 2 * NE:3 * NE]
                nblk, base = tab_f[:, 0:NE], tab_f[:, NE:2 * NE]
                link(ts_(nblk, cnt, float(C), 1.0, ALU.is_gt, ALU.add))
                for c in range(2, S // C):
                    link(ts_(small(7)[:, 0:NE], cnt, float(c * C), None, ALU.is_gt))
                    link(tt_(nblk, nblk, small(7)[:, 0:NE], ALU.add))
                link(dve.tensor_tensor_scan(base, ones[:, 0:NE], nblk, 0.0, ALU.mult, ALU.add))
                link(dve.tensor_copy(tab_f[:, 2 * NE:2 * NE + 1], tab_f[:, 2 * NE - 1:2 * NE]))
                link(tt_(base, base, nblk, ALU.subtract))
                dve.tensor_copy(tab_i[:, 0:2 * NE + 1], tab_f[0:1, 0:2 * NE + 1]).then_inc(m["tab_ready"], 1)
                link(stt(v3(6), base.unsqueeze(1).to_broadcast([P, NT, NE]), float(C),
                         bank[1][:, 0:2 * NE].rearrange("p (t e) -> p t e", t=NT), ALU.mult, ALU.add))
                for r in range(2):
                    link(tt_(small(7), small(3 + r), small(6), ALU.mult))
                    dve.tensor_reduce(tok4[:, :, r], v3(7), AX.X, ALU.add).then_inc(m["slots_ready"], 1)
                    dve.wait_ge(m["slots_ready"], r + 1)
                dve.memset(spread, 0.0).then_inc(m["s_ready"], 1)
                dve.memset(ymoe[:, 0:W], 0.0).then_inc(m["y0_ready"], 1)
                dve.memset(ymoe[:, W:D], 0.0).then_inc(m["y1_ready"], 1)
                dve.memset(hid, 0.0).then_inc(m["hid_ready"], 1)
                link(dve.tensor_copy(pcol[:], pcol0[:]))

                def pick_step(wait_for):
                    for tt in range(NT):
                        ts_(pick2[:, tt, :], iota64[:], tok4[:, tt, 1:2], None, ALU.is_equal)
                        ins = ts_(pick[:, tt, :], iota64[:], tok4[:, tt, 0:1], None, ALU.is_equal)
                    wait_for(ins)
                    return tt_(pick, pick, pick2, ALU.add)

                pick_step(link).then_inc(m["p_ready"], 1)
                dve.wait_ge(m["slot_full"], 1)
                link(ts_(tok4[:, :, 0:2], tok4[:, :, 0:2], -float(C), None, ALU.add))
                dve.wait_ge(m["rows_ready"], 1)
                dve.wait_ge(m["tab_ready"], 1)
                total = dve.value_load(tab_i[0:1, 2 * NE:2 * NE + 1], min_val=NE, max_val=2 * NE)
                steps = 4
                with dve.Fori(0, total) as g:
                    def after(ins, n):
                        ins.then_inc(m["chain"], 1)
                        dve.wait_ge(m["chain"], g * steps + (n + 1))

                    dve.wait_ge(m["gath_full"], g + 1)
                    pick_step(lambda ins: after(ins, 0)).then_inc(m["p_ready"], 1)
                    ts_(tok4[:, :, 0:2], tok4[:, :, 0:2], -float(C), None, ALU.add)
                    after(stt(spread2, rows4[:, 1, :], pcol[0:C, :], rows4[:, 3, :], ALU.is_equal, ALU.mult), 1)
                    dve.wait_ge(m["silu_done"], g + 1)
                    tt_(hid.rearrange("p f c -> p (f c)"), hsil.rearrange("p f c -> p (f c)"),
                        bank[5][:, FB * C:2 * FB * C], ALU.mult).then_inc(m["hid_ready"], 1)
                    dve.wait_ge(m["scat_done"], g + 2)
                    after(stt(spread, rows4[:, 0, :], pcol[0:C, :], rows4[:, 2, :], ALU.is_equal, ALU.mult), 2)
                    tt_(spread, spread, spread2, ALU.add).then_inc(m["s_ready"], 1)
                    after(ts_(pcol[:], pcol[:], float(C), None, ALU.add), 3)
                    dve.wait_ge(m["down_half"], g * 2 + 2)
                    dve.tensor_copy(ymoe[:, W:D], bank[7][0:C, :]).then_inc(m["y1_ready"], 1)
                dve.wait_ge(m["scat_done"], total + 2)
                residual(k)

            if NSUB >= 2:
                moe(0, 1)
            if NSUB >= 3:
                modulation(1)
                norm(2)
                def mix_used(n):
                    return (lora_full, n + 1) if n < 3 else (proj_full, FULL_LORA + 4 * (n - 3) + 4)

                dve.wait_ge(h_ready, 3)
                tt_(xx[:, :, 1:S], hT[:, :, 0:S - 1], hT[:, :, 1:S], ALU.subtract)
                link(ts_(xx[:, :, 0:1], hT[:, :, 0:1], -1.0, None, ALU.mult))
                for n, i in enumerate((3, 4, 5, 1, 0, 2)):
                    if n >= 2:
                        dve.wait_ge(*mix_used(n - 2))
                    for b in range(KB):
                        ins = stt(mixed[n % 2][:, b, :], xx[:, b, :], col("od_mu", i * KB + b), hT[:, b, :],
                                  ALU.mult, ALU.add)
                    ins.then_inc(mix_ready, 1)
                    if n == 3:
                        dve.wait_ge(proj_evac, 26 + 4)
                        dve.memset(cum[:, :, 0:1], 0.0)
                        for b in range(KB):
                            ins = dve.tensor_tensor_scan(cum[:, b, 1:], ones[:, 0:S], sgT[:, b, :], 0.0,
                                                         ALU.mult, ALU.add)
                        ins.then_inc(cum_ready, 1)
                dve.wait_ge(proj_evac, 26 + 12 + 4)
                for b in range(KB):
                    ins = ts_(kkT[:, b, :], k1T[:, b, :], col("od_k_k", b), None, ALU.mult)
                link(ins)
                dve.wait_ge(*mix_used(5))
                tt_(mixed[0][:, :, :], kkT[:, :, :], kkT[:, :, :], ALU.mult).then_inc(kk_sq, 1)
                dve.wait_ge(head_sum, 3)
                for b in range(KB):
                    ins = ts_(mixed[0][:, b, :], aT[:, b, :], -1.0, col("od_k_a", b), ALU.add, ALU.mult)
                link(ins)
                for b in range(KB):
                    ins = stt(k1T[:, b, :], mixed[0][:, b, :], 1.0, k1T[:, b, :], ALU.add, ALU.mult)
                link(ins)
                dve.wait_ge(proj_evac, 26 + 12 + 8)
                for b in range(KB):
                    ins = stt(mixed[1][:, b, :], rT[:, b, :], col("od_r_k", b), k1T[:, b, :], ALU.mult, ALU.mult)
                ins.then_inc(rk_ready, 1)
                dve.wait_ge(head_root, 3)
                link(ts_(rs_root[:], rs_root[:], 1e-12, None, ALU.max))
                dve.reciprocal(rstd[:], rs_root[:]).then_inc(head_rstd, 1)
                for u in range(4):
                    dve.wait_ge(head_bcast, u + 5)
                    v = kkT[:, 2 * u:2 * u + 2, :].rearrange("p k s -> p (k s)")
                    tt_(v, v, bank[6 + u % 2][:], ALU.mult).then_inc(bcast_used, 1)
                dve.wait_ge(head_sum, 4)
                dve.tensor_copy(beta[:], bank[5][:, 0:2 * NH])
                dve.wait_ge(cum_ready, 1)
                for tt in range(NT):
                    mid = cum[:, :, tt * P + MID:tt * P + MID + 1].to_broadcast([P, KB, P])
                    ins = tt_(by_tile(4)[:, :, tt, :], cum[:, :, 1 + tt * P:1 + (tt + 1) * P], mid, ALU.subtract)
                ins.then_inc(rw_diff, 1)
                for tt in range(NT):
                    mid = cum[:, :, tt * P + MID:tt * P + MID + 1].to_broadcast([P, KB, P])
                    ins = tt_(by_tile(10)[:, :, tt, :], cum[:, :, tt * P:(tt + 1) * P], mid, ALU.subtract)
                ins.then_inc(rw_diff, 1)
                tt_(kmid[:], cum[:, :, MID], cum[:, :, P + MID], ALU.subtract).then_inc(kmid_diff, 1)
                dve.wait_ge(bcast_used, 8)
                link(tt_(buf(8), buf(8), buf(11), ALU.mult))
                dve.wait_ge(rw_exp, 1)
                tt_(AR[:, :, :, 1, :], by_tile(5), by_tile(3), ALU.mult).then_inc(rw_ops, 1)
                dve.wait_ge(rw_exp, 2)
                tt_(AR[:, :, :, 0, :], by_tile(11), by_tile(10), ALU.mult).then_inc(rw_ops, 1)
                dve.wait_ge(rw_exp, 3)
                tt_(buf(8), buf(8), buf(4), ALU.mult).then_inc(rw_ops, 1)
                tt_(buf(6), buf(6), buf(4), ALU.mult).then_inc(rw_ops, 1)
                dve.wait_ge(rw_ops, 4)
                dve.wait_ge(kmid_ready, 1)

                def u4(x):
                    return x.rearrange("p (u s) -> p u s", s=P)

                def take_scores(pr):
                    n = 6 * pr
                    for which, keys in ((0, rwK), (1, rwB)):
                        ins = ts_(kcross(pr, which), keys[:, pr, 0, :], kmid[:, pr:pr + 1], None, ALU.mult)
                    ins.then_inc(kc_ready, 1)
                    for kind in range(2):
                        for hh in range(2):
                            dve.wait_ge(rsc_full, n + 2 * kind + hh + 1)
                            ps = bank[hh][:].rearrange("p (t a s) -> p t a s", t=2, a=2)
                            to_a, to_r = (part(pr, (2 * kind + a) * 4, 4).rearrange(
                                "p (t h s) -> p t h s", t=2, h=2)[:, :, hh, :] for a in range(2))
                            two = lambda mask: mask[:].unsqueeze(1).to_broadcast([P, 2, P])
                            ins = stt(to_a, ps[:, :, 0, :], -1.0 if kind else 1.0, two(strict), ALU.mult, ALU.mult)
                            if kind and hh:
                                ins.then_inc(lt_ready, 1)
                            tt_(to_r, ps[:, :, 1, :], two(causal), ALU.mult).then_inc(rsc_evac, 1)
                    dve.wait_ge(lt_ready, pr + 1)
                    link(tt_(u4(xinvT(pr)), u4(part(pr, 8, 4)), level[:, 0:1, :].to_broadcast([P, 4, P]), ALU.mult))
                    tt_(u4(xinvT(pr)), u4(xinvT(pr)), ident[:].unsqueeze(1).to_broadcast([P, 4, P]),
                        ALU.add).then_inc(xt1_ready, 1)
                    for hh in range(2):
                        dve.wait_ge(rsc_full, n + 4 + hh + 1)
                        dve.tensor_copy(part(pr, 16, 8).rearrange("p (q h s) -> p q h s", q=4, h=2)[:, :, hh, :],
                                        u4(bank[hh][:])).then_inc(rsc_evac, 1)

                for jj in range(KB // 2):
                    prs = (2 * jj, 2 * jj + 1)
                    for pr in prs:
                        take_scores(pr)
                    for pr in prs:
                        dve.wait_ge(x1_full, pr + 1)
                        dve.tensor_copy(xinv(pr), bank[4 + 2 * (pr % 2)][:]).then_inc(x1_ready, 1)
                    for i in range(1, 7):
                        for pr in prs:
                            n = jj * 12 + 2 * (i - 1) + pr % 2
                            dve.wait_ge(xm_full, n + 1)
                            if i == 1:
                                dve.wait_ge(x1_ready, pr + 1)
                                dve.wait_ge(xt1_ready, pr + 1)
                            else:
                                dve.wait_ge(xm_ready, n - 1)
                            if i < 6:
                                tt_(xinv(pr), xinv(pr), bank[4 + 2 * (pr % 2)][:], ALU.add)
                            tt_(xinvT(pr), xinvT(pr), bank[5 + 2 * (pr % 2)][:], ALU.add).then_inc(xm_ready, 1)
                    for pr in prs:
                        dve.wait_ge(ry_full, pr + 1)
                        dve.tensor_copy(oR[:, pr, :, :], bank[4 + 2 * (pr % 2)][:, 0:S].rearrange(
                            "p (t s) -> p t s", t=NT)).then_inc(ry_ready, 1)

                dve.wait_ge(ry_ready, KB)
                tt_(bvN, vN1, beta[:].rearrange("p (t h) -> p t h", t=NT).unsqueeze(3).to_broadcast(
                    [P, NT, NH, HEAD]), ALU.mult).then_inc(bv_ready, 1)
                dve.wait_ge(head_sum, 5)
                ts_(gm_mean[:], bank[4][:, 0:2 * NH], 1.0 / HEAD, None, ALU.mult).then_inc(gn_mean, 1)
                four = lambda x: x.rearrange("p (k t s) -> p k t s", k=2, t=NT)
                for u in range(4):
                    dve.wait_ge(head_bcast, u + 9)
                    v = oR[:, 2 * u:2 * u + 2, :, :]
                    tt_(v, v, four(bank[6 + u % 2][:]), ALU.subtract).then_inc(bcast_used, 1)
                dve.wait_ge(head_root, 4)
                dve.reciprocal(rstd[:], rs_root[:]).then_inc(head_rstd, 1)
                for u in range(4):
                    dve.wait_ge(head_bcast, u + 13)
                    v = oR[:, 2 * u:2 * u + 2, :, :]
                    tt_(v, v, four(bank[6 + u % 2][:]), ALU.mult).then_inc(bcast_used, 1)
                dve.wait_ge(bcast_used, 16)
                og = by_tile(4)
                for b in range(KB):
                    ins = ts_(og[:, b, :, :], oR[:, b, :, :], col("od_ln_w", b), col("od_ln_b", b), ALU.mult, ALU.add)
                link(ins)
                dve.wait_ge(bvT_full, 1)
                for b in range(0, KB, 2):
                    v = blocks(4)[:, b:b + 2, :].rearrange("p k s -> p (k s)")
                    ins = tt_(v, v, bank[b // 2][:], ALU.add)
                link(ins)
                tt_(buf(4), buf(4), buf(9), ALU.mult).then_inc(og_ready, 1)
                dve.wait_ge(tile_used, USED[1])
                residual(2)
            if NSUB >= 4:
                moe(1, 3)
            norm(NSUB)


INPUTS = ["x", "c", "mod_w", "mod_b", "norm_w", "hg_lb_logits", "ev_w_in", "ev_hg_norm", "ev_conv_w", "ev_conv_b",
          "ev_dt_bias", "ev_a_log", "ev_d_skip", "ev_ssm_norm", "ev_w_out", "od_mu", "od_w_rkv", "od_w_dec0",
          "od_w_dec1", "od_w_dec2", "od_a0", "od_a1", "od_a2", "od_g1", "od_g2", "od_k_k", "od_k_a", "od_r_k",
          "od_ln_w", "od_ln_b", "od_w_o", "router_w", "router_b", "moe_w1", "moe_w3", "moe_w2", "final_norm_w"]


def kernel(**inputs):
    import numpy as np
    import concourse.bacc as bacc
    from concourse.bass_utils import run_bass_kernel_spmd as run

    nc = bacc.Bacc("TRN2", target_bir_lowering=False, num_devices=1, dynamic_dma_scratch_size=1024)
    arrays, args = {}, {}
    for name in INPUTS:
        a = np.ascontiguousarray(inputs[name])
        arrays[f"in_{name}"] = a
        args[name] = nc.dram_tensor(f"in_{name}", a.shape, mybir.dt.from_np(a.dtype), kind="ExternalInput").ap()
    out = nc.dram_tensor("out_0", (1, S, D), F32, kind="ExternalOutput").ap()
    trunk(nc, args, out)
    r = run(nc, [arrays], core_ids=[0])
    return r.results[0]["out_0"]
```

```python
from contextlib import ExitStack

import concourse.bass as bass
from concourse import mybir

F32 = mybir.dt.float32
I32 = mybir.dt.int32
ALU = mybir.AluOpType
ACT = mybir.ActivationFunctionType
AX = mybir.AxisListType

P = 128
D = 1024
S = 256
KB = D // P
NT = S // P
LAYERS = 2
EPS = 1e-6
GN_EPS = 64e-5
HEAD = 64
NH = D // HEAD
GROUPS = 2
TAPS = 4
XBC = D + 2 * GROUPS * P
XBLK = XBC // P
IN_COLS = 4 * D + D + XBC + NH
NE = 16
FF = D // 2
FB = FF // P
MID = P // 2
C = 64
SLOTS = 6
TILE = 4096
W = 512
E05 = 0.6065306597126334
HALVES = [1, 2, 4, 8, 16, 32, 64]
MOD_FIRST = 4
NSUB = 4


def layout_vectors():
    groups = [
        [("mod_b", 96), ("norm_w", 32)],
        [("c", 8), ("final_norm_w", 8), ("hg_lb_logits", 24), ("ev_hg_norm", 8), ("ev_conv_w", 48),
         ("ev_conv_b", 12), ("ev_ssm_norm", 8)],
        [("od_mu", 48), ("od_w_dec0", 8), ("od_a0", 8), ("od_k_k", 8), ("od_k_a", 8), ("od_r_k", 8),
         ("od_ln_w", 8), ("od_ln_b", 8)],
    ]
    at = {}
    for g, rows in enumerate(groups):
        r = 0
        for name, n in rows:
            at[name] = (g, r, n)
            r += n
    return at


VEC = layout_vectors()


def weight_tiles():
    first = [("mod", 0, j) for j in range(MOD_FIRST)]
    first += [("in", 0, j) for j in (2, 3, 0, 1, 4, 5, 12, 10, 11, 8, 9, 6, 7)]
    first += [("mod", 0, j) for j in range(MOD_FIRST, 12)] + [("mod", 1, j) for j in range(12)]
    first += [("out", 0, j) for j in range(4)]
    second = [("la", 0, 0), ("lb", 0, 0)]
    second += [("rkv", i, j) for i in (1, 0, 2) for j in range(2)]
    second += [("wo", 0, j) for j in range(2)]
    return [first, second]


def trunk(nc, t, out):
    tiles = weight_tiles()

    landed = [0] * SLOTS
    plan = []
    moe_base = []
    n_dma = {"la": 3, "lb": 3}
    for stage in tiles:
        rows = []
        for n, tile in enumerate(stage):
            slot = n % SLOTS
            landed[slot] += n_dma.get(tile[0], 1)
            rows.append((tile, slot, landed[slot]))
        plan.append(rows)
        moe_base.append(list(landed))
        landed = [x + NE // 2 for x in landed]

    start = {(s, kind): min(n for n, row in enumerate(rows) if row[0][0] == kind)
             for s, rows in enumerate(plan) for kind in {row[0][0] for row in rows}}

    FULL_IN = 2 * 13
    FULL_LORA = FULL_IN + 12
    USED = [4, 6]

    with ExitStack() as ctx:
        def sb(name, shape, dt=F32):
            return ctx.enter_context(nc.sbuf_tensor(name, shape, dt))

        def sem(name):
            return ctx.enter_context(nc.semaphore(name))

        ctx.enter_context(nc.allow_non_contiguous_dma(reason="a few small vectors"))

        bank = [ctx.enter_context(nc.psum_tensor(f"bank{i}", [P, W], F32)) for i in range(8)]

        ring = sb("ring", [P, SLOTS * TILE])
        BUF = KB * S
        XPAD = XBLK * (S + TAPS - 1)
        arena = sb("arena", [P, 12 * BUF + XPAD])

        def buf(i, n=1):
            return arena[:, i * BUF:(i + n) * BUF]

        def blocks(i):
            return buf(i).rearrange("p (k s) -> p k s", k=KB)

        def by_tile(i):
            return buf(i).rearrange("p (k t s) -> p k t s", k=KB, t=NT)

        xpad = arena[:, 12 * BUF:12 * BUF + XPAD].rearrange("p (k s) -> p k s", k=XBLK)

        xT = blocks(0)
        hT = blocks(1)
        xN = buf(8).rearrange("p (t d) -> p t d", t=NT)
        squares = blocks(11)

        ident = sb("ident", [P, P])
        ones = sb("ones", [P, S])
        thirty2 = sb("thirty2", [P, 1])
        halves = sb("halves", [P, 2])
        causal = sb("causal", [P, P])
        strict = sb("strict", [P, P])
        tri = buf(7)[:, 0:6 * P].rearrange("p (i s) -> p i s", i=6)
        level = sb("level", [P, 7, P])
        iota = sb("iota", [P, P])
        pcol0 = sb("pcol0", [P, 1])
        tie4 = sb("tie4", [P, 4])

        vrows = buf(9)[:, 0:3 * P].rearrange("p (g r) -> p g r", g=3)
        vcols = sb("vcols", [P, 3, P])

        def col(name, i):
            g, r, n = VEC[name]
            assert i < n
            return vcols[:, g, r + i:r + i + 1]

        def cols(name, a, b):
            g, r, n = VEC[name]
            return vcols[:, g, r + a:r + b]

        modT = sb("modT", [P, LAYERS, 48])
        gain = sb("gain", [P, LAYERS, 2, KB])
        csilu = sb("csilu", [P, KB])
        rs_root = sb("rs_root", [P, 2 * NH])
        rstd = sb("rstd", [P, 2 * NH])
        gm_mean = sb("gm_mean", [P, 2 * NH])
        beta = sb("beta", [P, 2 * NH])
        lb = sb("lb", [P, KB])
        oml = sb("oml", [P, KB])
        lbe = sb("lbe", [P, 3, KB])
        lbm = sb("lbm", [P, KB])
        dt_bias = sb("dt_bias", [NH, 1])
        a_log = sb("a_log", [NH, 1])
        a_neg = sb("a_neg", [NH, 1])
        dskip = sb("dskip", [P, KB])
        w_dt = sb("w_dt", [P, KB, NH])
        router_w = sb("router_w", [P, KB, NE])
        router_b = sb("router_b", [P, NE])
        eps_col = sb("eps_col", [P, 2])

        tile_landed = [sem(f"tile_landed{i}") for i in range(SLOTS)]
        tile_used = sem("tile_used")
        vec_landed = sem("vec_landed")
        x_landed = sem("x_landed")
        small_landed = sem("small_landed")
        vrows_zeroed = sem("vrows_zeroed")
        consts = sem("consts")
        stored = sem("stored")
        pool_chain = sem("pool_chain")
        dve_chain = sem("dve_chain")
        act_chain = sem("act_chain")

        weight = lambda slot: ring[:, slot * TILE:(slot + 1) * TILE]
        w_cols = lambda slot: weight(slot).rearrange("p (k n) -> p k n", k=KB)
        w_rows = lambda slot: weight(slot).rearrange("p (k n) -> p k n", k=4)
        row_block = lambda ap: ap.rearrange("(k p) n -> p k n", p=P)

        vec_T = sem("vec_T")
        vec_cols = sem("vec_cols")
        xT_psum = sem("xT_psum")
        xT_evac = sem("xT_evac")
        csilu_ready = sem("csilu_ready")
        mod_full = sem("mod_full")
        mod_row = sem("mod_row")
        mod_cols = sem("mod_cols")
        mod_taken = sem("mod_taken")
        x_ready = sem("x_ready")
        sq_ready = sem("sq_ready")
        sums_psum = sem("sums_psum")
        root_ready = sem("root_ready")
        rstd_ready = sem("rstd_ready")
        bcast_psum = sem("bcast_psum")
        h_ready = sem("h_ready")
        proj_full = sem("proj_full")
        proj_evac = sem("proj_evac")
        lb_max = sem("lb_max")
        start_exp = sem("start_exp")
        logf_ready = sem("logf_ready")
        k_ready = sem("k_ready")
        b_ready = sem("b_ready")
        dl_ready = sem("dl_ready")
        dr_ready = sem("dr_ready")
        el_exp = sem("el_exp")
        ek_ready = sem("ek_ready")
        eq_ready = sem("eq_ready")
        score_full = sem("score_full")
        score_evac = sem("score_evac")
        o_full = sem("o_full")
        o_evac = sem("o_evac")
        head_sum = sem("head_sum")
        head_root = sem("head_root")
        head_rstd = sem("head_rstd")
        head_bcast = sem("head_bcast")
        bcast_used = sem("bcast_used")
        oa_ready = sem("oa_ready")
        silu_g = sem("silu_g")
        dt_full = sem("dt_full")
        dtz = sem("dtz")
        dtabs = sem("dtabs")
        dtln = sem("dtln")
        dt_ready = sem("dt_ready")
        dtN_full = sem("dtN_full")
        dtN_ready = sem("dtN_ready")
        conv_zero = sem("conv_zero")
        conv_done = sem("conv_done")
        conv_silu = sem("conv_silu")
        xs_full = sem("xs_full")
        xdt_ready = sem("xdt_ready")
        cb_full = sem("cb_full")
        cb_ready = sem("cb_ready")
        row_full = sem("row_full")
        dec_diff = sem("dec_diff")
        dec_exp = sem("dec_exp")
        dec_mat = sem("dec_mat")
        y_full = sem("y_full")
        y_ready = sem("y_ready")
        ysq_ready = sem("ysq_ready")
        yb_full = sem("yb_full")
        ob_ready = sem("ob_ready")
        mix_ready = sem("mix_ready")
        lora_full = sem("lora_full")
        lora_evac = sem("lora_evac")
        cum_ready = sem("cum_ready")
        kk_sq = sem("kk_sq")
        rk_ready = sem("rk_ready")
        rw_diff = sem("rw_diff")
        rw_exp = sem("rw_exp")
        rw_ops = sem("rw_ops")
        kc_ready = sem("kc_ready")
        rsc_full = sem("rsc_full")
        rsc_evac = sem("rsc_evac")
        lt_ready = sem("lt_ready")
        xt1_ready = sem("xt1_ready")
        x1_full = sem("x1_full")
        x1_ready = sem("x1_ready")
        lm_ready = sem("lm_ready")
        tm_full = sem("tm_full")
        tm_ready = sem("tm_ready")
        xm_full = sem("xm_full")
        xm_ready = sem("xm_ready")
        w_full = sem("w_full")
        w_ready = sem("w_ready")
        u_full = sem("u_full")
        u_ready = sem("u_ready")
        ry_full = sem("ry_full")
        ry_ready = sem("ry_ready")
        gn_mean = sem("gn_mean")
        gn_sq = sem("gn_sq")
        bv_ready = sem("bv_ready")
        bvT_full = sem("bvT_full")
        kmid_diff = sem("kmid_diff")
        kmid_ready = sem("kmid_ready")
        og_ready = sem("og_ready")
        shared = {n: sem(f"moe_{n}") for n in ("logit_full", "lmax", "lexp", "sel_ready", "rank_full", "tab_ready",
                                               "slots_ready", "slot_full", "rows_ready", "hN_full", "hN_evac")}
        moe_names = ["pick_ready", "gath_full", "hga_ready", "hgb_ready", "w1_done", "w3_done", "silu_done", "hid_ready",
                     "hidT_full", "hidT_ready", "down_half", "y0_ready", "y1_ready", "spread_ready", "scat_done",
                     "chain"]
        M = [dict(shared, **{n: sem(f"m{l}_{n}") for n in moe_names}) for l in range(LAYERS)]

        mod_rows = buf(1)[:, 0:2 * W].rearrange("p (u n) -> p u n", u=2)

        qT, kT, bT, zT, gT = blocks(2), blocks(4), blocks(5), blocks(11), blocks(10)
        fT = blocks(3)
        eT = [3, 7]
        vN = buf(6).rearrange("p (t d) -> p t d", t=NT)
        scd = buf(8).rearrange("p (t h s) -> p t h s", t=NT, h=KB)
        scx = buf(9)[:, 0:KB * P].rearrange("p (h s) -> p h s", h=KB)
        oa = blocks(2)
        cbm = buf(9)[:, KB * P:KB * P + 6 * P].rearrange("p (g n) -> p g n", g=GROUPS)
        xdt = buf(4).rearrange("p (t d) -> p t d", t=NT)
        NDEC = 5
        dec = buf(7)[:, 0:NDEC * 3 * P].rearrange("p (r n) -> p r n", r=NDEC)
        yT = blocks(5)
        kmid = sb("kmid", [P, KB])
        scratch = sb("scratch", [P, 7 * S])
        ctmp = scratch[:, 0:2 * S].rearrange("p (u s) -> p u s", u=2)
        dts = scratch[0:NH, 2 * S:7 * S].rearrange("p (u s) -> p u s", u=5)
        dtN = sb("dtN", [P, 2, NT, NH])

        xx = blocks(2)
        mixed = [blocks(3), blocks(4)]
        rT, kkT, aT, ggT = blocks(5), blocks(11), blocks(8), blocks(9)
        k1T = blocks(6)
        vN1 = buf(7).rearrange("p (t h n) -> p t h n", t=NT, h=NH)
        sgT = blocks(10)
        cum = arena[:, 12 * BUF:12 * BUF + KB * (S + 1)].rearrange("p (k s) -> p k s", k=KB)
        AR = buf(1, 2).rearrange("p (k t a s) -> p k t a s", k=KB, t=NT, a=2)
        rwB, rwK = by_tile(8), by_tile(6)
        oR = AR[:, :, :, 0, :]
        lora = [scratch[:, i * S:(i + 1) * S] for i in range(3)]
        bvN = buf(5).rearrange("p (t h n) -> p t h n", t=NT, h=NH)
        pslot = [arena[:, 3 * BUF:6 * BUF], arena[:, 10 * BUF:13 * BUF]]

        def part(pr, off, n):
            return pslot[pr % 2][:, off * P:(off + n) * P]

        def sc(pr, kind, tt, hh):
            return part(pr, kind * 4 + tt * 2 + hh, 1)

        def scro(pr, kind, hh):
            return part(pr, 16 + kind * 2 + hh, 1)

        def kcross(pr, which):
            return part(pr, 24 + which, 1)

        def xinv(pr):
            return part(pr, 26, 4)

        def xinvT(pr):
            return part(pr, 30, 4)

        def tmid(pr):
            return part(pr, 34, 4)

        def lmask(pr, i):
            return part(pr, 38 + 4 * (i % 2), 4)

        def uneg(pr, tt):
            return part(pr, 46 + tt, 1)

        assert 48 * P <= 3 * BUF and 10 * BUF + 48 * P <= 12 * BUF + XPAD

        hN = buf(2).rearrange("p (t d) -> p t d", t=NT)
        m3 = buf(3)
        pick = m3[:, 0:2 * P].rearrange("p (t c) -> p t c", t=NT)
        pick2 = m3[:, 2 * P:4 * P].rearrange("p (t c) -> p t c", t=NT)
        spread = m3[:, 4 * P:6 * P]
        spread2 = m3[:, 6 * P:8 * P]
        hid = m3[:, 8 * P:12 * P]
        hsil = m3[:, 12 * P:16 * P]
        ymoe = buf(4)[:, 0:D]
        rows4 = buf(4)[:, D:D + 4 * S].rearrange("p (r s) -> p r s", r=4)
        hgT = buf(6)[:, 0:KB * P].rearrange("p (k c) -> p k c", k=KB)
        hidT = buf(6)[:, KB * P:KB * P + FB * P].rearrange("p (f c) -> p f c", f=FB)
        rt = buf(5)

        def small(i, n=1):
            return rt[:, i * 32:(i + n) * 32]

        tok4 = sb("tok4", [P, NT, 4])
        pcol = sb("pcol", [P, 1])
        tab_f = sb("tab_f", [P, 64])
        tab_i = sb("tab_i", [1, 64], I32)

        block = ctx.enter_context(nc.Block())

        @block.sync
        def _(sp):
            def load(tile, slot):
                kind, l, j = tile
                if kind == "mod":
                    srcs = [(w_cols(slot), row_block(t["mod_w"][l])[:, :, j * W:(j + 1) * W])]
                elif kind == "in":
                    srcs = [(w_cols(slot), row_block(t["ev_w_in"][0])[:, :, j * W:(j + 1) * W])]
                elif kind == "out":
                    srcs = [(w_rows(slot), row_block(t["ev_w_out"][0])[:, 4 * j:4 * j + 4, :])]
                elif kind == "rkv":
                    srcs = [(w_cols(slot), row_block(t["od_w_rkv"][0, l])[:, :, j * W:(j + 1) * W])]
                elif kind == "wo":
                    srcs = [(w_rows(slot), row_block(t["od_w_o"][0])[:, 4 * j:4 * j + 4, :])]
                elif kind == "la":
                    wt = weight(slot)
                    srcs = [(wt[:, 0:512].rearrange("p (k n) -> p k n", k=KB), row_block(t["od_w_dec1"][0])),
                            (wt[:, 512:1024].rearrange("p (k n) -> p k n", k=KB), row_block(t["od_a1"][0])),
                            (wt[:, 1024:2048].rearrange("p (k n) -> p k n", k=KB), row_block(t["od_g1"][0]))]
                elif kind == "lb":
                    wt = weight(slot)
                    srcs = [(wt[0:64, 0:D], t["od_w_dec2"][0]), (wt[0:64, D:2 * D], t["od_a2"][0]),
                            (wt[:, 2 * D:3 * D], t["od_g2"][0])]
                for dst, src in srcs:
                    sp.dma_start(dst, src).then_inc(tile_landed[slot], 16)

            def wait_used(l, n):
                kind, l_mod, j = plan[l][n][0]
                at = n - start[l, kind]
                if kind == "mod":
                    sp.wait_ge(mod_full, 12 * l_mod + j + 1)
                elif kind == "in":
                    sp.wait_ge(proj_full, 2 * at + 2)
                elif kind in ("out", "wo"):
                    sp.wait_ge(tile_used, (USED[0] if l else 0) + at + 1)
                elif kind == "la":
                    sp.wait_ge(lora_full, 3)
                elif kind == "lb":
                    sp.wait_ge(proj_full, FULL_LORA)
                elif kind == "rkv":
                    sp.wait_ge(proj_full, FULL_LORA + 2 * at + 2)

            for l in range((NSUB + 1) // 2):
                base = M[l]
                for n, (tile, slot, _) in enumerate(plan[l]):
                    if n >= SLOTS:
                        wait_used(l, n - SLOTS)
                    elif l > 0 and n == 0:
                        g_end = sp.value_load(tab_i[0:1, NE:NE + 1], min_val=NE // 2, max_val=NE)
                        sp.wait_ge(M[l - 1]["w1_done"], g_end)
                    elif l > 0 and n == 2:
                        sp.wait_ge(M[l - 1]["w3_done"], g_end)
                    elif l > 0 and n == 4:
                        sp.wait_ge(M[l - 1]["down_half"], g_end * 2)
                    load(tile, slot)
                n_stage = len(plan[l])
                if NSUB < 2 * l + 2:
                    break
                for slot in range(SLOTS):
                    kind, e = slot // 2, slot % 2
                    last = max(n for n in range(n_stage) if n % SLOTS == slot)
                    wait_used(l, last)
                    src = row_block([t["moe_w1"], t["moe_w3"], t["moe_w2"]][kind][l, e])
                    sp.dma_start((w_rows if kind == 2 else w_cols)(slot), src).then_inc(tile_landed[slot], 16)
                sp.wait_ge(base["tab_ready"], l + 1)
                views = [t[name][l].rearrange("e (k p) n -> p e k n", p=P) for name in ("moe_w1", "moe_w3", "moe_w2")]
                with sp.Fori(1, NE // 2) as i:
                    done = sp.value_load(tab_i[0:1, bass.ds(i + NE // 2, 1)], min_val=1, max_val=NE)
                    for slot in range(SLOTS):
                        kind, e = slot // 2, slot % 2
                        if kind == 0 and e == 0:
                            sp.wait_ge(base["w1_done"], done)
                        elif kind == 1 and e == 0:
                            sp.wait_ge(base["w3_done"], done)
                        elif kind == 2 and e == 0:
                            sp.wait_ge(base["down_half"], done * 2)
                        sp.dma_start((w_rows if kind == 2 else w_cols)(slot), views[kind][:, bass.ds(2 * i + e, 1)]
                                     .rearrange("p e k n -> p (e k) n")).then_inc(tile_landed[slot], 16)
            for tt in range(NT):
                sp.wait_ge(o_evac, 4 + 4 * (tt + 1))
                sp.dma_start(out[0, tt * P:(tt + 1) * P, :], hN[:, tt, :]).then_inc(stored, 16)
            sp.wait_ge(stored, 16 * NT)

        @block.gpsimd
        def _(pool):
            count = [0]

            def link(ins):
                count[0] += 1
                ins.then_inc(pool_chain, 1)
                pool.wait_ge(pool_chain, count[0])

            link(pool.memset(ident[:], 0.0))
            link(pool.affine_select(out=ident[:], in_=ident[:], compare_op=ALU.not_equal, fill=1.0, base=0,
                                    pattern=[[-1, P]], channel_multiplier=1))
            pool.memset(ones[:], 1.0)
            pool.memset(thirty2[:], 1.0 / 32)
            link(pool.memset(halves[:], 0.0))
            for hh in range(2):
                link(pool.memset(halves[hh * HEAD:(hh + 1) * HEAD, hh:hh + 1], 1.0))
            pool.iota(iota[:], pattern=[[1, P]], base=0, channel_multiplier=0, allow_small_or_imprecise_dtypes=True)
            pool.iota(tie4[:], pattern=[[1, 4]], base=0, channel_multiplier=0, allow_small_or_imprecise_dtypes=True)
            pool.iota(pcol0[:], pattern=[[0, 1]], base=0, channel_multiplier=1, allow_small_or_imprecise_dtypes=True)
            pool.memset(eps_col[:, 0:1], EPS)
            pool.memset(eps_col[:, 1:2], GN_EPS)
            for i in range(6):
                h = 2 << i
                v = tri[:, i, :].rearrange("p (b s) -> p b s", s=h)
                link(pool.memset(tri[:, i, :], 1.0))
                link(pool.affine_select(out=v, in_=v, compare_op=ALU.is_ge, fill=0.0, base=0,
                                        pattern=[[-h, P // h], [0, h]], channel_multiplier=1))
                link(pool.affine_select(out=v, in_=v, compare_op=ALU.is_ge, fill=0.0, base=h - 1,
                                        pattern=[[h, P // h], [0, h]], channel_multiplier=-1))
                link(pool.affine_select(out=tri[:, i, :], in_=tri[:, i, :], compare_op=ALU.is_ge, fill=0.0,
                                        base=0, pattern=[[1, P]], channel_multiplier=-1))
            link(pool.memset(causal[:], 1.0))
            link(pool.affine_select(out=causal[:], in_=causal[:], compare_op=ALU.is_ge, fill=0.0, base=0,
                                    pattern=[[1, P]], channel_multiplier=-1))
            link(pool.tensor_tensor(strict[:], causal[:], ident[:], ALU.subtract))
            inner = [ident[:]] + [tri[:, i, :] for i in range(6)]
            outer = [tri[:, i, :] for i in range(6)] + [causal[:]]
            for i in range(7):
                link(pool.tensor_tensor(level[:, i, :], outer[i], inner[i], ALU.subtract))
            pool.memset(xpad[:, :, 0:TAPS - 1], 0.0).then_inc(conv_zero, 1)
            pool.memset(eps_col[:, 0:1], EPS).then_inc(consts, 1)

            pool.wait_ge(b_ready, 1)
            for i, h in enumerate(HALVES + [P]):
                e = buf(eT[i % 2]).rearrange("p (b two h) -> p b two h", two=2, h=h)
                b = buf(5).rearrange("p (b two h) -> p b two h", two=2, h=h)
                kv = buf(4).rearrange("p (b two h) -> p b two h", two=2, h=h)
                nb = KB * S // (2 * h)
                if i >= 2:
                    pool.wait_ge(score_full, 4 + 2 * (i - 1))
                mid = b[:, :, 0, h - 1:h].to_broadcast([P, nb, h])
                pool.tensor_tensor(e[:, :, 0, :], mid, b[:, :, 0, :], ALU.subtract).then_inc(dl_ready, 1)
                pool.wait_ge(el_exp, i + 1)
                pool.wait_ge(k_ready, 1)
                pool.tensor_tensor(e[:, :, 0, :], e[:, :, 0, :], kv[:, :, 0, :], ALU.mult).then_inc(ek_ready, 1)
            if NSUB < 3:
                return

            for jj in range(KB // 2):
                for i in range(1, 7):
                    for pr in (2 * jj, 2 * jj + 1):
                        pool.wait_ge(lt_ready, pr + 1)
                        if i >= 3:
                            pool.wait_ge(tm_full, jj * 12 + 2 * (i - 3) + pr % 2 + 1)
                        elif jj > 0:
                            pool.wait_ge(tm_full, jj * 12)
                        src = part(pr, 8, 4).rearrange("p (u s) -> p u s", u=4)
                        dst = lmask(pr, i).rearrange("p (u s) -> p u s", u=4)
                        pool.tensor_tensor(dst, src, level[:, i:i + 1, :].to_broadcast([P, 4, P]),
                                           ALU.mult).then_inc(lm_ready, 1)

        @block.tensor
        def _(pe):
            pe.wait_ge(consts, 1)

            def column_sums(dst, src, tt, n):
                for k in range(n):
                    mm = pe.matmul(dst, src(k)[:, tt * P:(tt + 1) * P], ones[:, 0:1], start=(k == 0),
                                   stop=(k == n - 1))
                return mm

            def norm(k):
                pe.wait_ge(sq_ready, k + 1)
                for tt in range(NT):
                    mm = column_sums(bank[7][:, tt:tt + 1], lambda b: squares[:, b, :], tt, KB)
                mm.then_inc(sums_psum, 1)
                pe.wait_ge(rstd_ready, k + 1)
                for tt in range(NT):
                    mm = pe.matmul(bank[6][:, tt * P:(tt + 1) * P], rstd[:, tt:tt + 1].to_broadcast([P, P]),
                                   ident[:], start=True, stop=True)
                mm.then_inc(bcast_psum, 1)

            used = [0]
            full = [0]

            def take(stage, n):
                tile, slot, count = plan[stage][n]
                pe.wait_ge(tile_landed[slot], 16 * count)
                return tile, slot

            def proj_bank():
                n = full[0]
                if n >= 4:
                    pe.wait_ge(proj_evac, n - 3)
                full[0] += 1
                return bank[n % 4]

            def project_T(slot, src):
                for half in range(2):
                    ps = proj_bank()
                    for c in range(2):
                        for k in range(KB):
                            mm = pe.matmul(ps[:, c * S:(c + 1) * S],
                                           w_cols(slot)[:, k, (2 * half + c) * P:(2 * half + c + 1) * P],
                                           src[:, k, :], start=(k == 0), stop=(k == KB - 1))
                    mm.then_inc(proj_full, 1)
                return mm

            def project_N(slot, src):
                for tt in range(NT):
                    ps = proj_bank()
                    for k in range(KB):
                        mm = pe.matmul(ps[:, :], src[:, k, tt * P:(tt + 1) * P], w_cols(slot)[:, k, :],
                                       start=(k == 0), stop=(k == KB - 1))
                    mm.then_inc(proj_full, 1)
                return mm

            def mod_columns(m, cols_bank):
                pe.wait_ge(mod_row, m + 1)
                for c in range(4):
                    mm = pe.matmul(cols_bank[:, 4 * m + c:4 * m + c + 1], mod_rows[:, m % 2, c * P:(c + 1) * P],
                                   thirty2[:], start=True, stop=True)
                mm.then_inc(mod_cols, 1)

            def modulation(m, row_banks, cols_bank):
                n = m if m < MOD_FIRST else start[0, "in"] + 13 + m - MOD_FIRST
                _, slot = take(0, n)
                if m >= 2:
                    pe.wait_ge(mod_row, m - 1)
                for r in range(2):
                    for c in range(4):
                        k = 4 * r + c
                        mm = pe.matmul(row_banks[m % 2][32 * c:32 * (c + 1), :], csilu[:, k:k + 1].to_broadcast([P, 32]),
                                       w_cols(slot)[:, k, :], start=(r == 0), stop=(r == 1))
                mm.then_inc(mod_full, 1)
                if m != MOD_FIRST and m > 0:
                    mod_columns(m - 1, cols_bank)

            mod_next = [MOD_FIRST]

            def modulation_step():
                if mod_next[0] < 24:
                    modulation(mod_next[0], (bank[0], bank[1]), bank[2])
                    mod_next[0] += 1

            def out_projection(stage, first, n, srcs, ready):
                for j in range(n):
                    ready(j)
                    _, slot = take(stage, first + j)
                    for d in range(KB):
                        for kk in range(4):
                            mm = pe.matmul(bank[d // 2][:, (d % 2) * S:(d % 2 + 1) * S],
                                           w_rows(slot)[:, kk, d * P:(d + 1) * P], srcs(4 * j + kk),
                                           start=(j == 0 and kk == 0 and d % 2 == 0),
                                           stop=(j == n - 1 and kk == 3), skip_group_check=True)
                    mm.then_inc(tile_used, 1)

            pe.wait_ge(vec_landed, 16 * len(VEC))
            for g in range(3):
                mm = pe.transpose(bank[4][:, g * P:(g + 1) * P], vrows[:, g, :], ident[:])
            mm.then_inc(vec_T, 1)
            pe.wait_ge(x_landed, 16)
            for k in range(KB):
                for tt in range(NT):
                    mm = pe.transpose(bank[k // 2][:, (k % 2) * S + tt * P:(k % 2) * S + (tt + 1) * P],
                                      xN[:, tt, k * P:(k + 1) * P], ident[:])
                if k % 2:
                    mm.then_inc(xT_psum, 1)
            pe.wait_ge(csilu_ready, 1)
            for m in range(MOD_FIRST):
                modulation(m, (bank[6], bank[7]), bank[5])
            mod_columns(MOD_FIRST - 1, bank[5])
            norm(0)
            pe.wait_ge(h_ready, 1)
            pe.wait_ge(xT_evac, 1)

            scores = [0]

            def score_bank():
                m = scores[0]
                if m >= 2:
                    pe.wait_ge(score_evac, m - 1)
                scores[0] += 1
                return bank[4 + m % 2]

            def diagonal():
                pe.wait_ge(proj_evac, 8)
                pe.wait_ge(k_ready, 1)
                for r in range(2):
                    for tt in range(NT):
                        ps = score_bank()
                        for h in range(4):
                            ss = slice(tt * P, (tt + 1) * P)
                            mm = pe.matmul(ps[:, h * P:(h + 1) * P], kT[:, 4 * r + h, ss], qT[:, 4 * r + h, ss],
                                           start=True, stop=True)
                        mm.then_inc(score_full, 1)

            def level_scores(i):
                h = (HALVES + [P])[i]
                pe.wait_ge(ek_ready, i + 1)
                pe.wait_ge(eq_ready, i + 1)
                e = blocks(eT[i % 2])
                if h < P:
                    for tt in range(NT):
                        ps = score_bank()
                        for hh in range(KB):
                            et = e[:, hh, tt * P:(tt + 1) * P]
                            right = et.rearrange("p (b two h) -> p b two h", two=2, h=h)[:, :, 1, :]
                            mm = pe.matmul(ps[:, hh * 64:(hh + 1) * 64], et, right, start=True, stop=True)
                        mm.then_inc(score_full, 1)
                else:
                    for r in range(2):
                        ps = score_bank()
                        for hh in range(4):
                            mm = pe.matmul(ps[:, hh * P:(hh + 1) * P], e[:, 4 * r + hh, 0:P],
                                           e[:, 4 * r + hh, P:S], start=True, stop=True)
                        mm.then_inc(score_full, 1)

            extra = {4: [diagonal, lambda: level_scores(0)], 5: [lambda: level_scores(1)],
                     6: [lambda: level_scores(2)], 7: [lambda: level_scores(3)], 8: [lambda: level_scores(4)],
                     9: [lambda: level_scores(5)], 10: [lambda: level_scores(6)], 11: [lambda: level_scores(7)]}
            for n in range(13):
                (_, _, j), slot = take(0, start[0, "in"] + n)
                mm = (project_N if j in (4, 5) else project_T)(slot, hT)
                if n == 8:
                    pe.wait_ge(small_landed, 16 * 7)
                    for k in range(KB):
                        mm = pe.matmul(bank[6][0:NH, 0:S], w_dt[:, k, :], hT[:, k, :], start=(k == 0),
                                       stop=(k == KB - 1))
                    mm.then_inc(dt_full, 1)
                for f in extra.get(n, []):
                    f()

            pe.wait_ge(score_evac, 20)
            pe.wait_ge(proj_evac, 26)
            pe.wait_ge(mod_taken, 1)
            for u in range(4):
                if u >= 2:
                    pe.wait_ge(o_evac, u - 1)
                elif u == 0:
                    pe.wait_ge(dtz, 1)
                for c in range(2):
                    h = 2 * u + c
                    hs = slice(h * P, (h + 1) * P)
                    o = bank[6 + u % 2]
                    pe.matmul(o[:, c * S:c * S + P], vN[:, 0, hs], scd[:, 0, h, :], start=True, stop=True)
                    pe.matmul(o[:, c * S + P:(c + 1) * S], vN[:, 0, hs], scx[:, h, :], start=True, stop=False)
                    mm = pe.matmul(o[:, c * S + P:(c + 1) * S], vN[:, 1, hs], scd[:, 1, h, :], start=False, stop=True)
                mm.then_inc(o_full, 1)
                modulation_step()

            pe.wait_ge(dt_ready, 1)
            for a in range(2):
                for tt in range(NT):
                    mm = pe.transpose(bank[4][:, (2 * a + tt) * NH:(2 * a + tt + 1) * NH],
                                      dts[:, 3 + a, tt * P:(tt + 1) * P], ident[0:NH, 0:NH])
            mm.then_inc(dtN_full, 1)
            pe.wait_ge(conv_silu, 1)
            pe.wait_ge(o_evac, 4)
            for u in range(4):
                tt, half = u // 2, u % 2
                if u == 3:
                    pe.wait_ge(xdt_ready, 1)
                ps = bank[[5, 6, 7, 5][u]]
                for c in range(4):
                    mm = pe.transpose(ps[:, c * P:(c + 1) * P],
                                      xpad[:, 4 * half + c, TAPS - 1 + tt * P:TAPS - 1 + (tt + 1) * P], ident[:])
                mm.then_inc(xs_full, 1)
            pe.wait_ge(xdt_ready, 3)
            for g in range(GROUPS):
                ps = bank[6 + g]
                B = xpad[:, KB + g, TAPS - 1:]
                Cq = xpad[:, KB + GROUPS + g, TAPS - 1:]
                pe.matmul(ps[:, 0:S], B[:, 0:P], Cq[:, 0:S], start=True, stop=True)
                mm = pe.matmul(ps[:, S:S + P], B[:, P:S], Cq[:, P:S], start=True, stop=True)
                mm.then_inc(cb_full, 1)
            pe.wait_ge(dtN_ready, 1)
            pe.wait_ge(xdt_ready, 4)
            for h in range(KB):
                for tt in range(NT):
                    mm = pe.matmul(bank[4][:, tt * KB + h:tt * KB + h + 1], fT[:, h, tt * P:(tt + 1) * P],
                                   ones[:, 0:1], start=True, stop=True)
            mm.then_inc(head_sum, 1)
            pe.wait_ge(head_rstd, 1)
            for u in range(4):
                if u >= 2:
                    pe.wait_ge(bcast_used, u - 1)
                for c in range(2):
                    for tt in range(NT):
                        r = tt * KB + 2 * u + c
                        mm = pe.matmul(bank[4 + u % 2][:, c * S + tt * P:c * S + (tt + 1) * P],
                                       rstd[:, r:r + 1].to_broadcast([P, P]), ident[:], start=True, stop=True)
                mm.then_inc(head_bcast, 1)
            pe.wait_ge(cb_ready, 2)
            pe.wait_ge(bcast_used, 4)

            def decay_row(h):
                if h >= 2:
                    pe.wait_ge(dec_diff, h - 1)
                pe.matmul(bank[4 + h % 2][:, 0:S], ident[0:NH, h:h + 1].to_broadcast([NH, P]), dts[:, 4, :],
                          start=True, stop=True).then_inc(row_full, 1)

            def head_out(h):
                pe.wait_ge(dec_mat, h + 1)
                pr, c = h // 2, h % 2
                if pr >= 2 and c == 0:
                    pe.wait_ge(y_ready, pr - 1)
                o = bank[6 + pr % 2][c * HEAD:(c + 1) * HEAD, :]
                m = dec[:, h % NDEC, :]
                hs = slice(h * HEAD, (h + 1) * HEAD)
                pe.matmul(o[:, 0:S], xdt[:, 0, hs], m[:, 0:S], start=True, stop=True)
                pe.matmul(o[:, P:S], xdt[:, 1, hs], m[:, S:S + P], start=False, stop=True,
                          skip_group_check=True).then_inc(y_full, 1)

            for h in range(NH + 2):
                if h < NH:
                    decay_row(h)
                    modulation_step()
                if h >= 2:
                    head_out(h - 2)
            mod_columns(23, bank[2])
            pe.wait_ge(ysq_ready, 1)
            pe.wait_ge(dec_diff, NH)
            for g in range(GROUPS):
                for tt in range(NT):
                    for k in range(4):
                        mm = pe.matmul(bank[4][:, 2 * g + tt:2 * g + tt + 1],
                                       fT[:, 4 * g + k, tt * P:(tt + 1) * P], ones[:, 0:1],
                                       start=(k == 0), stop=(k == 3))
            mm.then_inc(head_sum, 1)
            pe.wait_ge(head_rstd, 2)
            for g in range(GROUPS):
                for tt in range(NT):
                    r = 2 * g + tt
                    mm = pe.matmul(bank[5][:, g * S + tt * P:g * S + (tt + 1) * P],
                                   rstd[:, r:r + 1].to_broadcast([P, P]), ident[:], start=True, stop=True)
            mm.then_inc(yb_full, 1)
            pe.wait_ge(mod_taken, 2)
            out_projection(0, start[0, "out"], 4, lambda i: oa[:, i, :] if i < KB else yT[:, i - KB, :],
                           lambda j: pe.wait_ge(oa_ready, 1) if j == 0 else pe.wait_ge(ob_ready, 1))

            def moe(l, k):
                m = M[l]
                norm(k)
                pe.wait_ge(h_ready, k + 1)
                for u in range(4):
                    tt, half = u // 2, u % 2
                    for c in range(4):
                        mm = pe.transpose(bank[4 + u][:, c * P:(c + 1) * P],
                                          hT[:, 4 * half + c, tt * P:(tt + 1) * P], ident[:])
                    mm.then_inc(m["hN_full"], 1)
                for tt in range(NT):
                    for kk in range(KB):
                        mm = pe.matmul(bank[0][:, tt * NE:(tt + 1) * NE], hT[:, kk, tt * P:(tt + 1) * P],
                                       router_w[:, kk, :], start=(kk == 0), stop=(kk == KB - 1))
                mm.then_inc(m["logit_full"], 1)
                pe.wait_ge(m["sel_ready"], l + 1)
                sel = small(8).rearrange("p (t e) -> p t e", t=NT)
                pe.matmul(bank[1][:, 0:NE], strict[:], sel[:, 0, :], start=True, stop=True)
                pe.matmul(bank[1][:, NE:2 * NE], ones[:, 0:P], sel[:, 0, :], start=True, stop=False)
                pe.matmul(bank[1][:, NE:2 * NE], strict[:], sel[:, 1, :], start=False, stop=True)
                pe.matmul(bank[1][:, 2 * NE:3 * NE], ones[:, 0:P], sel[:, 0, :], start=True, stop=False)
                pe.matmul(bank[1][:, 2 * NE:3 * NE], ones[:, 0:P], sel[:, 1, :], start=False,
                          stop=True).then_inc(m["rank_full"], 1)
                pe.wait_ge(m["slots_ready"], 2 * l + 2)
                for r in range(4):
                    for tt in range(NT):
                        mm = pe.matmul(bank[2 + r // 2][:, (r % 2) * S + tt * P:(r % 2) * S + (tt + 1) * P],
                                       tok4[:, tt, r:r + 1].to_broadcast([P, P]), ident[:], start=True, stop=True)
                mm.then_inc(m["slot_full"], 1)

                def gather():
                    for kb in range(KB):
                        for tt in range(NT):
                            mm = pe.matmul(bank[6 + kb // 4][:, (kb % 4) * P:(kb % 4 + 1) * P],
                                           hN[:, tt, kb * P:(kb + 1) * P], pick[:, tt, :],
                                           start=(tt == 0), stop=(tt == NT - 1))
                    mm.then_inc(m["gath_full"], 1)

                def scatter(half, first=False, last=False):
                    for d in range(4 * half, 4 * half + 4):
                        mm = pe.matmul(bank[d // 2][:, (d % 2) * S:(d % 2 + 1) * S], ymoe[:, d * P:(d + 1) * P],
                                       spread, start=(first and d % 2 == 0), stop=last, skip_group_check=True)
                    if half:
                        mm.then_inc(m["scat_done"], 1)

                pe.wait_ge(m["hN_evac"], 4 * l + 4)
                pe.wait_ge(m["pick_ready"], 1)
                gather()
                pe.wait_ge(m["y0_ready"], 1)
                pe.wait_ge(m["y1_ready"], 1)
                pe.wait_ge(m["spread_ready"], 1)
                pe.wait_ge(m["rows_ready"], l + 1)
                scatter(0, first=True)
                scatter(1, first=True)
                lo = moe_base[l]
                with pe.Fori(0, NE // 2) as i:
                    n = pe.value_load(tab_i[0:1, bass.ds(i, 1)], min_val=1, max_val=4)
                    g0 = pe.value_load(tab_i[0:1, bass.ds(i + NE // 2, 1)], min_val=0, max_val=NE)
                    with pe.Fori(0, n) as j:
                        g = g0 + j
                        pe.wait_ge(m["hga_ready"], g + 1)
                        pe.wait_ge(m["hgb_ready"], g + 1)
                        for half in range(2):
                            if half:
                                pe.wait_ge(m["y0_ready"], g + 1)
                            for e in range(2):
                                pe.wait_ge(tile_landed[2 * half + e], (i + (lo[2 * half + e] + 1)) * 16)
                            for kb in range(KB):
                                for e in range(2):
                                    mm = pe.matmul(bank[4 + half][e * C:(e + 1) * C, :], hgT[:, kb, e * C:(e + 1) * C],
                                                   w_cols(2 * half + e)[:, kb, :], start=(kb == 0), stop=(kb == KB - 1))
                            mm.then_inc(m["w3_done" if half else "w1_done"], 1)
                        pe.wait_ge(m["y1_ready"], g + 1)
                        pe.wait_ge(m["pick_ready"], g + 2)
                        gather()
                        pe.wait_ge(m["spread_ready"], g + 1)
                        scatter(0)
                        pe.wait_ge(m["hid_ready"], g + 1)
                        for f in range(FB):
                            mm = pe.transpose(bank[4][:, f * P:(f + 1) * P], hid[:, f * P:(f + 1) * P], ident[:])
                        mm.then_inc(m["hidT_full"], 1)
                        scatter(1)
                        pe.wait_ge(m["hidT_ready"], g + 1)
                        for e in range(2):
                            pe.wait_ge(tile_landed[4 + e], (i + (lo[4 + e] + 1)) * 16)
                        for half in range(2):
                            if half:
                                pe.wait_ge(m["hga_ready"], g + 2)
                            for f in range(FB):
                                for e in range(2):
                                    mm = pe.matmul(bank[5 + half][e * C:(e + 1) * C, :], hidT[:, f, e * C:(e + 1) * C],
                                                   w_rows(4 + e)[:, f, half * W:(half + 1) * W],
                                                   start=(f == 0), stop=(f == FB - 1))
                            mm.then_inc(m["down_half"], 1)
                total = pe.value_load(tab_i[0:1, NE:NE + 1], min_val=NE // 2, max_val=NE)
                pe.wait_ge(m["y0_ready"], total + 1)
                pe.wait_ge(m["y1_ready"], total + 1)
                pe.wait_ge(m["spread_ready"], total + 1)
                scatter(0, last=True)
                scatter(1, last=True)

            if NSUB >= 2:
                moe(0, 1)
            if NSUB >= 3:
                norm(2)
                pe.wait_ge(h_ready, 3)
                _, sa = take(1, start[1, "la"])
                _, sl = take(1, start[1, "lb"])
                wa, wl = weight(sa), weight(sl)
                first = [wa[:, 0:512].rearrange("p (k n) -> p k n", k=KB),
                         wa[:, 512:1024].rearrange("p (k n) -> p k n", k=KB),
                         wa[:, 1024:2048].rearrange("p (k n) -> p k n", k=KB)]
                second = [wl[0:64, 0:D], wl[0:64, D:2 * D], wl[:, 2 * D:3 * D]]
                rank = [64, 64, P]
                for i in range(3):
                    pe.wait_ge(mix_ready, i + 1)
                    for k in range(KB):
                        mm = pe.matmul(bank[4][0:rank[i], 0:S], first[i][:, k, :], mixed[i % 2][:, k, :],
                                       start=(k == 0), stop=(k == KB - 1))
                    mm.then_inc(lora_full, 1)
                    pe.wait_ge(lora_evac, i + 1)
                    for u in range(4):
                        ps = proj_bank()
                        for c in range(2):
                            d = 2 * u + c
                            mm = pe.matmul(ps[:, c * S:(c + 1) * S], second[i][:, d * P:(d + 1) * P],
                                           lora[i][0:rank[i], :], start=True, stop=True)
                        mm.then_inc(proj_full, 1)
                for n, i in enumerate((1, 0, 2)):
                    pe.wait_ge(mix_ready, 4 + n)
                    for j in range(2):
                        _, slot = take(1, start[1, "rkv"] + 2 * n + j)
                        (project_N if i == 2 else project_T)(slot, mixed[(3 + n) % 2])

                def head_sums(ps, src):
                    for pr in range(KB):
                        for tt in range(NT):
                            r = tt * NH + 2 * pr
                            mm = pe.matmul(ps[:, r:r + 2], src[:, pr, tt, :], halves[:], start=True, stop=True)
                    return mm

                def head_rows(ps, colsrc, pr):
                    for tt in range(NT):
                        for hh in range(2):
                            r = tt * NH + 2 * pr + hh
                            mm = pe.matmul(ps[hh * HEAD:(hh + 1) * HEAD, tt * P:(tt + 1) * P],
                                           colsrc[:, r:r + 1].to_broadcast([P, HEAD]), ident[:],
                                           start=True, stop=True)
                    return mm

                def head_rows_ring(colsrc, base):
                    for u in range(4):
                        if u >= 2:
                            pe.wait_ge(bcast_used, base + u - 1)
                        for c in range(2):
                            mm = head_rows(bank[6 + u % 2][:, c * S:(c + 1) * S], colsrc, 2 * u + c)
                        mm.then_inc(head_bcast, 1)

                pe.wait_ge(kk_sq, 1)
                head_sums(bank[4], by_tile(3)).then_inc(head_sum, 1)
                pe.wait_ge(rk_ready, 1)
                head_sums(bank[5], by_tile(4)).then_inc(head_sum, 1)
                pe.wait_ge(head_rstd, 3)
                head_rows_ring(rstd, 4)
                pe.wait_ge(rw_ops, 4)

                nsc = [0]

                def rscore_bank():
                    m = nsc[0]
                    if m >= 2:
                        pe.wait_ge(rsc_evac, m - 1)
                    nsc[0] += 1
                    return bank[m % 2]

                def pair_scores(pr):
                    for kind, keys in ((0, rwK), (1, rwB)):
                        for hh in range(2):
                            ps = rscore_bank()
                            fs = slice(hh * HEAD, (hh + 1) * HEAD)
                            for tt in range(NT):
                                mm = pe.matmul(ps[:, tt * S:(tt + 1) * S], keys[fs, pr, tt, :],
                                               AR[fs, pr, tt, :, :], start=True, stop=True)
                            mm.then_inc(rsc_full, 1)
                    pe.wait_ge(kc_ready, pr + 1)
                    for hh in range(2):
                        ps = rscore_bank()
                        fs = slice(hh * HEAD, (hh + 1) * HEAD)
                        for kind in range(2):
                            mm = pe.matmul(ps[:, kind * S:(kind + 1) * S], kcross(pr, kind)[fs, :],
                                           AR[fs, pr, 1, :, :], start=True, stop=True)
                        mm.then_inc(rsc_full, 1)

                def invert(jj):
                    prs = (2 * jj, 2 * jj + 1)
                    for pr in prs:
                        pe.wait_ge(xt1_ready, pr + 1)
                        for u in range(4):
                            mm = pe.transpose(bank[4 + 2 * (pr % 2)][:, u * P:(u + 1) * P],
                                              xinvT(pr)[:, u * P:(u + 1) * P], ident[:])
                        mm.then_inc(x1_full, 1)
                    for i in range(1, 7):
                        for pr in prs:
                            n = jj * 12 + 2 * (i - 1) + pr % 2
                            pe.wait_ge(lm_ready, n + 1)
                            if i == 1:
                                pe.wait_ge(x1_ready, pr + 1)
                            else:
                                pe.wait_ge(xm_ready, n - 1)
                            for u in range(4):
                                us = slice(u * P, (u + 1) * P)
                                mm = pe.matmul(bank[2 + pr % 2][:, us], lmask(pr, i)[:, us], xinv(pr)[:, us],
                                               start=True, stop=True)
                            mm.then_inc(tm_full, 1)
                        for pr in prs:
                            n = jj * 12 + 2 * (i - 1) + pr % 2
                            pe.wait_ge(tm_ready, n + 1)
                            for u in range(4):
                                us = slice(u * P, (u + 1) * P)
                                mm = pe.matmul(bank[5 + 2 * (pr % 2)][:, us], tmid(pr)[:, us], xinvT(pr)[:, us],
                                               start=True, stop=True)
                            if i < 6:
                                for u in range(4):
                                    us = slice(u * P, (u + 1) * P)
                                    mm = pe.matmul(bank[4 + 2 * (pr % 2)][:, us], xinvT(pr)[:, us],
                                                   tmid(pr)[:, us], start=True, stop=True)
                            mm.then_inc(xm_full, 1)

                def solve(pr):
                    n = (pr // 2) * 12 + 10 + pr % 2
                    pe.wait_ge(xm_ready, n + 1)
                    bw = bank[2 + pr % 2]
                    for tt in range(NT):
                        for hh in range(2):
                            o = bw[:, hh * HEAD:(hh + 1) * HEAD]
                            h = 2 * pr + hh
                            mm = pe.matmul(o, sc(pr, 0, tt, hh), vN1[:, tt, h, :], start=True, stop=(tt == 0))
                            if tt:
                                pe.matmul(o, scro(pr, 0, hh), vN1[:, 0, h, :], start=False, stop=False)
                                mm = pe.matmul(o, scro(pr, 2, hh), uneg(pr, 0)[:, hh * HEAD:(hh + 1) * HEAD],
                                               start=False, stop=True)
                        mm.then_inc(w_full, 1)
                        pe.wait_ge(w_ready, 2 * pr + tt + 1)
                        for hh in range(2):
                            mm = pe.matmul(bw[:, P + hh * HEAD:P + (hh + 1) * HEAD],
                                           xinvT(pr)[:, (2 * tt + hh) * P:(2 * tt + hh + 1) * P],
                                           tmid(pr)[:, (2 * tt + hh) * HEAD:(2 * tt + hh + 1) * HEAD],
                                           start=True, stop=True)
                        mm.then_inc(u_full, 1)
                        pe.wait_ge(u_ready, 2 * pr + tt + 1)
                    for hh in range(2):
                        h = 2 * pr + hh
                        o = bank[4 + 2 * (pr % 2)][hh * HEAD:(hh + 1) * HEAD, :]
                        un = lambda tt: uneg(pr, tt)[:, hh * HEAD:(hh + 1) * HEAD]
                        pe.matmul(o[:, 0:P], vN1[:, 0, h, :], sc(pr, 1, 0, hh), start=True, stop=False)
                        pe.matmul(o[:, 0:P], un(0), sc(pr, 3, 0, hh), start=False, stop=True)
                        pe.matmul(o[:, P:S], vN1[:, 1, h, :], sc(pr, 1, 1, hh), start=True, stop=False)
                        pe.matmul(o[:, P:S], un(1), sc(pr, 3, 1, hh), start=False, stop=False)
                        pe.matmul(o[:, P:S], vN1[:, 0, h, :], scro(pr, 1, hh), start=False, stop=False)
                        mm = pe.matmul(o[:, P:S], un(0), scro(pr, 3, hh), start=False, stop=True)
                    mm.then_inc(ry_full, 1)

                pe.wait_ge(proj_evac, 26 + 12 + 12)
                pe.wait_ge(bcast_used, 8)
                for jj in range(KB // 2):
                    for pr in (2 * jj, 2 * jj + 1):
                        pair_scores(pr)
                    if jj > 0:
                        pe.wait_ge(ry_ready, 2 * jj)
                    invert(jj)
                    for pr in (2 * jj, 2 * jj + 1):
                        solve(pr)

                pe.wait_ge(ry_ready, KB)

                head_sums(bank[4], oR).then_inc(head_sum, 1)
                pe.wait_ge(gn_mean, 1)
                head_rows_ring(gm_mean, 8)
                pe.wait_ge(gn_sq, 1)
                head_sums(bank[4], by_tile(3)).then_inc(head_sum, 1)
                pe.wait_ge(head_rstd, 4)
                pe.wait_ge(bcast_used, 12)
                head_rows_ring(rstd, 12)
                pe.wait_ge(bv_ready, 1)
                pe.wait_ge(ry_ready, KB)
                for pr in range(KB):
                    for tt in range(NT):
                        mm = pe.transpose(bank[pr // 2][:, (pr % 2) * S + tt * P:(pr % 2) * S + (tt + 1) * P],
                                          bvN[:, tt, 2 * pr:2 * pr + 2, :].rearrange("p h n -> p (h n)"), ident[:])
                mm.then_inc(bvT_full, 1)
                pe.wait_ge(og_ready, 1)
                og = blocks(4)
                out_projection(1, start[1, "wo"], 2, lambda i: og[:, i, :], lambda j: None)
            if NSUB >= 4:
                moe(1, 3)
            norm(NSUB)
            pe.wait_ge(h_ready, NSUB + 1)
            for u in range(8):
                tt, q = u // 4, u % 4
                for c in range(2):
                    mm = pe.transpose(bank[u][:, c * P:(c + 1) * P],
                                      hT[:, 2 * q + c, tt * P:(tt + 1) * P], ident[:])
                mm.then_inc(o_full, 1)

        @block.scalar
        def _(act):
            count = [0]

            def link(ins):
                count[0] += 1
                ins.then_inc(act_chain, 1)
                act.wait_ge(act_chain, count[0])

            act.wait_ge(vrows_zeroed, 1)
            for name, (g, r, n) in VEC.items():
                src = t[name]
                flat = src.rearrange({1: "a -> a", 2: "a b -> (a b)", 3: "a b c -> (a b c)"}[len(src.shape)])
                act.dma_start(vrows[r:r + n, g, :], flat.rearrange("(n p) -> n p", p=P)).then_inc(vec_landed, 16)
            act.dma_start(xN[:, :, :], t["x"][0].rearrange("(t p) d -> p t d", p=P)).then_inc(x_landed, 16)
            act.dma_start(dt_bias[:], t["ev_dt_bias"].rearrange("a h -> h a")).then_inc(small_landed, 16)
            act.dma_start(a_log[:], t["ev_a_log"].rearrange("a h -> h a")).then_inc(small_landed, 16)
            skip = t["ev_d_skip"].rearrange("a (j two) -> two (a j)", two=2)
            for hh in range(2):
                act.dma_start(dskip[hh * HEAD:(hh + 1) * HEAD, :],
                              skip[hh:hh + 1, :].to_broadcast([HEAD, KB])).then_inc(small_landed, 16)
            act.dma_start(w_dt[:], row_block(t["ev_w_in"][0])[:, :, IN_COLS - NH:IN_COLS]).then_inc(small_landed, 16)
            act.dma_start(router_w[:], row_block(t["router_w"])).then_inc(small_landed, 16)
            act.dma_start(router_b[:], t["router_b"].rearrange("(a e) -> a e", a=1).to_broadcast([P, NE])
                          ).then_inc(small_landed, 16)

            act.wait_ge(vec_cols, 1)
            act.activation(csilu[:], cols("c", 0, KB), ACT.Silu).then_inc(csilu_ready, 1)
            for u in range(4):
                act.wait_ge(xT_psum, u + 1)
                ins = act.activation(xT[:, 2 * u:2 * u + 2, :].rearrange("p k s -> p (k s)"), bank[u][:], ACT.Copy)
            ins.then_inc(xT_evac, 1)
            act.wait_ge(consts, 1)

            def mod_evac(m, row_banks):
                act.wait_ge(mod_full, m + 1)
                if m >= 2:
                    act.wait_ge(mod_cols, m - 1)
                act.activation(mod_rows[:, m % 2, :], row_banks[m % 2][:], ACT.Copy).then_inc(mod_row, 1)

            mod_next = [MOD_FIRST]

            def modulation_step():
                if mod_next[0] < 24:
                    mod_evac(mod_next[0], (bank[0], bank[1]))
                    mod_next[0] += 1

            for m in range(MOD_FIRST):
                mod_evac(m, (bank[6], bank[7]))

            def norm(k):
                if k == 0:
                    act.wait_ge(xT_evac, 1)
                else:
                    act.wait_ge(x_ready, k)
                act.activation(squares[:, :, :], xT[:, :, :], ACT.Square).then_inc(sq_ready, 1)
                act.wait_ge(sums_psum, k + 1)
                act.activation(rs_root[:, 0:NT], bank[7][:, 0:NT], ACT.Sqrt, bias=eps_col[:, 0:1],
                               scale=1.0 / D).then_inc(root_ready, 1)

            norm(0)
            evac = [0]

            def evacuate(dst, func=ACT.Copy, **kw):
                n = evac[0]
                act.wait_ge(proj_full, n + 1)
                act.activation(dst, bank[n % 4][:], func, **kw).then_inc(proj_evac, 1)
                evac[0] += 1

            def evac_T(dst, first):
                for u in range(2):
                    b = first + 2 * u
                    evacuate(dst[:, b:b + 2, :].rearrange("p k s -> p (k s)"), ACT.Copy)

            act.wait_ge(lb_max, 1)
            act.activation(lbe[:], lbe[:], ACT.Exp).then_inc(start_exp, 1)
            act.wait_ge(small_landed, 16 * 7)
            act.activation(a_neg[:], a_log[:], ACT.Exp).then_inc(start_exp, 1)
            for u in range(4):
                n = evac[0]
                act.wait_ge(proj_full, n + 1)
                act.activation(fT[:, 2 * u:2 * u + 2, :].rearrange("p k s -> p (k s)"), bank[n % 4][:],
                               ACT.Sigmoid).then_inc(proj_evac, 1)
                evac[0] += 1
            act.wait_ge(k_ready, 1)
            act.activation(fT[:, :, :], fT[:, :, :], ACT.Ln).then_inc(logf_ready, 1)
            evac_T(qT, 0)
            evac_T(qT, 4)

            def level_exp(i):
                act.wait_ge(dl_ready, i + 1)
                act.wait_ge(dr_ready, i + 1)
                act.activation(buf(eT[i % 2]), buf(eT[i % 2]), ACT.Exp).then_inc(el_exp, 1)

            def evac_v(j):
                for tt in range(NT):
                    evacuate(vN[:, tt, j * W:(j + 1) * W])

            def evac_xbc(first):
                for u in range(2):
                    n = evac[0]
                    b = first + 2 * u
                    act.wait_ge(conv_zero, 1)
                    act.wait_ge(proj_full, n + 1)
                    act.activation(xpad[:, b:b + 2, TAPS - 1:],
                                   bank[n % 4][:].rearrange("p (k s) -> p k s", k=2), ACT.Copy).then_inc(proj_evac, 1)
                    evac[0] += 1

            level_exp(0)
            evac_v(0)
            level_exp(1)
            evac_v(1)
            level_exp(2)
            evac_xbc(8)
            level_exp(3)
            evac_xbc(0)
            level_exp(4)
            evac_xbc(4)
            level_exp(5)
            act.wait_ge(dtz, 1)
            act.activation(dts[:, 1, :], dts[:, 0, :], ACT.Abs).then_inc(dtabs, 1)
            act.wait_ge(dtabs, 1)
            link(act.activation(dts[:, 1, :], dts[:, 1, :], ACT.Exp, scale=-1.0))
            act.activation(dts[:, 2, :], dts[:, 1, :], ACT.Ln, bias=1.0).then_inc(dtln, 1)
            evac_T(zT, 0)
            level_exp(6)
            evac_T(zT, 4)
            level_exp(7)
            evac_T(gT, 0)
            evac_T(gT, 4)
            act.wait_ge(proj_evac, 26)
            act.wait_ge(conv_done, XBLK)
            act.activation(xpad[:, :, TAPS - 1:], xpad[:, :, TAPS - 1:], ACT.Silu).then_inc(conv_silu, 1)
            act.activation(buf(10), buf(10), ACT.Silu)
            act.activation(buf(11), buf(11), ACT.Silu).then_inc(silu_g, 1)
            for u in range(4):
                act.wait_ge(o_full, u + 1)
                dst = lambda x: x[:, 2 * u:2 * u + 2, :].rearrange("p k s -> p (k s)")
                act.activation(dst(oa), bank[6 + u % 2][:], ACT.Copy)
                act.activation(dst(fT), bank[6 + u % 2][:], ACT.Square).then_inc(o_evac, 1)
                modulation_step()
            act.wait_ge(head_sum, 1)
            act.activation(rs_root[:, 0:2 * KB], bank[4][:, 0:2 * KB], ACT.Sqrt, bias=eps_col[:, 0:1],
                           scale=1.0 / P).then_inc(head_root, 1)
            for h in range(NH):
                act.wait_ge(dec_diff, h + 1)
                act.activation(dec[:, h % NDEC, :], dec[:, h % NDEC, :], ACT.Exp).then_inc(dec_exp, 1)
                modulation_step()
            act.wait_ge(y_ready, KB)
            act.wait_ge(head_sum, 1)
            act.activation(fT[:, :, :], yT[:, :, :], ACT.Square).then_inc(ysq_ready, 1)
            act.wait_ge(head_sum, 2)
            act.activation(rs_root[:, 0:4], bank[4][:, 0:4], ACT.Sqrt, bias=eps_col[:, 0:1],
                           scale=1.0 / (4 * P)).then_inc(head_root, 1)

            def moe(l, k):
                m = M[l]
                norm(k)
                for u in range(4):
                    tt, half = u // 2, u % 2
                    act.wait_ge(m["hN_full"], 4 * l + u + 1)
                    act.activation(hN[:, tt, half * W:(half + 1) * W], bank[4 + u][:], ACT.Copy).then_inc(m["hN_evac"], 1)
                act.wait_ge(m["lmax"], l + 1)
                act.activation(small(1), small(1), ACT.Exp).then_inc(m["lexp"], 1)
                act.wait_ge(m["slot_full"], l + 1)
                for r in range(2):
                    ins = act.activation(rows4[:, 2 * r:2 * r + 2, :].rearrange("p r s -> p (r s)"),
                                         bank[2 + r][:], ACT.Copy)
                ins.then_inc(m["rows_ready"], 1)

                def take_a():
                    act.activation(hgT[:, 0:4, :].rearrange("p k c -> p (k c)"), bank[6][:],
                                   ACT.Copy).then_inc(m["hga_ready"], 1)

                act.wait_ge(m["gath_full"], 1)
                take_a()
                total = act.value_load(tab_i[0:1, NE:NE + 1], min_val=NE // 2, max_val=NE)
                with act.Fori(0, total) as g:
                    act.wait_ge(m["w1_done"], g + 1)
                    act.activation(hsil, bank[4][:], ACT.Silu).then_inc(m["silu_done"], 1)
                    act.wait_ge(m["gath_full"], g + 2)
                    take_a()
                    act.wait_ge(m["hidT_full"], g + 1)
                    act.activation(hidT[:, :, :].rearrange("p f c -> p (f c)"), bank[4][:],
                                   ACT.Copy).then_inc(m["hidT_ready"], 1)
                    act.wait_ge(m["down_half"], g * 2 + 1)
                    act.wait_ge(m["scat_done"], g + 2)
                    act.activation(ymoe[:, 0:W], bank[5][:], ACT.Copy).then_inc(m["y0_ready"], 1)

            if NSUB >= 2:
                moe(0, 1)
            if NSUB >= 3:
                norm(2)
                lora_func = [ACT.Tanh, ACT.Copy, ACT.Sigmoid]
                for i, (dst, bias) in enumerate(((sgT, "od_w_dec0"), (aT, "od_a0"), (ggT, None))):
                    r = P if i == 2 else 64
                    act.wait_ge(lora_full, i + 1)
                    act.activation(lora[i][0:r, :], bank[4][0:r, 0:S], lora_func[i]).then_inc(lora_evac, 1)
                    for u in range(4):
                        n = evac[0]
                        act.wait_ge(proj_full, n + 1)
                        if bias is None:
                            ins = act.activation(dst[:, 2 * u:2 * u + 2, :].rearrange("p k s -> p (k s)"),
                                                 bank[n % 4][:], ACT.Copy)
                        else:
                            for c in range(2):
                                b = 2 * u + c
                                ins = act.activation(dst[:, b, :], bank[n % 4][:, c * S:(c + 1) * S], ACT.Sigmoid,
                                                     bias=col(bias, b))
                        ins.then_inc(proj_evac, 1)
                        evac[0] += 1
                evac_T(k1T, 0)
                evac_T(k1T, 4)
                evac_T(rT, 0)
                evac_T(rT, 4)
                for j in range(2):
                    for tt in range(NT):
                        evacuate(vN1[:, tt, 8 * j:8 * j + 8, :].rearrange("p h n -> p (h n)"))
                act.wait_ge(head_sum, 3)
                act.activation(rs_root[:], bank[4][:, 0:2 * NH], ACT.Sqrt).then_inc(head_root, 1)
                act.wait_ge(rw_diff, 2)
                act.activation(buf(3), buf(4), ACT.Exp, scale=-E05).then_inc(rw_exp, 1)
                act.activation(buf(10), buf(10), ACT.Exp, scale=-E05).then_inc(rw_exp, 1)
                act.wait_ge(rw_exp, 1)
                act.activation(buf(4), buf(4), ACT.Exp, scale=E05).then_inc(rw_exp, 1)
                act.wait_ge(kmid_diff, 1)
                act.activation(kmid[:], kmid[:], ACT.Exp, scale=E05).then_inc(kmid_ready, 1)
                for i in range(KB // 2 * 12):
                    jj, r = i // 12, i % 12
                    pr = 2 * jj + r % 2
                    act.wait_ge(tm_full, i + 1)
                    act.activation(tmid(pr), bank[2 + pr % 2][:], ACT.Copy).then_inc(tm_ready, 1)
                    if r == 11:
                        for q in (2 * jj, 2 * jj + 1):
                            for tt in range(NT):
                                act.wait_ge(w_full, 2 * q + tt + 1)
                                act.activation(tmid(q)[:, tt * P:(tt + 1) * P], bank[2 + q % 2][:, 0:P],
                                               ACT.Copy).then_inc(w_ready, 1)
                                act.wait_ge(u_full, 2 * q + tt + 1)
                                act.activation(uneg(q, tt), bank[2 + q % 2][:, P:2 * P], ACT.Copy,
                                               scale=-1.0).then_inc(u_ready, 1)
                act.wait_ge(bcast_used, 12)
                act.activation(buf(3).rearrange("p (k t s) -> p k t s", k=KB, t=NT), oR, ACT.Square).then_inc(gn_sq, 1)
                act.wait_ge(head_sum, 6)
                act.activation(rs_root[:], bank[4][:, 0:2 * NH], ACT.Sqrt, bias=eps_col[:, 1:2],
                               scale=1.0 / HEAD).then_inc(head_root, 1)
            if NSUB >= 4:
                moe(1, 3)
            norm(NSUB)
            for u in range(8):
                tt, q = u // 4, u % 4
                act.wait_ge(o_full, 4 + u + 1)
                act.activation(hN[:, tt, 2 * q * P:(2 * q + 2) * P], bank[u][:, 0:S],
                               ACT.Copy).then_inc(o_evac, 1)

        @block.vector
        def _(dve):
            count = [0]

            def link(ins):
                count[0] += 1
                ins.then_inc(dve_chain, 1)
                dve.wait_ge(dve_chain, count[0])

            tt_ = dve.tensor_tensor
            ts_ = dve.tensor_scalar
            stt = dve.scalar_tensor_tensor

            dve.memset(vrows[:], 0.0).then_inc(vrows_zeroed, 1)
            dve.wait_ge(vec_T, 1)
            dve.tensor_copy(vcols[:].rearrange("p g r -> p (g r)"), bank[4][:, 0:3 * P]).then_inc(vec_cols, 1)
            dve.wait_ge(vec_cols, 1)
            lg = cols("hg_lb_logits", 0, 3 * KB).rearrange("p (r k) -> p r k", r=3)
            link(tt_(lbm[:], lg[:, 0, :], lg[:, 1, :], ALU.max))
            link(tt_(lbm[:], lbm[:], lg[:, 2, :], ALU.max))
            tt_(lbe[:], lg, lbm[:].unsqueeze(1).to_broadcast([P, 3, KB]), ALU.subtract).then_inc(lb_max, 1)
            dve.wait_ge(start_exp, 1)
            link(tt_(lbm[:], lbe[:, 0, :], lbe[:, 1, :], ALU.add))
            link(tt_(lbm[:], lbm[:], lbe[:, 2, :], ALU.add))
            link(dve.reciprocal(lbm[:], lbm[:]))
            link(tt_(lb[:], lbe[:, 1, :], lbm[:], ALU.mult))
            link(ts_(oml[:], lb[:], -1.0, 1.0, ALU.mult, ALU.add))

            def modulation(l, a, b, cols_bank):
                return tt_(modT[:, l, a:b], cols_bank[:, 48 * l + a:48 * l + b],
                           cols("mod_b", 48 * l + a, 48 * l + b), ALU.add)

            def gains(l, f):
                link(ts_(gain[:, l, f, :], modT[:, l, (3 * f + 1) * KB:(3 * f + 2) * KB], 1.0, None, ALU.add))
                link(tt_(gain[:, l, f, :], gain[:, l, f, :], cols("norm_w", (2 * l + f) * KB, (2 * l + f + 1) * KB),
                         ALU.mult))

            def norm(k):
                dve.wait_ge(root_ready, k + 1)
                dve.reciprocal(rstd[:, 0:NT], rs_root[:, 0:NT]).then_inc(rstd_ready, 1)
                dve.wait_ge(bcast_psum, k + 1)
                link(tt_(hT[:, :, :], xT[:, :, :], bank[6][:, 0:S].unsqueeze(1).to_broadcast([P, KB, S]), ALU.mult))
                for b in range(KB):
                    if k == NSUB:
                        ins = ts_(hT[:, b, :], hT[:, b, :], col("final_norm_w", b), None, ALU.mult)
                    else:
                        l, f = k // 2, k % 2
                        sh = modT[:, l, 3 * f * KB + b:3 * f * KB + b + 1]
                        ins = ts_(hT[:, b, :], hT[:, b, :], gain[:, l, f, b:b + 1], sh, ALU.mult, ALU.add)
                ins.then_inc(h_ready, 1)

            def residual(k):
                l, f = k // 2, k % 2
                for b in range(KB):
                    gt = modT[:, l, (3 * f + 2) * KB + b:(3 * f + 2) * KB + b + 1]
                    ins = stt(xT[:, b, :], bank[b // 2][:, (b % 2) * S:(b % 2 + 1) * S], gt, xT[:, b, :],
                              ALU.mult, ALU.add)
                ins.then_inc(x_ready, 1)

            dve.wait_ge(mod_cols, MOD_FIRST)
            modulation(0, 0, 4 * MOD_FIRST, bank[5]).then_inc(mod_taken, 1)
            dve.wait_ge(mod_taken, 1)
            gains(0, 0)
            dve.wait_ge(xT_evac, 1)
            norm(0)

            dve.wait_ge(proj_evac, 4)
            for b in range(KB):
                ins = ts_(fT[:, b, :], fT[:, b, :], oml[:, b:b + 1], lb[:, b:b + 1], ALU.mult, ALU.add)
            link(ins)
            ts_(kT[:, :, :], fT[:, :, :], -1.0, 1.0, ALU.mult, ALU.add).then_inc(k_ready, 1)
            dve.wait_ge(consts, 1)
            dve.wait_ge(logf_ready, 1)
            for b in range(KB):
                ins = dve.tensor_tensor_scan(bT[:, b, :], ones[:, 0:S], fT[:, b, :], 0.0, ALU.mult, ALU.add)
            ins.then_inc(b_ready, 1)
            dve.wait_ge(b_ready, 1)

            def level_diff(i):
                h = (HALVES + [P])[i]
                e = buf(eT[i % 2]).rearrange("p (b two h) -> p b two h", two=2, h=h)
                b = buf(5).rearrange("p (b two h) -> p b two h", two=2, h=h)
                if i >= 2:
                    dve.wait_ge(score_full, 4 + 2 * (i - 1))
                mid = b[:, :, 0, h - 1:h].to_broadcast([P, KB * S // (2 * h), h])
                tt_(e[:, :, 1, :], b[:, :, 1, :], mid, ALU.subtract).then_inc(dr_ready, 1)

            def level_mult(i):
                h = (HALVES + [P])[i]
                e = buf(eT[i % 2]).rearrange("p (b two h) -> p b two h", two=2, h=h)
                q = buf(2).rearrange("p (b two h) -> p b two h", two=2, h=h)
                dve.wait_ge(el_exp, i + 1)
                dve.wait_ge(proj_evac, 8)
                tt_(e[:, :, 1, :], e[:, :, 1, :], q[:, :, 1, :], ALU.mult).then_inc(eq_ready, 1)

            def level_take(i):
                h = HALVES[i]
                for tt in range(NT):
                    m = 4 + 2 * i + tt
                    dve.wait_ge(score_full, m + 1)
                    src = bank[4 + m % 2][:].rearrange("p (u s) -> p u s", s=64)
                    dst = scd[:, tt, :, :].rearrange("p u (b two h) -> p u b two h", two=2, h=h)[:, :, :, 1, :]
                    mk = level[:, i, :].rearrange("p (b two h) -> p b two h", two=2, h=h)[:, :, 1, :]
                    ins = dve.copy_predicated(dst, mk.unsqueeze(1).to_broadcast([P, KB, 64 // h, h]).bitcast(I32),
                                              src.rearrange("p u (b h) -> p u b h", h=h))
                    ins.then_inc(score_evac, 1)

            level_diff(0)
            level_diff(1)
            for r in range(2):
                for tt in range(NT):
                    m = 2 * r + tt
                    dve.wait_ge(score_full, m + 1)
                    tt_(scd[:, tt, 4 * r:4 * r + 4, :], bank[4 + m % 2][:].rearrange("p (u s) -> p u s", u=4),
                        ident[:].unsqueeze(1).to_broadcast([P, 4, P]), ALU.mult).then_inc(score_evac, 1)
            dve.wait_ge(score_evac, 4)
            for i in range(8):
                level_mult(i)
                if i < 7:
                    level_take(i)
                if i + 2 < 8:
                    level_diff(i + 2)
                if i == 5:
                    dve.wait_ge(dt_full, 1)
                    dve.wait_ge(small_landed, 16 * 7)
                    ts_(dts[:, 0, :], bank[6][0:NH, 0:S], dt_bias[:], None, ALU.add).then_inc(dtz, 1)
                if i == 6:
                    dve.wait_ge(start_exp, 2)
                    dve.wait_ge(dtln, 1)
                    link(stt(dts[:, 3, :], dts[:, 0, :], 0.0, dts[:, 2, :], ALU.max, ALU.add))
                    link(ts_(dts[:, 2, :], dts[:, 3, :], a_neg[:], -1.0, ALU.mult, ALU.mult))
                    dve.tensor_tensor_scan(dts[:, 4, :], ones[0:NH, 0:S], dts[:, 2, :], 0.0, ALU.mult,
                                           ALU.add).then_inc(dt_ready, 1)
            for r in range(2):
                m = 18 + r
                dve.wait_ge(score_full, m + 1)
                dve.tensor_copy(scx[:, 4 * r:4 * r + 4, :].rearrange("p u s -> p (u s)"),
                                bank[4 + m % 2][:]).then_inc(score_evac, 1)
            dve.wait_ge(proj_evac, 18)
            for b in range(XBLK):
                tmp = ctmp[:, b % 2, :]
                wt = lambda j: col("ev_conv_w", j * XBLK + b)
                link(ts_(tmp, xpad[:, b, 0:S], wt(0), col("ev_conv_b", b), ALU.mult, ALU.add))
                for j in range(1, TAPS - 1):
                    link(stt(tmp, xpad[:, b, j:j + S], wt(j), tmp, ALU.mult, ALU.add))
                stt(xpad[:, b, TAPS - 1:], xpad[:, b, TAPS - 1:], wt(TAPS - 1), tmp, ALU.mult,
                    ALU.add).then_inc(conv_done, 1)
            dve.wait_ge(dtN_full, 1)
            dve.tensor_copy(dtN[:].rearrange("p a t h -> p (a t h)"), bank[4][:, 0:4 * NH]).then_inc(dtN_ready, 1)
            dve.wait_ge(dtN_ready, 1)
            for u in range(4):
                tt, half = u // 2, u % 2
                dve.wait_ge(xs_full, u + 1)
                tt_(xdt[:, tt, half * W:(half + 1) * W].rearrange("p (h n) -> p h n", n=HEAD),
                    bank[[5, 6, 7, 5][u]][:].rearrange("p (h n) -> p h n", n=HEAD),
                    dtN[:, 0, tt, 8 * half:8 * half + 8].unsqueeze(2).to_broadcast([P, 8, HEAD]),
                    ALU.mult).then_inc(xdt_ready, 1)
            for g in range(GROUPS):
                dve.wait_ge(cb_full, g + 1)
                ps = bank[6 + g]
                tt_(cbm[:, g, 0:P], ps[:, 0:P], causal[:], ALU.mult)
                tt_(cbm[:, g, 2 * P:3 * P], ps[:, S:S + P], causal[:], ALU.mult)
                dve.tensor_copy(cbm[:, g, P:S], ps[:, P:S]).then_inc(cb_ready, 1)
            dve.wait_ge(head_root, 1)
            dve.reciprocal(rstd[:, 0:2 * KB], rs_root[:, 0:2 * KB]).then_inc(head_rstd, 1)
            dve.wait_ge(silu_g, 1)
            for u in range(4):
                dve.wait_ge(head_bcast, u + 1)
                o = oa[:, 2 * u:2 * u + 2, :].rearrange("p k s -> p (k s)")
                ins = tt_(o, o, bank[4 + u % 2][:], ALU.mult)
                ins.then_inc(bcast_used, 1)
            dve.wait_ge(bcast_used, 4)
            for h in range(KB):
                ins = stt(oa[:, h, :], oa[:, h, :], col("ev_hg_norm", h), gT[:, h, :], ALU.mult, ALU.mult)
            ins.then_inc(oa_ready, 1)

            def decay_diff(h):
                dve.wait_ge(row_full, h + 1)
                if h >= NDEC:
                    dve.wait_ge(y_full, h - NDEC + 1)
                row = bank[4 + h % 2]
                dd = dec[:, h % NDEC, :]
                ts_(dd[:, 0:S], row[:, 0:S], dtN[:, 1, 0, h:h + 1], 0.0, ALU.subtract, ALU.min)
                ts_(dd[:, S:S + P], row[:, P:S], dtN[:, 1, 1, h:h + 1], 0.0, ALU.subtract,
                    ALU.min).then_inc(dec_diff, 1)

            def decay_mult(h):
                dve.wait_ge(dec_exp, h + 1)
                dd = dec[:, h % NDEC, :]
                tt_(dd, dd, cbm[:, h // 8, :], ALU.mult).then_inc(dec_mat, 1)

            def ssd_out(pr):
                dve.wait_ge(y_full, 2 * pr + 2)
                link(stt(yT[:, pr, :], xpad[:, pr, TAPS - 1:], dskip[:, pr:pr + 1], bank[6 + pr % 2][:, 0:S],
                         ALU.mult, ALU.add))
                tt_(yT[:, pr, :], yT[:, pr, :], zT[:, pr, :], ALU.mult).then_inc(y_ready, 1)

            dve.wait_ge(cb_ready, 2)
            for h in range(NH + 4):
                if h < NH:
                    decay_diff(h)
                if 1 <= h <= NH:
                    decay_mult(h - 1)
                if h >= 4 and h % 2 == 1:
                    ssd_out((h - 4) // 2)
            dve.wait_ge(mod_cols, 24)
            modulation(0, 4 * MOD_FIRST, 48, bank[2])
            modulation(1, 0, 48, bank[2]).then_inc(mod_taken, 1)
            dve.wait_ge(mod_taken, 2)
            for l, f in ((0, 1), (1, 0), (1, 1)):
                gains(l, f)
            dve.wait_ge(head_root, 2)
            dve.reciprocal(rstd[:, 0:4], rs_root[:, 0:4]).then_inc(head_rstd, 1)
            dve.wait_ge(yb_full, 1)
            for b in range(KB):
                g = b // 4
                ins = stt(yT[:, b, :], yT[:, b, :], col("ev_ssm_norm", b), bank[5][:, g * S:(g + 1) * S],
                          ALU.mult, ALU.mult)
            ins.then_inc(ob_ready, 1)
            dve.wait_ge(tile_used, USED[0])
            residual(0)

            def first_of(dst, vals, top, shape, scratch):
                link(tt_(dst, vals, top, ALU.is_equal))
                link(ts_(scratch[0], dst, -4.0, 4.0, ALU.mult, ALU.add))
                link(tt_(scratch[0], scratch[0], shape[0], ALU.add))
                link(dve.tensor_reduce(scratch[1], scratch[0], AX.X, ALU.min))
                link(tt_(dst, shape[0], scratch[1].unsqueeze(len(scratch[1].shape)).to_broadcast(shape[1]),
                         ALU.is_equal))

            def moe(l, k):
                m = M[l]
                norm(k)
                v3 = lambda i: small(i).rearrange("p (t e) -> p t e", t=NT)
                v8 = lambda i: small(i).rearrange("p (a e) -> p a e", e=4)
                dve.wait_ge(m["logit_full"], l + 1)
                dve.wait_ge(small_landed, 16 * 7)
                link(tt_(v3(0), bank[0][:, 0:2 * NE].rearrange("p (t e) -> p t e", t=NT),
                         router_b[:].unsqueeze(1).to_broadcast([P, NT, NE]), ALU.add))
                mx = small(20)[:, 0:2]
                link(dve.tensor_reduce(mx, v3(0), AX.X, ALU.max))
                tt_(v3(1), v3(0), mx.unsqueeze(2).to_broadcast([P, NT, NE]), ALU.subtract).then_inc(m["lmax"], 1)
                dve.wait_ge(m["lexp"], l + 1)
                sm = small(20)[:, 2:4]
                link(dve.tensor_reduce(sm, v3(1), AX.X, ALU.add))
                link(dve.reciprocal(sm, sm))
                link(tt_(v3(2), v3(1), sm.unsqueeze(2).to_broadcast([P, NT, NE]), ALU.mult))
                p8 = v8(2)
                pos = tie4[:].unsqueeze(1).to_broadcast([P, 8, 4])
                t1, t2 = small(20)[:, 8:16], small(20)[:, 16:24]
                scr = (v8(5), small(20)[:, 24:32])
                b8 = lambda x: x.unsqueeze(2).to_broadcast([P, 8, 4])
                link(dve.tensor_reduce(t1, p8, AX.X, ALU.max))
                first_of(v8(3), p8, b8(t1), (pos, [P, 8, 4]), scr)
                link(stt(v8(6), v8(3), -2.0, p8, ALU.mult, ALU.add))
                link(dve.tensor_reduce(t2, v8(6), AX.X, ALU.max))
                first_of(v8(4), v8(6), b8(t2), (pos, [P, 8, 4]), scr)
                gs = small(21)[:, 0:8].rearrange("p (t g) -> p t g", t=NT)
                gm = small(21)[:, 8:16].rearrange("p (t g) -> p t g", t=NT)
                gx = small(21)[:, 16:18]
                pos2 = tie4[:].unsqueeze(1).to_broadcast([P, NT, 4])
                scr2 = (small(21)[:, 20:28].rearrange("p (t g) -> p t g", t=NT), small(21)[:, 28:30])
                link(tt_(small(21)[:, 0:8], t1, t2, ALU.add))
                link(dve.tensor_reduce(gx, gs, AX.X, ALU.max))
                first_of(gm, gs, gx.unsqueeze(2).to_broadcast([P, NT, 4]), (pos2, [P, NT, 4]), scr2)
                gmb = b8(small(21)[:, 8:16])
                link(tt_(v8(3), v8(3), gmb, ALU.mult))
                link(tt_(v8(4), v8(4), gmb, ALU.mult))
                tt_(small(8), small(3), small(4), ALU.add).then_inc(m["sel_ready"], 1)
                ga, gb_ = small(22)[:, 0:2], small(22)[:, 2:4]
                link(tt_(small(6), small(3), small(2), ALU.mult))
                link(dve.tensor_reduce(ga, v3(6), AX.X, ALU.add))
                link(tt_(small(6), small(4), small(2), ALU.mult))
                link(dve.tensor_reduce(gb_, v3(6), AX.X, ALU.add))
                gsum = small(22)[:, 4:6]
                link(tt_(gsum, ga, gb_, ALU.add))
                link(dve.reciprocal(gsum, gsum))
                link(tt_(tok4[:, :, 2], ga, gsum, ALU.mult))
                link(tt_(tok4[:, :, 3], gb_, gsum, ALU.mult))
                dve.wait_ge(m["rank_full"], l + 1)
                cnt = bank[1][:, 2 * NE:3 * NE]
                need, tmp = small(22)[:, 8:8 + NE], small(7)[:, 0:NE]
                link(ts_(need, cnt, float(C), 1.0, ALU.is_gt, ALU.add))
                for c in range(2, S // C):
                    link(ts_(tmp, cnt, float(c * C), None, ALU.is_gt))
                    link(tt_(need, need, tmp, ALU.add))
                nblk, base = tab_f[:, 0:NE // 2], tab_f[:, NE // 2:NE]
                link(dve.tensor_reduce(nblk, need.rearrange("p (i e) -> p i e", e=2), AX.X, ALU.max))
                link(dve.tensor_tensor_scan(base, ones[:, 0:NE // 2], nblk, 0.0, ALU.mult, ALU.add))
                link(dve.tensor_copy(tab_f[:, NE:NE + 1], tab_f[:, NE - 1:NE]))
                link(tt_(base, base, nblk, ALU.subtract))
                dve.tensor_copy(tab_i[:, 0:NE + 1], tab_f[0:1, 0:NE + 1]).then_inc(m["tab_ready"], 1)
                rank = bank[1][:, 0:2 * NE]
                link(dve.tensor_copy(small(6), rank))
                for c in range(1, S // C):
                    link(ts_(small(7), rank, c * C - 0.5, float(C), ALU.is_gt, ALU.mult))
                    link(tt_(small(6), small(6), small(7), ALU.add))
                pairs = small(6).rearrange("p (t i e) -> p t i e", t=NT, e=2)
                link(ts_(pairs[:, :, :, 1], pairs[:, :, :, 1], float(C), None, ALU.add))
                for e in range(2):
                    ins = stt(pairs[:, :, :, e], base.unsqueeze(1).to_broadcast([P, NT, NE // 2]), float(P),
                              pairs[:, :, :, e], ALU.mult, ALU.add)
                link(ins)
                for r in range(2):
                    link(tt_(small(7), small(3 + r), small(6), ALU.mult))
                    dve.tensor_reduce(tok4[:, :, r], v3(7), AX.X, ALU.add).then_inc(m["slots_ready"], 1)
                    dve.wait_ge(m["slots_ready"], 2 * l + r + 1)
                dve.memset(spread, 0.0).then_inc(m["spread_ready"], 1)
                dve.memset(ymoe[:, 0:W], 0.0).then_inc(m["y0_ready"], 1)
                dve.memset(ymoe[:, W:D], 0.0).then_inc(m["y1_ready"], 1)
                link(dve.tensor_copy(pcol[:], pcol0[:]))

                def pick_step(wait_for):
                    for tt in range(NT):
                        ts_(pick2[:, tt, :], iota[:], tok4[:, tt, 1:2], None, ALU.is_equal)
                        ins = ts_(pick[:, tt, :], iota[:], tok4[:, tt, 0:1], None, ALU.is_equal)
                    wait_for(ins)
                    return tt_(pick, pick, pick2, ALU.add)

                def take_b():
                    dve.tensor_copy(hgT[:, 4:8, :].rearrange("p k c -> p (k c)"), bank[7][:]).then_inc(m["hgb_ready"], 1)

                pick_step(link).then_inc(m["pick_ready"], 1)
                dve.wait_ge(m["slot_full"], l + 1)
                link(ts_(tok4[:, :, 0:2], tok4[:, :, 0:2], -float(P), None, ALU.add))
                dve.wait_ge(m["rows_ready"], l + 1)
                dve.wait_ge(m["tab_ready"], l + 1)
                total = dve.value_load(tab_i[0:1, NE:NE + 1], min_val=NE // 2, max_val=NE)
                dve.wait_ge(m["gath_full"], 1)
                take_b()
                pick_step(link).then_inc(m["pick_ready"], 1)
                link(ts_(tok4[:, :, 0:2], tok4[:, :, 0:2], -float(P), None, ALU.add))
                steps = 4
                with dve.Fori(0, total) as g:
                    def after(ins, n):
                        ins.then_inc(m["chain"], 1)
                        dve.wait_ge(m["chain"], g * steps + (n + 1))

                    dve.wait_ge(m["silu_done"], g + 1)
                    dve.wait_ge(m["w3_done"], g + 1)
                    tt_(hid, hsil, bank[5][:], ALU.mult).then_inc(m["hid_ready"], 1)
                    dve.wait_ge(m["gath_full"], g + 2)
                    take_b()
                    pick_step(lambda ins: after(ins, 0)).then_inc(m["pick_ready"], 1)
                    after(ts_(tok4[:, :, 0:2], tok4[:, :, 0:2], -float(P), None, ALU.add), 1)
                    stt(spread2, rows4[:, 1, :], pcol[:], rows4[:, 3, :], ALU.is_equal, ALU.mult)
                    dve.wait_ge(m["scat_done"], g + 2)
                    after(stt(spread, rows4[:, 0, :], pcol[:], rows4[:, 2, :], ALU.is_equal, ALU.mult), 2)
                    tt_(spread, spread, spread2, ALU.add).then_inc(m["spread_ready"], 1)
                    after(ts_(pcol[:], pcol[:], float(P), None, ALU.add), 3)
                    dve.wait_ge(m["down_half"], g * 2 + 2)
                    dve.tensor_copy(ymoe[:, W:D], bank[6][:]).then_inc(m["y1_ready"], 1)
                dve.wait_ge(m["scat_done"], total + 2)
                residual(k)

            if NSUB >= 2:
                moe(0, 1)
            if NSUB >= 3:
                norm(2)
                def mix_used(n):
                    return (lora_full, n + 1) if n < 3 else (proj_full, FULL_LORA + 4 * (n - 3) + 4)

                dve.wait_ge(h_ready, 3)
                tt_(xx[:, :, 1:S], hT[:, :, 0:S - 1], hT[:, :, 1:S], ALU.subtract)
                link(ts_(xx[:, :, 0:1], hT[:, :, 0:1], -1.0, None, ALU.mult))
                for n, i in enumerate((3, 4, 5, 1, 0, 2)):
                    if n >= 2:
                        dve.wait_ge(*mix_used(n - 2))
                    for b in range(KB):
                        ins = stt(mixed[n % 2][:, b, :], xx[:, b, :], col("od_mu", i * KB + b), hT[:, b, :],
                                  ALU.mult, ALU.add)
                    ins.then_inc(mix_ready, 1)
                    if n == 3:
                        dve.wait_ge(proj_evac, 26 + 4)
                        dve.memset(cum[:, :, 0:1], 0.0)
                        for b in range(KB):
                            ins = dve.tensor_tensor_scan(cum[:, b, 1:], ones[:, 0:S], sgT[:, b, :], 0.0,
                                                         ALU.mult, ALU.add)
                        ins.then_inc(cum_ready, 1)
                dve.wait_ge(proj_evac, 26 + 12 + 4)
                for b in range(KB):
                    ins = ts_(kkT[:, b, :], k1T[:, b, :], col("od_k_k", b), None, ALU.mult)
                link(ins)
                dve.wait_ge(*mix_used(5))
                tt_(mixed[0][:, :, :], kkT[:, :, :], kkT[:, :, :], ALU.mult).then_inc(kk_sq, 1)
                dve.wait_ge(head_sum, 3)
                for b in range(KB):
                    ins = ts_(mixed[0][:, b, :], aT[:, b, :], -1.0, col("od_k_a", b), ALU.add, ALU.mult)
                link(ins)
                for b in range(KB):
                    ins = stt(k1T[:, b, :], mixed[0][:, b, :], 1.0, k1T[:, b, :], ALU.add, ALU.mult)
                link(ins)
                dve.wait_ge(proj_evac, 26 + 12 + 8)
                for b in range(KB):
                    ins = stt(mixed[1][:, b, :], rT[:, b, :], col("od_r_k", b), k1T[:, b, :], ALU.mult, ALU.mult)
                ins.then_inc(rk_ready, 1)
                dve.wait_ge(head_root, 3)
                link(ts_(rs_root[:], rs_root[:], 1e-12, None, ALU.max))
                dve.reciprocal(rstd[:], rs_root[:]).then_inc(head_rstd, 1)
                for u in range(4):
                    dve.wait_ge(head_bcast, u + 5)
                    v = kkT[:, 2 * u:2 * u + 2, :].rearrange("p k s -> p (k s)")
                    tt_(v, v, bank[6 + u % 2][:], ALU.mult).then_inc(bcast_used, 1)
                dve.wait_ge(head_sum, 4)
                dve.tensor_copy(beta[:], bank[5][:, 0:2 * NH])
                dve.wait_ge(cum_ready, 1)
                for tt in range(NT):
                    mid = cum[:, :, tt * P + MID:tt * P + MID + 1].to_broadcast([P, KB, P])
                    ins = tt_(by_tile(4)[:, :, tt, :], cum[:, :, 1 + tt * P:1 + (tt + 1) * P], mid, ALU.subtract)
                ins.then_inc(rw_diff, 1)
                for tt in range(NT):
                    mid = cum[:, :, tt * P + MID:tt * P + MID + 1].to_broadcast([P, KB, P])
                    ins = tt_(by_tile(10)[:, :, tt, :], cum[:, :, tt * P:(tt + 1) * P], mid, ALU.subtract)
                ins.then_inc(rw_diff, 1)
                tt_(kmid[:], cum[:, :, MID], cum[:, :, P + MID], ALU.subtract).then_inc(kmid_diff, 1)
                dve.wait_ge(bcast_used, 8)
                link(tt_(buf(8), buf(8), buf(11), ALU.mult))
                dve.wait_ge(rw_exp, 1)
                tt_(AR[:, :, :, 1, :], by_tile(5), by_tile(3), ALU.mult).then_inc(rw_ops, 1)
                dve.wait_ge(rw_exp, 2)
                tt_(AR[:, :, :, 0, :], by_tile(11), by_tile(10), ALU.mult).then_inc(rw_ops, 1)
                dve.wait_ge(rw_exp, 3)
                tt_(buf(8), buf(8), buf(4), ALU.mult).then_inc(rw_ops, 1)
                tt_(buf(6), buf(6), buf(4), ALU.mult).then_inc(rw_ops, 1)
                dve.wait_ge(rw_ops, 4)
                dve.wait_ge(kmid_ready, 1)

                def u4(x):
                    return x.rearrange("p (u s) -> p u s", s=P)

                def take_scores(pr):
                    n = 6 * pr
                    for which, keys in ((0, rwK), (1, rwB)):
                        ins = ts_(kcross(pr, which), keys[:, pr, 0, :], kmid[:, pr:pr + 1], None, ALU.mult)
                    ins.then_inc(kc_ready, 1)
                    for kind in range(2):
                        for hh in range(2):
                            dve.wait_ge(rsc_full, n + 2 * kind + hh + 1)
                            ps = bank[hh][:].rearrange("p (t a s) -> p t a s", t=2, a=2)
                            to_a, to_r = (part(pr, (2 * kind + a) * 4, 4).rearrange(
                                "p (t h s) -> p t h s", t=2, h=2)[:, :, hh, :] for a in range(2))
                            two = lambda mask: mask[:].unsqueeze(1).to_broadcast([P, 2, P])
                            ins = stt(to_a, ps[:, :, 0, :], -1.0 if kind else 1.0, two(strict), ALU.mult, ALU.mult)
                            if kind and hh:
                                ins.then_inc(lt_ready, 1)
                            tt_(to_r, ps[:, :, 1, :], two(causal), ALU.mult).then_inc(rsc_evac, 1)
                    dve.wait_ge(lt_ready, pr + 1)
                    link(tt_(u4(xinvT(pr)), u4(part(pr, 8, 4)), level[:, 0:1, :].to_broadcast([P, 4, P]), ALU.mult))
                    tt_(u4(xinvT(pr)), u4(xinvT(pr)), ident[:].unsqueeze(1).to_broadcast([P, 4, P]),
                        ALU.add).then_inc(xt1_ready, 1)
                    for hh in range(2):
                        dve.wait_ge(rsc_full, n + 4 + hh + 1)
                        dve.tensor_copy(part(pr, 16, 8).rearrange("p (q h s) -> p q h s", q=4, h=2)[:, :, hh, :],
                                        u4(bank[hh][:])).then_inc(rsc_evac, 1)

                for jj in range(KB // 2):
                    prs = (2 * jj, 2 * jj + 1)
                    for pr in prs:
                        take_scores(pr)
                    for pr in prs:
                        dve.wait_ge(x1_full, pr + 1)
                        dve.tensor_copy(xinv(pr), bank[4 + 2 * (pr % 2)][:]).then_inc(x1_ready, 1)
                    for i in range(1, 7):
                        for pr in prs:
                            n = jj * 12 + 2 * (i - 1) + pr % 2
                            dve.wait_ge(xm_full, n + 1)
                            if i == 1:
                                dve.wait_ge(x1_ready, pr + 1)
                                dve.wait_ge(xt1_ready, pr + 1)
                            else:
                                dve.wait_ge(xm_ready, n - 1)
                            if i < 6:
                                tt_(xinv(pr), xinv(pr), bank[4 + 2 * (pr % 2)][:], ALU.add)
                            tt_(xinvT(pr), xinvT(pr), bank[5 + 2 * (pr % 2)][:], ALU.add).then_inc(xm_ready, 1)
                    for pr in prs:
                        dve.wait_ge(ry_full, pr + 1)
                        dve.tensor_copy(oR[:, pr, :, :], bank[4 + 2 * (pr % 2)][:, 0:S].rearrange(
                            "p (t s) -> p t s", t=NT)).then_inc(ry_ready, 1)

                dve.wait_ge(ry_ready, KB)
                tt_(bvN, vN1, beta[:].rearrange("p (t h) -> p t h", t=NT).unsqueeze(3).to_broadcast(
                    [P, NT, NH, HEAD]), ALU.mult).then_inc(bv_ready, 1)
                dve.wait_ge(head_sum, 5)
                ts_(gm_mean[:], bank[4][:, 0:2 * NH], 1.0 / HEAD, None, ALU.mult).then_inc(gn_mean, 1)
                four = lambda x: x.rearrange("p (k t s) -> p k t s", k=2, t=NT)
                for u in range(4):
                    dve.wait_ge(head_bcast, u + 9)
                    v = oR[:, 2 * u:2 * u + 2, :, :]
                    tt_(v, v, four(bank[6 + u % 2][:]), ALU.subtract).then_inc(bcast_used, 1)
                dve.wait_ge(head_root, 4)
                dve.reciprocal(rstd[:], rs_root[:]).then_inc(head_rstd, 1)
                for u in range(4):
                    dve.wait_ge(head_bcast, u + 13)
                    v = oR[:, 2 * u:2 * u + 2, :, :]
                    tt_(v, v, four(bank[6 + u % 2][:]), ALU.mult).then_inc(bcast_used, 1)
                dve.wait_ge(bcast_used, 16)
                og = by_tile(4)
                for b in range(KB):
                    ins = ts_(og[:, b, :, :], oR[:, b, :, :], col("od_ln_w", b), col("od_ln_b", b), ALU.mult, ALU.add)
                link(ins)
                dve.wait_ge(bvT_full, 1)
                for b in range(0, KB, 2):
                    v = blocks(4)[:, b:b + 2, :].rearrange("p k s -> p (k s)")
                    ins = tt_(v, v, bank[b // 2][:], ALU.add)
                link(ins)
                tt_(buf(4), buf(4), buf(9), ALU.mult).then_inc(og_ready, 1)
                dve.wait_ge(tile_used, USED[1])
                residual(2)
            if NSUB >= 4:
                moe(1, 3)
            norm(NSUB)


INPUTS = ["x", "c", "mod_w", "mod_b", "norm_w", "hg_lb_logits", "ev_w_in", "ev_hg_norm", "ev_conv_w", "ev_conv_b",
          "ev_dt_bias", "ev_a_log", "ev_d_skip", "ev_ssm_norm", "ev_w_out", "od_mu", "od_w_rkv", "od_w_dec0",
          "od_w_dec1", "od_w_dec2", "od_a0", "od_a1", "od_a2", "od_g1", "od_g2", "od_k_k", "od_k_a", "od_r_k",
          "od_ln_w", "od_ln_b", "od_w_o", "router_w", "router_b", "moe_w1", "moe_w3", "moe_w2", "final_norm_w"]


def kernel(**inputs):
    import numpy as np
    import concourse.bacc as bacc
    from concourse.bass_utils import run_bass_kernel_spmd as run

    nc = bacc.Bacc("TRN2", target_bir_lowering=False, num_devices=1, dynamic_dma_scratch_size=1024)
    arrays, args = {}, {}
    for name in INPUTS:
        a = np.ascontiguousarray(inputs[name])
        arrays[f"in_{name}"] = a
        args[name] = nc.dram_tensor(f"in_{name}", a.shape, mybir.dt.from_np(a.dtype), kind="ExternalInput").ap()
    out = nc.dram_tensor("out_0", (1, S, D), F32, kind="ExternalOutput").ap()
    trunk(nc, args, out)
    r = run(nc, [arrays], core_ids=[0])
    return r.results[0]["out_0"]
```

```python
from contextlib import ExitStack

import concourse.bass as bass
from concourse import mybir

F32 = mybir.dt.float32
I32 = mybir.dt.int32
ALU = mybir.AluOpType
ACT = mybir.ActivationFunctionType
AX = mybir.AxisListType

P = 128
D = 1024
S = 256
KB = D // P
NT = S // P
LAYERS = 2
EPS = 1e-6
GN_EPS = 64e-5
HEAD = 64
NH = D // HEAD
GROUPS = 2
TAPS = 4
XBC = D + 2 * GROUPS * P
XBLK = XBC // P
IN_COLS = 4 * D + D + XBC + NH
NE = 16
FF = D // 2
FB = FF // P
MID = P // 2
C = 64
SLOTS = 6
BORROWED = (0, 1, 2)
TILE = 4096
W = 512
E05 = 0.6065306597126334
HALVES = [1, 2, 4, 8, 16, 32, 64]
MOD_FIRST = 4
NSUB = 4


def layout_vectors():
    groups = [
        [("mod_b", 96), ("norm_w", 32)],
        [("c", 8), ("final_norm_w", 8), ("hg_lb_logits", 24), ("ev_hg_norm", 8), ("ev_conv_w", 48),
         ("ev_conv_b", 12), ("ev_ssm_norm", 8)],
        [("od_mu", 48), ("od_w_dec0", 8), ("od_a0", 8), ("od_k_k", 8), ("od_k_a", 8), ("od_r_k", 8),
         ("od_ln_w", 8), ("od_ln_b", 8)],
    ]
    at = {}
    for g, rows in enumerate(groups):
        r = 0
        for name, n in rows:
            at[name] = (g, r, n)
            r += n
    return at


VEC = layout_vectors()


def weight_tiles():
    first = [("mod", 0, j) for j in range(MOD_FIRST)]
    for n, j in enumerate((2, 3, 0, 1, 4, 5, 12, 10, 11, 8, 9, 6, 7)):
        first.append(("in", 0, j))
        if MOD_FIRST + n < 12:
            first.append(("mod", 0, MOD_FIRST + n))
    first += [("mod", 1, j) for j in range(12)]
    first += [("out", 0, j) for j in range(4)]
    second = [("la", 0, 0), ("lb", 0, 0)]
    second += [("rkv", i, j) for i in (1, 0, 2) for j in range(2)]
    second += [("wo", 0, j) for j in range(2)]
    return [first, second]


def trunk(nc, t, out):
    tiles = weight_tiles()

    landed = [0] * SLOTS
    plan = []
    moe_base = []
    n_dma = {"la": 3, "lb": 3}
    for stage in tiles:
        rows = []
        for n, tile in enumerate(stage):
            slot = n % SLOTS
            landed[slot] += n_dma.get(tile[0], 1)
            rows.append((tile, slot, landed[slot]))
        plan.append(rows)
        moe_base.append(list(landed))
        landed = [x + NE // 2 - (slot in BORROWED) for slot, x in enumerate(landed)]

    places = {(s, kind): [n for n, row in enumerate(rows) if row[0][0] == kind]
              for s, rows in enumerate(plan) for kind in {row[0][0] for row in rows}}

    FULL_IN = 2 * 13
    FULL_LORA = FULL_IN + 12
    USED = [4, 6]

    with ExitStack() as ctx:
        def sb(name, shape, dt=F32):
            return ctx.enter_context(nc.sbuf_tensor(name, shape, dt))

        def sem(name):
            return ctx.enter_context(nc.semaphore(name))

        ctx.enter_context(nc.allow_non_contiguous_dma(reason="a few small vectors"))

        bank = [ctx.enter_context(nc.psum_tensor(f"bank{i}", [P, W], F32)) for i in range(8)]

        ring = sb("ring", [P, SLOTS * TILE])
        BUF = KB * S
        XPAD = XBLK * (S + TAPS - 1)
        arena = sb("arena", [P, 12 * BUF + XPAD])

        def buf(i, n=1):
            return arena[:, i * BUF:(i + n) * BUF]

        def blocks(i):
            return buf(i).rearrange("p (k s) -> p k s", k=KB)

        def by_tile(i):
            return buf(i).rearrange("p (k t s) -> p k t s", k=KB, t=NT)

        xpad = arena[:, 12 * BUF:12 * BUF + XPAD].rearrange("p (k s) -> p k s", k=XBLK)

        xT = blocks(0)
        hT = blocks(1)
        xN = buf(8).rearrange("p (t d) -> p t d", t=NT)
        squares = blocks(6)

        ident = sb("ident", [P, P])
        ones = sb("ones", [P, S])
        thirty2 = sb("thirty2", [P, 1])
        halves = sb("halves", [P, 2])
        causal = sb("causal", [P, P])
        strict = sb("strict", [P, P])
        tri = buf(7)[:, 0:6 * P].rearrange("p (i s) -> p i s", i=6)
        level = sb("level", [P, 7, P])
        iota = sb("iota", [P, P])
        pcol0 = sb("pcol0", [P, 1])
        tie4 = sb("tie4", [P, 4])

        vrows = buf(9)[:, 0:3 * P].rearrange("p (g r) -> p g r", g=3)
        vcols = sb("vcols", [P, 3, P])

        def col(name, i):
            g, r, n = VEC[name]
            assert i < n
            return vcols[:, g, r + i:r + i + 1]

        def cols(name, a, b):
            g, r, n = VEC[name]
            return vcols[:, g, r + a:r + b]

        modT = sb("modT", [P, LAYERS, 48])
        gain = sb("gain", [P, LAYERS, 2, KB])
        csilu = sb("csilu", [P, KB])
        rs_root = sb("rs_root", [P, 2 * NH])
        rstd = sb("rstd", [P, 2 * NH])
        gm_mean = sb("gm_mean", [P, 2 * NH])
        beta = sb("beta", [P, 2 * NH])
        lb = sb("lb", [P, KB])
        oml = sb("oml", [P, KB])
        lbe = sb("lbe", [P, 3, KB])
        lbm = sb("lbm", [P, KB])
        dt_bias = sb("dt_bias", [NH, 1])
        a_log = sb("a_log", [NH, 1])
        a_neg = sb("a_neg", [NH, 1])
        dskip = sb("dskip", [P, KB])
        w_dt = sb("w_dt", [P, KB, NH])
        router_w = sb("router_w", [P, KB, NE])
        router_b = sb("router_b", [P, NE])
        eps_col = sb("eps_col", [P, 2])

        tile_landed = [sem(f"tile_landed{i}") for i in range(SLOTS)]
        tile_used = sem("tile_used")
        ahead_landed = sem("ahead_landed")
        vec_landed = sem("vec_landed")
        x_landed = sem("x_landed")
        small_landed = sem("small_landed")
        vrows_zeroed = sem("vrows_zeroed")
        basics = sem("basics")
        consts = sem("consts")
        stored = sem("stored")
        pool_chain = sem("pool_chain")
        dve_chain = sem("dve_chain")
        act_chain = sem("act_chain")

        def weight(slot):
            if slot < SLOTS:
                return ring[:, slot * TILE:(slot + 1) * TILE]
            return arena[:, 7 * BUF + (slot - SLOTS) * TILE:7 * BUF + (slot - SLOTS + 1) * TILE]

        w_cols = lambda slot: weight(slot).rearrange("p (k n) -> p k n", k=KB)
        w_rows = lambda slot: weight(slot).rearrange("p (k n) -> p k n", k=4)
        row_block = lambda ap: ap.rearrange("(k p) n -> p k n", p=P)

        vec_T = sem("vec_T")
        vec_cols = sem("vec_cols")
        xT_psum = sem("xT_psum")
        xT_evac = sem("xT_evac")
        csilu_ready = sem("csilu_ready")
        mod_full = sem("mod_full")
        mod_row = sem("mod_row")
        mod_cols = sem("mod_cols")
        mod_taken = sem("mod_taken")
        x_ready = sem("x_ready")
        sq_ready = sem("sq_ready")
        parts_full = sem("parts_full")
        parts_evac = sem("parts_evac")
        total_full = sem("total_full")
        root_ready = sem("root_ready")
        scaled = sem("scaled")
        h_ready = sem("h_ready")
        proj_full = sem("proj_full")
        proj_evac = sem("proj_evac")
        lb_max = sem("lb_max")
        start_exp = sem("start_exp")
        logf_ready = sem("logf_ready")
        k_ready = sem("k_ready")
        b_ready = sem("b_ready")
        dl_ready = sem("dl_ready")
        dr_ready = sem("dr_ready")
        el_exp = sem("el_exp")
        ek_ready = sem("ek_ready")
        eq_ready = sem("eq_ready")
        score_full = sem("score_full")
        score_evac = sem("score_evac")
        o_full = sem("o_full")
        o_evac = sem("o_evac")
        head_sum = sem("head_sum")
        head_root = sem("head_root")
        head_rstd = sem("head_rstd")
        head_bcast = sem("head_bcast")
        bcast_used = sem("bcast_used")
        oa_ready = sem("oa_ready")
        silu_g = sem("silu_g")
        dt_full = sem("dt_full")
        dtz = sem("dtz")
        dtabs = sem("dtabs")
        dtln = sem("dtln")
        dt_ready = sem("dt_ready")
        dtN_full = sem("dtN_full")
        dtN_ready = sem("dtN_ready")
        conv_done = sem("conv_done")
        conv_silu = sem("conv_silu")
        xs_full = sem("xs_full")
        xdt_ready = sem("xdt_ready")
        cb_full = sem("cb_full")
        cb_ready = sem("cb_ready")
        row_full = sem("row_full")
        dec_diff = sem("dec_diff")
        dec_exp = sem("dec_exp")
        dec_mat = sem("dec_mat")
        y_full = sem("y_full")
        y_ready = sem("y_ready")
        yb_full = sem("yb_full")
        ob_ready = sem("ob_ready")
        mix_ready = sem("mix_ready")
        lora_full = sem("lora_full")
        lora_evac = sem("lora_evac")
        cum_ready = sem("cum_ready")
        sums_in = sem("sums_in")
        rw_diff = sem("rw_diff")
        rw_exp = sem("rw_exp")
        rw_ops = sem("rw_ops")
        kc_ready = sem("kc_ready")
        rsc_full = sem("rsc_full")
        rsc_evac = sem("rsc_evac")
        lt_ready = sem("lt_ready")
        xt1_ready = sem("xt1_ready")
        x1_full = sem("x1_full")
        x1_ready = sem("x1_ready")
        lm_ready = sem("lm_ready")
        tm_full = sem("tm_full")
        tm_ready = sem("tm_ready")
        xm_full = sem("xm_full")
        xm_ready = sem("xm_ready")
        w_full = sem("w_full")
        w_ready = sem("w_ready")
        u_full = sem("u_full")
        u_ready = sem("u_ready")
        ry_full = sem("ry_full")
        ry_ready = sem("ry_ready")
        gn_mean = sem("gn_mean")
        squares_ready = sem("squares_ready")
        hrow_full = sem("hrow_full")
        hrow_evac = sem("hrow_evac")
        xi_full = sem("xi_full")
        xi_ready = sem("xi_ready")
        bv_ready = sem("bv_ready")
        bvT_full = sem("bvT_full")
        og_ready = sem("og_ready")
        shared = {n: sem(f"moe_{n}") for n in ("logit_full", "lmax", "lexp", "sel_ready", "rank_full", "tab_ready",
                                               "slots_ready", "slot_full", "rows_ready", "hN_full", "hN_evac")}
        moe_names = ["pick_ready", "gath_full", "hga_ready", "hgb_ready", "w1_done", "w3_done", "silu_done", "hid_ready",
                     "hidT_full", "hidT_ready", "down_half", "y0_ready", "y1_ready", "spread_ready", "scat_done",
                     "chain"]
        M = [dict(shared, **{n: sem(f"m{l}_{n}") for n in moe_names}) for l in range(LAYERS)]

        mod_rows = [buf(i)[:, 0:2 * W].rearrange("p (u n) -> p u n", u=2) for i in (10, 1)]

        qT, kT, bT, zT, gT = blocks(2), blocks(4), blocks(5), blocks(11), blocks(10)
        fT = blocks(3)
        eT = [3, 7]
        vN = buf(6).rearrange("p (t d) -> p t d", t=NT)
        scd = buf(8).rearrange("p (t h s) -> p t h s", t=NT, h=KB)
        scx = buf(9)[:, 0:KB * P].rearrange("p (h s) -> p h s", h=KB)
        oa = blocks(2)
        cbm = buf(9)[:, KB * P:KB * P + 6 * P].rearrange("p (g n) -> p g n", g=GROUPS)
        xdt = buf(4).rearrange("p (t d) -> p t d", t=NT)
        NDEC = 5
        dec = buf(7)[:, 0:NDEC * 3 * P].rearrange("p (r n) -> p r n", r=NDEC)
        yT = blocks(5)
        scratch = sb("scratch", [P, 7 * S])
        norm_parts, norm_rstd = scratch[:, 0:S], scratch[:, S:2 * S]
        kmid = sb("kmid", [P, KB])
        ctmp = scratch[:, 0:2 * S].rearrange("p (u s) -> p u s", u=2)
        dts = scratch[0:NH, 2 * S:7 * S].rearrange("p (u s) -> p u s", u=5)
        dtN = sb("dtN", [P, 2, NT, NH])

        xx = blocks(2)
        mixed = [blocks(3), blocks(4)]
        rT, kkT, aT, ggT = blocks(5), blocks(11), blocks(8), blocks(9)
        k1T = blocks(6)
        vN1 = buf(7).rearrange("p (t h n) -> p t h n", t=NT, h=NH)
        sgT = blocks(10)
        cum = arena[:, 12 * BUF:12 * BUF + KB * (S + 1)].rearrange("p (k s) -> p k s", k=KB)
        AR = buf(1, 2).rearrange("p (k t a s) -> p k t a s", k=KB, t=NT, a=2)
        rwB, rwK = by_tile(8), by_tile(6)
        oR = AR[:, :, :, 0, :]
        hrows = scratch[0:NH, 3 * S:4 * S]
        lora = [scratch[:, i * S:(i + 1) * S] for i in range(3)]
        bvN = buf(5).rearrange("p (t h n) -> p t h n", t=NT, h=NH)
        pslot = [ring[:, 4 * TILE:4 * TILE + 48 * P], ring[:, 0:48 * P],
                 arena[:, 3 * BUF:3 * BUF + 48 * P], arena[:, 10 * BUF:10 * BUF + 48 * P]]

        def part(pr, off, n):
            return pslot[pr % 4][:, off * P:(off + n) * P]

        def sc(pr, kind, tt, hh):
            return part(pr, kind * 4 + tt * 2 + hh, 1)

        def scro(pr, kind, hh):
            return part(pr, 16 + kind * 2 + hh, 1)

        def kcross(pr, which):
            return part(pr, 24 + which, 1)

        def xinv(pr):
            return part(pr, 26, 4)

        def xinvT(pr):
            return part(pr, 30, 4)

        def tmid(pr):
            return part(pr, 34, 4)

        def lmask(pr, i):
            return part(pr, 38 + 4 * (i % 2), 4)

        def uneg(pr, tt):
            return part(pr, 46 + tt, 1)

        def xi(jj, i, pr):
            return jj * 10 + 2 * (i - 1) + pr % 2

        assert 48 * P <= 3 * BUF and 10 * BUF + 48 * P <= 12 * BUF + XPAD

        hN = buf(2).rearrange("p (t d) -> p t d", t=NT)
        m3 = buf(3)
        pick = m3[:, 0:2 * P].rearrange("p (t c) -> p t c", t=NT)
        pick2 = m3[:, 2 * P:4 * P].rearrange("p (t c) -> p t c", t=NT)
        spread = m3[:, 4 * P:6 * P]
        spread2 = m3[:, 6 * P:8 * P]
        hid = m3[:, 8 * P:12 * P]
        hsil = m3[:, 12 * P:16 * P]
        ymoe = buf(4)[:, 0:D]
        rows4 = buf(4)[:, D:D + 4 * S].rearrange("p (r s) -> p r s", r=4)
        hgT = buf(6)[:, 0:KB * P].rearrange("p (k c) -> p k c", k=KB)
        hidT = buf(6)[:, KB * P:KB * P + FB * P].rearrange("p (f c) -> p f c", f=FB)
        rt = buf(5)

        def small(i, n=1):
            return rt[:, i * 32:(i + n) * 32]

        tok4 = sb("tok4", [P, NT, 4])
        pcol = sb("pcol", [P, 1])
        tab_f = sb("tab_f", [P, 64])
        tab_i = sb("tab_i", [1, 64], I32)

        block = ctx.enter_context(nc.Block())

        @block.sync
        def _(sp):
            def load(tile, slot):
                kind, l, j = tile
                if kind == "mod":
                    srcs = [(w_cols(slot), row_block(t["mod_w"][l])[:, :, j * W:(j + 1) * W])]
                elif kind == "in":
                    srcs = [(w_cols(slot), row_block(t["ev_w_in"][0])[:, :, j * W:(j + 1) * W])]
                elif kind == "out":
                    srcs = [(w_rows(slot), row_block(t["ev_w_out"][0])[:, 4 * j:4 * j + 4, :])]
                elif kind == "rkv":
                    srcs = [(w_cols(slot), row_block(t["od_w_rkv"][0, l])[:, :, j * W:(j + 1) * W])]
                elif kind == "wo":
                    srcs = [(w_rows(slot), row_block(t["od_w_o"][0])[:, 4 * j:4 * j + 4, :])]
                elif kind == "la":
                    wt = weight(slot)
                    srcs = [(wt[:, 0:512].rearrange("p (k n) -> p k n", k=KB), row_block(t["od_w_dec1"][0])),
                            (wt[:, 512:1024].rearrange("p (k n) -> p k n", k=KB), row_block(t["od_a1"][0])),
                            (wt[:, 1024:2048].rearrange("p (k n) -> p k n", k=KB), row_block(t["od_g1"][0]))]
                elif kind == "lb":
                    wt = weight(slot)
                    srcs = [(wt[0:64, 0:D], t["od_w_dec2"][0]), (wt[0:64, D:2 * D], t["od_a2"][0]),
                            (wt[:, 2 * D:3 * D], t["od_g2"][0])]
                for dst, src in srcs:
                    sp.dma_start(dst, src).then_inc(tile_landed[slot], 16)

            def wait_used(l, n):
                kind, l_mod, j = plan[l][n][0]
                at = places[l, kind].index(n)
                if kind == "mod":
                    sp.wait_ge(mod_full, 12 * l_mod + j + 1)
                elif kind == "in":
                    sp.wait_ge(proj_full, 2 * at + 2)
                elif kind in ("out", "wo"):
                    sp.wait_ge(tile_used, (USED[0] if l else 0) + at + 1)
                elif kind == "la":
                    sp.wait_ge(lora_full, 3)
                elif kind == "lb":
                    sp.wait_ge(proj_full, FULL_LORA)
                elif kind == "rkv":
                    sp.wait_ge(proj_full, FULL_LORA + 2 * at + 2)

            for l in range((NSUB + 1) // 2):
                base = M[l]
                for n, (tile, slot, _) in enumerate(plan[l]):
                    if n >= SLOTS:
                        wait_used(l, n - SLOTS)
                    elif l == 0 and n == 1:
                        sp.wait_ge(vec_landed, 16 * len(VEC))
                    elif l > 0 and n == 0:
                        g_end = sp.value_load(tab_i[0:1, NE:NE + 1], min_val=NE // 2, max_val=NE)
                        sp.wait_ge(M[l - 1]["w1_done"], g_end)
                    elif l > 0 and n == 2:
                        sp.wait_ge(M[l - 1]["w3_done"], g_end)
                    elif l > 0 and n == 4:
                        sp.wait_ge(M[l - 1]["down_half"], g_end * 2)
                    load(tile, slot)
                n_stage = len(plan[l])
                if NSUB < 2 * l + 2:
                    break
                names = ("moe_w1", "moe_w3", "moe_w2")

                def expert(pair, place, slot, signal):
                    kind, e = place // 2, place % 2
                    sp.dma_start((w_rows if kind == 2 else w_cols)(slot),
                                 row_block(t[names[kind]][l, 2 * pair + e])).then_inc(signal, 16)

                last = [max(n for n in range(n_stage) if n % SLOTS == slot) for slot in range(SLOTS)]
                first_out = places[l, "wo" if l else "out"][0]
                order = sorted(range(SLOTS), key=lambda slot: last[slot])
                for slot in [x for x in order if last[x] < first_out]:
                    wait_used(l, last[slot])
                    if l:
                        sp.wait_ge(ry_full, 6)
                    expert(0, slot, slot, tile_landed[slot])
                sp.wait_ge(og_ready if l else ob_ready, 1)
                for place in BORROWED:
                    expert(1, place, SLOTS + place, ahead_landed)
                for slot in [x for x in order if last[x] >= first_out]:
                    wait_used(l, last[slot])
                    expert(0, slot, slot, tile_landed[slot])
                sp.wait_ge(base["tab_ready"], l + 1)
                done = sp.value_load(tab_i[0:1, NE // 2 + 1:NE // 2 + 2], min_val=1, max_val=NE)
                sp.wait_ge(base["w1_done"], done)
                expert(2, 0, 0, tile_landed[0])
                sp.wait_ge(base["w3_done"], done)
                expert(1, 3, 3, tile_landed[3])
                expert(2, 1, 1, tile_landed[1])
                sp.wait_ge(base["down_half"], done * 2)
                expert(1, 4, 4, tile_landed[4])
                expert(1, 5, 5, tile_landed[5])
                expert(2, 2, 2, tile_landed[2])
                done = sp.value_load(tab_i[0:1, NE // 2 + 2:NE // 2 + 3], min_val=1, max_val=NE)
                sp.wait_ge(base["w3_done"], done)
                expert(2, 3, 3, tile_landed[3])
                sp.wait_ge(base["down_half"], done * 2)
                expert(2, 4, 4, tile_landed[4])
                expert(2, 5, 5, tile_landed[5])
                views = [t[name][l].rearrange("e (k p) n -> p e k n", p=P) for name in names]
                with sp.Fori(3, NE // 2) as i:
                    done = sp.value_load(tab_i[0:1, bass.ds(i + NE // 2, 1)], min_val=1, max_val=NE)
                    for slot in range(SLOTS):
                        kind, e = slot // 2, slot % 2
                        if kind == 0 and e == 0:
                            sp.wait_ge(base["w1_done"], done)
                        elif kind == 1 and e == 0:
                            sp.wait_ge(base["w3_done"], done)
                        elif kind == 2 and e == 0:
                            sp.wait_ge(base["down_half"], done * 2)
                        sp.dma_start((w_rows if kind == 2 else w_cols)(slot), views[kind][:, bass.ds(2 * i + e, 1)]
                                     .rearrange("p e k n -> p (e k) n")).then_inc(tile_landed[slot], 16)
            for tt in range(NT):
                sp.wait_ge(o_evac, 4 + 7 + tt)
                sp.dma_start(out[0, tt * P:(tt + 1) * P, :], hN[:, tt, :]).then_inc(stored, 16)
            sp.wait_ge(stored, 16 * NT)

        @block.gpsimd
        def _(pool):
            count = [0]

            def link(ins):
                count[0] += 1
                ins.then_inc(pool_chain, 1)
                pool.wait_ge(pool_chain, count[0])

            link(pool.memset(ident[:], 0.0))
            link(pool.affine_select(out=ident[:], in_=ident[:], compare_op=ALU.not_equal, fill=1.0, base=0,
                                    pattern=[[-1, P]], channel_multiplier=1))
            pool.memset(ones[:], 1.0)
            pool.memset(thirty2[:], 1.0 / 32)
            link(pool.memset(halves[:], 0.0))
            for hh in range(2):
                link(pool.memset(halves[hh * HEAD:(hh + 1) * HEAD, hh:hh + 1], 1.0))
            pool.iota(iota[:], pattern=[[1, P]], base=0, channel_multiplier=0, allow_small_or_imprecise_dtypes=True)
            pool.iota(tie4[:], pattern=[[1, 4]], base=0, channel_multiplier=0, allow_small_or_imprecise_dtypes=True)
            pool.iota(pcol0[:], pattern=[[0, 1]], base=0, channel_multiplier=1, allow_small_or_imprecise_dtypes=True)
            pool.memset(eps_col[:, 0:1], EPS)
            pool.memset(eps_col[:, 1:2], GN_EPS).then_inc(basics, 1)
            for i in range(6):
                h = 2 << i
                v = tri[:, i, :].rearrange("p (b s) -> p b s", s=h)
                link(pool.memset(tri[:, i, :], 1.0))
                link(pool.affine_select(out=v, in_=v, compare_op=ALU.is_ge, fill=0.0, base=0,
                                        pattern=[[-h, P // h], [0, h]], channel_multiplier=1))
                link(pool.affine_select(out=v, in_=v, compare_op=ALU.is_ge, fill=0.0, base=h - 1,
                                        pattern=[[h, P // h], [0, h]], channel_multiplier=-1))
                link(pool.affine_select(out=tri[:, i, :], in_=tri[:, i, :], compare_op=ALU.is_ge, fill=0.0,
                                        base=0, pattern=[[1, P]], channel_multiplier=-1))
            link(pool.memset(causal[:], 1.0))
            link(pool.affine_select(out=causal[:], in_=causal[:], compare_op=ALU.is_ge, fill=0.0, base=0,
                                    pattern=[[1, P]], channel_multiplier=-1))
            link(pool.tensor_tensor(strict[:], causal[:], ident[:], ALU.subtract))
            inner = [ident[:]] + [tri[:, i, :] for i in range(6)]
            outer = [tri[:, i, :] for i in range(6)] + [causal[:]]
            for i in range(7):
                link(pool.tensor_tensor(level[:, i, :], outer[i], inner[i], ALU.subtract))
            pool.memset(xpad[:, :, 0:TAPS - 1], 0.0).then_inc(consts, 1)

            pool.wait_ge(b_ready, 1)
            for i, h in enumerate(HALVES + [P]):
                e = buf(eT[i % 2]).rearrange("p (b two h) -> p b two h", two=2, h=h)
                b = buf(5).rearrange("p (b two h) -> p b two h", two=2, h=h)
                kv = buf(4).rearrange("p (b two h) -> p b two h", two=2, h=h)
                nb = KB * S // (2 * h)
                if i >= 2:
                    pool.wait_ge(score_full, 4 + 2 * (i - 1))
                mid = b[:, :, 0, h - 1:h].to_broadcast([P, nb, h])
                pool.tensor_tensor(e[:, :, 0, :], mid, b[:, :, 0, :], ALU.subtract).then_inc(dl_ready, 1)
                pool.wait_ge(el_exp, i + 1)
                pool.wait_ge(k_ready, 1)
                pool.tensor_tensor(e[:, :, 0, :], e[:, :, 0, :], kv[:, :, 0, :], ALU.mult).then_inc(ek_ready, 1)
            if NSUB < 3:
                return

            for jj in range(KB // 2):
                for i in range(1, 7):
                    for pr in (2 * jj, 2 * jj + 1):
                        pool.wait_ge(lt_ready, pr + 1)
                        if i >= 3:
                            pool.wait_ge(tm_full, jj * 12 + 2 * (i - 3) + pr % 2 + 1)
                        elif jj > 1:
                            pool.wait_ge(tm_full, (jj - 1) * 12)
                        src = part(pr, 8, 4).rearrange("p (u s) -> p u s", u=4)
                        dst = lmask(pr, i).rearrange("p (u s) -> p u s", u=4)
                        pool.tensor_tensor(dst, src, level[:, i:i + 1, :].to_broadcast([P, 4, P]),
                                           ALU.mult).then_inc(lm_ready, 1)

        @block.tensor
        def _(pe):
            pe.wait_ge(basics, 1)

            def norm(k):
                for b in range(KB):
                    pe.wait_ge(sq_ready, 4 * k + b // 2 + 1)
                    strip = b % 4
                    mm = pe.matmul(bank[7][32 * strip:32 * (strip + 1), 0:S], ones[:, 0:32], squares[:, b, :],
                                   start=(b < 4), stop=(b >= 4))
                mm.then_inc(parts_full, 1)
                pe.wait_ge(parts_evac, k + 1)
                pe.matmul(bank[6][:, 0:S], thirty2[:].to_broadcast([P, P]), norm_parts, start=True,
                          stop=True).then_inc(total_full, 1)

            full = [0]

            def take(stage, n):
                tile, slot, count = plan[stage][n]
                pe.wait_ge(tile_landed[slot], 16 * count)
                return tile, slot

            def proj_bank():
                n = full[0]
                if n >= 4:
                    pe.wait_ge(proj_evac, n - 3)
                full[0] += 1
                return bank[n % 4]

            def project_T(slot, src):
                for half in range(2):
                    ps = proj_bank()
                    for c in range(2):
                        for k in range(KB):
                            mm = pe.matmul(ps[:, c * S:(c + 1) * S],
                                           w_cols(slot)[:, k, (2 * half + c) * P:(2 * half + c + 1) * P],
                                           src[:, k, :], start=(k == 0), stop=(k == KB - 1))
                    mm.then_inc(proj_full, 1)
                return mm

            def project_N(slot, src):
                for tt in range(NT):
                    ps = proj_bank()
                    for k in range(KB):
                        mm = pe.matmul(ps[:, :], src[:, k, tt * P:(tt + 1) * P], w_cols(slot)[:, k, :],
                                       start=(k == 0), stop=(k == KB - 1))
                    mm.then_inc(proj_full, 1)
                return mm

            def mod_columns(m, cols_bank):
                pe.wait_ge(mod_row, m + 1)
                for c in range(4):
                    mm = pe.matmul(cols_bank[:, 4 * m + c:4 * m + c + 1], mod_rows[m // 12][:, m % 2, c * P:(c + 1) * P],
                                   thirty2[:], start=True, stop=True)
                mm.then_inc(mod_cols, 1)

            def modulation(m, row_banks, cols_bank):
                _, slot = take(0, places[0, "mod"][m])
                if m >= len(row_banks):
                    pe.wait_ge(mod_row, m + 1 - len(row_banks))
                for r in range(2):
                    for c in range(4):
                        k = 4 * r + c
                        mm = pe.matmul(row_banks[m % len(row_banks)][32 * c:32 * (c + 1), :], csilu[:, k:k + 1].to_broadcast([P, 32]),
                                       w_cols(slot)[:, k, :], start=(r == 0), stop=(r == 1))
                mm.then_inc(mod_full, 1)
                if m not in (0, MOD_FIRST, 12):
                    mod_columns(m - 1, cols_bank)

            mod_next = [12]

            def modulation_step():
                if mod_next[0] < 24:
                    modulation(mod_next[0], (bank[0], bank[1]), bank[2])
                    mod_next[0] += 1

            def out_projection(stage, first, n, srcs, ready):
                for j in range(n):
                    ready(j)
                    _, slot = take(stage, first + j)
                    for d in range(KB):
                        for kk in range(4):
                            mm = pe.matmul(bank[d // 2][:, (d % 2) * S:(d % 2 + 1) * S],
                                           w_rows(slot)[:, kk, d * P:(d + 1) * P], srcs(4 * j + kk),
                                           start=(j == 0 and kk == 0 and d % 2 == 0),
                                           stop=(j == n - 1 and kk == 3), skip_group_check=True)
                    mm.then_inc(tile_used, 1)

            pe.wait_ge(vec_landed, 16 * len(VEC))
            for g in range(3):
                mm = pe.transpose(bank[4][:, g * P:(g + 1) * P], vrows[:, g, :], ident[:])
            mm.then_inc(vec_T, 1)
            pe.wait_ge(x_landed, 16)
            for k in range(KB):
                for tt in range(NT):
                    mm = pe.transpose(bank[k // 2][:, (k % 2) * S + tt * P:(k % 2) * S + (tt + 1) * P],
                                      xN[:, tt, k * P:(k + 1) * P], ident[:])
                if k % 2:
                    mm.then_inc(xT_psum, 1)
            pe.wait_ge(csilu_ready, 1)
            norm(0)
            pe.wait_ge(root_ready, 1)
            for m in range(MOD_FIRST):
                modulation(m, (bank[6], bank[7]), bank[5])
            mod_columns(MOD_FIRST - 1, bank[5])
            pe.wait_ge(h_ready, 4)
            pe.wait_ge(xT_evac, 1)

            scores = [0]

            def score_bank():
                m = scores[0]
                if m >= 2:
                    pe.wait_ge(score_evac, m - 1)
                scores[0] += 1
                return bank[4 + m % 2]

            def diagonal():
                pe.wait_ge(proj_evac, 8)
                pe.wait_ge(k_ready, 1)
                for r in range(2):
                    for tt in range(NT):
                        ps = score_bank()
                        for h in range(4):
                            ss = slice(tt * P, (tt + 1) * P)
                            mm = pe.matmul(ps[:, h * P:(h + 1) * P], kT[:, 4 * r + h, ss], qT[:, 4 * r + h, ss],
                                           start=True, stop=True)
                        mm.then_inc(score_full, 1)

            def level_scores(i):
                h = (HALVES + [P])[i]
                pe.wait_ge(ek_ready, i + 1)
                pe.wait_ge(eq_ready, i + 1)
                e = blocks(eT[i % 2])
                if h < P:
                    for tt in range(NT):
                        ps = score_bank()
                        for hh in range(KB):
                            et = e[:, hh, tt * P:(tt + 1) * P]
                            right = et.rearrange("p (b two h) -> p b two h", two=2, h=h)[:, :, 1, :]
                            mm = pe.matmul(ps[:, hh * 64:(hh + 1) * 64], et, right, start=True, stop=True)
                        mm.then_inc(score_full, 1)
                else:
                    for r in range(2):
                        ps = score_bank()
                        for hh in range(4):
                            mm = pe.matmul(ps[:, hh * P:(hh + 1) * P], e[:, 4 * r + hh, 0:P],
                                           e[:, 4 * r + hh, P:S], start=True, stop=True)
                        mm.then_inc(score_full, 1)

            extra = {4: [diagonal, lambda: level_scores(0)], 5: [lambda: level_scores(1)],
                     6: [lambda: level_scores(2)], 7: [lambda: level_scores(3)], 8: [lambda: level_scores(4)],
                     9: [lambda: level_scores(5)], 10: [lambda: level_scores(6)], 11: [lambda: level_scores(7)]}
            for n in range(13):
                (_, _, j), slot = take(0, places[0, "in"][n])
                mm = (project_N if j in (4, 5) else project_T)(slot, hT)
                if MOD_FIRST + n < 12:
                    if n == 0:
                        pe.wait_ge(h_ready, 4)
                    modulation(MOD_FIRST + n, (bank[7],), bank[6])
                elif MOD_FIRST + n == 12:
                    mod_columns(11, bank[6])
                if n == 8:
                    pe.wait_ge(small_landed, 16 * 7)
                    pe.wait_ge(mod_row, 12)
                    for k in range(KB):
                        mm = pe.matmul(bank[7][0:NH, 0:S], w_dt[:, k, :], hT[:, k, :], start=(k == 0),
                                       stop=(k == KB - 1))
                    mm.then_inc(dt_full, 1)
                for f in extra.get(n, []):
                    f()

            pe.wait_ge(score_evac, 20)
            pe.wait_ge(proj_evac, 26)
            pe.wait_ge(mod_taken, 2)
            for u in range(4):
                if u >= 2:
                    pe.wait_ge(o_evac, u - 1)
                elif u == 0:
                    pe.wait_ge(dtz, 1)
                for c in range(2):
                    h = 2 * u + c
                    hs = slice(h * P, (h + 1) * P)
                    o = bank[6 + u % 2]
                    pe.matmul(o[:, c * S:c * S + P], vN[:, 0, hs], scd[:, 0, h, :], start=True, stop=True)
                    pe.matmul(o[:, c * S + P:(c + 1) * S], vN[:, 0, hs], scx[:, h, :], start=True, stop=False)
                    mm = pe.matmul(o[:, c * S + P:(c + 1) * S], vN[:, 1, hs], scd[:, 1, h, :], start=False, stop=True)
                mm.then_inc(o_full, 1)
                modulation_step()

            pe.wait_ge(dt_ready, 1)
            for a in range(2):
                for tt in range(NT):
                    mm = pe.transpose(bank[4][:, (2 * a + tt) * NH:(2 * a + tt + 1) * NH],
                                      dts[:, 3 + a, tt * P:(tt + 1) * P], ident[0:NH, 0:NH])
            mm.then_inc(dtN_full, 1)
            pe.wait_ge(conv_silu, 1)
            pe.wait_ge(o_evac, 4)
            for u in range(4):
                tt, half = u // 2, u % 2
                if u == 3:
                    pe.wait_ge(xdt_ready, 1)
                ps = bank[[5, 6, 7, 5][u]]
                for c in range(4):
                    mm = pe.transpose(ps[:, c * P:(c + 1) * P],
                                      xpad[:, 4 * half + c, TAPS - 1 + tt * P:TAPS - 1 + (tt + 1) * P], ident[:])
                mm.then_inc(xs_full, 1)
            pe.wait_ge(xdt_ready, 3)
            for g in range(GROUPS):
                ps = bank[6 + g]
                B = xpad[:, KB + g, TAPS - 1:]
                Cq = xpad[:, KB + GROUPS + g, TAPS - 1:]
                pe.matmul(ps[:, 0:S], B[:, 0:P], Cq[:, 0:S], start=True, stop=True)
                mm = pe.matmul(ps[:, S:S + P], B[:, P:S], Cq[:, P:S], start=True, stop=True)
                mm.then_inc(cb_full, 1)
            pe.wait_ge(dtN_ready, 1)
            pe.wait_ge(xdt_ready, 4)
            for h in range(KB):
                for tt in range(NT):
                    mm = pe.matmul(bank[4][:, tt * KB + h:tt * KB + h + 1], fT[:, h, tt * P:(tt + 1) * P],
                                   ones[:, 0:1], start=True, stop=True)
            mm.then_inc(head_sum, 1)
            pe.wait_ge(head_rstd, 1)
            for u in range(4):
                if u >= 2:
                    pe.wait_ge(bcast_used, u - 1)
                for c in range(2):
                    for tt in range(NT):
                        r = tt * KB + 2 * u + c
                        mm = pe.matmul(bank[4 + u % 2][:, c * S + tt * P:c * S + (tt + 1) * P],
                                       rstd[:, r:r + 1].to_broadcast([P, P]), ident[:], start=True, stop=True)
                mm.then_inc(head_bcast, 1)
            pe.wait_ge(cb_ready, 2)
            pe.wait_ge(bcast_used, 4)

            def decay_row(h):
                if h >= 2:
                    pe.wait_ge(dec_diff, h - 1)
                pe.matmul(bank[4 + h % 2][:, 0:S], ident[0:NH, h:h + 1].to_broadcast([NH, P]), dts[:, 4, :],
                          start=True, stop=True).then_inc(row_full, 1)

            def head_out(h):
                pe.wait_ge(dec_mat, h + 1)
                pr, c = h // 2, h % 2
                if pr >= 2 and c == 0:
                    pe.wait_ge(y_ready, pr - 1)
                o = bank[6 + pr % 2][c * HEAD:(c + 1) * HEAD, :]
                m = dec[:, h % NDEC, :]
                hs = slice(h * HEAD, (h + 1) * HEAD)
                pe.matmul(o[:, 0:S], xdt[:, 0, hs], m[:, 0:S], start=True, stop=True)
                pe.matmul(o[:, P:S], xdt[:, 1, hs], m[:, S:S + P], start=False, stop=True,
                          skip_group_check=True).then_inc(y_full, 1)

            for h in range(NH + 3):
                if h < NH:
                    decay_row(h)
                    modulation_step()
                if h >= 3:
                    head_out(h - 3)
            mod_columns(23, bank[2])
            pe.wait_ge(squares_ready, 1)
            pe.wait_ge(dec_diff, NH)
            for g in range(GROUPS):
                for tt in range(NT):
                    for k in range(4):
                        mm = pe.matmul(bank[4][:, 2 * g + tt:2 * g + tt + 1],
                                       fT[:, 4 * g + k, tt * P:(tt + 1) * P], ones[:, 0:1],
                                       start=(k == 0), stop=(k == 3))
            mm.then_inc(head_sum, 1)
            pe.wait_ge(head_rstd, 2)
            for g in range(GROUPS):
                for tt in range(NT):
                    r = 2 * g + tt
                    mm = pe.matmul(bank[5][:, g * S + tt * P:g * S + (tt + 1) * P],
                                   rstd[:, r:r + 1].to_broadcast([P, P]), ident[:], start=True, stop=True)
            mm.then_inc(yb_full, 1)
            pe.wait_ge(mod_taken, 3)
            out_projection(0, places[0, "out"][0], 4, lambda i: oa[:, i, :] if i < KB else yT[:, i - KB, :],
                           lambda j: pe.wait_ge(oa_ready, 1) if j == 0 else pe.wait_ge(ob_ready, 1))

            def moe(l, k):
                m = M[l]
                norm(k)
                pe.wait_ge(h_ready, 4 * k + 4)
                for tt in range(NT):
                    for kk in range(KB):
                        mm = pe.matmul(bank[0][:, tt * NE:(tt + 1) * NE], hT[:, kk, tt * P:(tt + 1) * P],
                                       router_w[:, kk, :], start=(kk == 0), stop=(kk == KB - 1))
                mm.then_inc(m["logit_full"], 1)
                for u in range(4):
                    half, tt = u // 2, u % 2
                    for c in range(4):
                        mm = pe.transpose(bank[4 + u][:, c * P:(c + 1) * P],
                                          hT[:, 4 * half + c, tt * P:(tt + 1) * P], ident[:])
                    mm.then_inc(m["hN_full"], 1)
                pe.wait_ge(m["sel_ready"], l + 1)
                sel = small(8).rearrange("p (t e) -> p t e", t=NT)
                pe.matmul(bank[1][:, 0:NE], strict[:], sel[:, 0, :], start=True, stop=True)
                pe.matmul(bank[1][:, NE:2 * NE], ones[:, 0:P], sel[:, 0, :], start=True, stop=False)
                pe.matmul(bank[1][:, NE:2 * NE], strict[:], sel[:, 1, :], start=False, stop=True)
                pe.matmul(bank[1][:, 2 * NE:3 * NE], ones[:, 0:P], sel[:, 0, :], start=True, stop=False)
                pe.matmul(bank[1][:, 2 * NE:3 * NE], ones[:, 0:P], sel[:, 1, :], start=False,
                          stop=True).then_inc(m["rank_full"], 1)
                pe.wait_ge(m["slots_ready"], 2 * l + 2)
                for r in range(4):
                    for tt in range(NT):
                        mm = pe.matmul(bank[2 + r // 2][:, (r % 2) * S + tt * P:(r % 2) * S + (tt + 1) * P],
                                       tok4[:, tt, r:r + 1].to_broadcast([P, P]), ident[:], start=True, stop=True)
                mm.then_inc(m["slot_full"], 1)

                def gather():
                    for kb in range(KB):
                        for tt in range(NT):
                            mm = pe.matmul(bank[6 + kb // 4][:, (kb % 4) * P:(kb % 4 + 1) * P],
                                           hN[:, tt, kb * P:(kb + 1) * P], pick[:, tt, :],
                                           start=(tt == 0), stop=(tt == NT - 1))
                    mm.then_inc(m["gath_full"], 1)

                def scatter(half, first=False, last=False):
                    for d in range(4 * half, 4 * half + 4):
                        mm = pe.matmul(bank[d // 2][:, (d % 2) * S:(d % 2 + 1) * S], ymoe[:, d * P:(d + 1) * P],
                                       spread, start=(first and d % 2 == 0), stop=last, skip_group_check=True)
                    if half:
                        mm.then_inc(m["scat_done"], 1)

                pe.wait_ge(m["hN_evac"], 4 * l + 4)
                pe.wait_ge(m["pick_ready"], 1)
                gather()
                pe.wait_ge(m["y0_ready"], 1)
                pe.wait_ge(m["y1_ready"], 1)
                pe.wait_ge(m["spread_ready"], 1)
                pe.wait_ge(m["rows_ready"], l + 1)
                scatter(0, first=True)
                scatter(1, first=True)
                lo = moe_base[l]
                def block_of_slots(g, slots, landed_wait):
                    pe.wait_ge(m["hga_ready"], g + 1)
                    pe.wait_ge(m["hgb_ready"], g + 1)
                    for half in range(2):
                        if half:
                            pe.wait_ge(m["y0_ready"], g + 1)
                        for e in range(2):
                            landed_wait(2 * half + e)
                        for kb in range(KB):
                            for e in range(2):
                                mm = pe.matmul(bank[4 + half][e * C:(e + 1) * C, :], hgT[:, kb, e * C:(e + 1) * C],
                                               w_cols(slots[2 * half + e])[:, kb, :], start=(kb == 0), stop=(kb == KB - 1))
                        mm.then_inc(m["w3_done" if half else "w1_done"], 1)
                    pe.wait_ge(m["y1_ready"], g + 1)
                    pe.wait_ge(m["pick_ready"], g + 2)
                    gather()
                    pe.wait_ge(m["spread_ready"], g + 1)
                    scatter(0)
                    pe.wait_ge(m["hid_ready"], g + 1)
                    for f in range(FB):
                        mm = pe.transpose(bank[4][:, f * P:(f + 1) * P], hid[:, f * P:(f + 1) * P], ident[:])
                    mm.then_inc(m["hidT_full"], 1)
                    scatter(1)
                    pe.wait_ge(m["hidT_ready"], g + 1)
                    for e in range(2):
                        landed_wait(4 + e)
                    for half in range(2):
                        if half:
                            pe.wait_ge(m["hga_ready"], g + 2)
                        for f in range(FB):
                            for e in range(2):
                                mm = pe.matmul(bank[5 + half][e * C:(e + 1) * C, :], hidT[:, f, e * C:(e + 1) * C],
                                               w_rows(4 + e)[:, f, half * W:(half + 1) * W],
                                               start=(f == 0), stop=(f == FB - 1))
                        mm.then_inc(m["down_half"], 1)

                ring_slots = tuple(range(SLOTS))
                for pair in range(2):
                    n = pe.value_load(tab_i[0:1, pair:pair + 1], min_val=1, max_val=4)
                    g0 = pe.value_load(tab_i[0:1, NE // 2 + pair:NE // 2 + pair + 1], min_val=0, max_val=NE)

                    def landed_wait(place, pair=pair):
                        if pair and place in BORROWED:
                            pe.wait_ge(ahead_landed, 16 * len(BORROWED) * (l + 1))
                        else:
                            pe.wait_ge(tile_landed[place], (lo[place] + pair + 1) * 16)

                    with pe.Fori(0, n) as j:
                        block_of_slots(g0 + j, tuple(SLOTS + x if x in BORROWED else x for x in ring_slots) if pair
                                       else ring_slots, landed_wait)
                with pe.Fori(2, NE // 2) as i:
                    n = pe.value_load(tab_i[0:1, bass.ds(i, 1)], min_val=1, max_val=4)
                    g0 = pe.value_load(tab_i[0:1, bass.ds(i + NE // 2, 1)], min_val=0, max_val=NE)
                    with pe.Fori(0, n) as j:
                        block_of_slots(g0 + j, ring_slots, lambda place: pe.wait_ge(
                            tile_landed[place], (i + (lo[place] + (place not in BORROWED))) * 16))
                total = pe.value_load(tab_i[0:1, NE:NE + 1], min_val=NE // 2, max_val=NE)
                pe.wait_ge(m["y0_ready"], total + 1)
                pe.wait_ge(m["y1_ready"], total + 1)
                pe.wait_ge(m["spread_ready"], total + 1)
                scatter(0, last=True)
                scatter(1, last=True)

            if NSUB >= 2:
                moe(0, 1)
            if NSUB >= 3:
                norm(2)
                _, sa = take(1, places[1, "la"][0])
                _, sl = take(1, places[1, "lb"][0])
                wa, wl = weight(sa), weight(sl)
                first = [wa[:, 0:512].rearrange("p (k n) -> p k n", k=KB),
                         wa[:, 512:1024].rearrange("p (k n) -> p k n", k=KB),
                         wa[:, 1024:2048].rearrange("p (k n) -> p k n", k=KB)]
                second = [wl[0:64, 0:D], wl[0:64, D:2 * D], wl[:, 2 * D:3 * D]]
                rank = [64, 64, P]
                for i in range(3):
                    for k in range(KB):
                        pe.wait_ge(mix_ready, i + 4 if i else k // 2 + 1)
                        mm = pe.matmul(bank[4][0:rank[i], 0:S], first[i][:, k, :], mixed[i % 2][:, k, :],
                                       start=(k == 0), stop=(k == KB - 1))
                    mm.then_inc(lora_full, 1)
                    pe.wait_ge(lora_evac, i + 1)
                    for u in range(4):
                        ps = proj_bank()
                        for c in range(2):
                            d = 2 * u + c
                            mm = pe.matmul(ps[:, c * S:(c + 1) * S], second[i][:, d * P:(d + 1) * P],
                                           lora[i][0:rank[i], :], start=True, stop=True)
                        mm.then_inc(proj_full, 1)
                def head_sums(ps, src):
                    for pr in range(KB):
                        for tt in range(NT):
                            r = tt * NH + 2 * pr
                            mm = pe.matmul(ps[:, r:r + 2], src[:, pr, tt, :], halves[:], start=True, stop=True)
                    return mm

                def head_rows_ring(colsrc, n):
                    for tt in range(NT):
                        mm = pe.transpose(bank[4][0:NH, (1 + tt) * P:(2 + tt) * P], colsrc[:, tt * NH:(tt + 1) * NH],
                                          ident[:])
                    mm.then_inc(hrow_full, 1)
                    pe.wait_ge(hrow_evac, n + 1)
                    for u in range(4):
                        pe.wait_ge(bcast_used, 4 + 4 * n + max(u - 1, 0))
                        for c in range(2):
                            for hh in range(2):
                                h = 2 * (2 * u + c) + hh
                                mm = pe.matmul(bank[6 + u % 2][hh * HEAD:(hh + 1) * HEAD, c * S:(c + 1) * S],
                                               ident[0:NH, h:h + 1].to_broadcast([NH, HEAD]), hrows,
                                               start=True, stop=True)
                        mm.then_inc(head_bcast, 1)

                for n, i in enumerate((1, 0, 2)):
                    pe.wait_ge(mix_ready, 7 + n)
                    for j in range(2):
                        _, slot = take(1, places[1, "rkv"][2 * n + j])
                        (project_N if i == 2 else project_T)(slot, mixed[(3 + n) % 2])
                        if (n, j) == (1, 1):
                            pe.wait_ge(sums_in, 1)
                            head_sums(bank[4], by_tile(1)).then_inc(head_sum, 1)
                        if (n, j) == (2, 0):
                            pe.wait_ge(sums_in, 2)
                            head_sums(bank[5], by_tile(2)).then_inc(head_sum, 1)
                            pe.wait_ge(head_rstd, 3)
                            head_rows_ring(rstd, 0)
                pe.wait_ge(rw_ops, 4)

                def score_fill(pr, q):
                    m = 6 * pr + q
                    if m >= 2:
                        pe.wait_ge(rsc_evac, m - 1)
                    kind, hh = q // 2, q % 2
                    fs = slice(hh * HEAD, (hh + 1) * HEAD)
                    if kind == 2:
                        pe.wait_ge(kc_ready, pr + 1)
                    for half in range(2):
                        if kind == 2:
                            keys, tt = kcross(pr, half)[fs, :], 1
                        else:
                            keys, tt = (rwK, rwB)[kind][fs, pr, half, :], half
                        mm = pe.matmul(bank[hh][:, half * S:(half + 1) * S], keys, AR[fs, pr, tt, :, :],
                                       start=True, stop=True)
                    mm.then_inc(rsc_full, 1)

                def invert(jj):
                    prs = (2 * jj, 2 * jj + 1)
                    for pr in prs:
                        pe.wait_ge(xt1_ready, pr + 1)
                        for u in range(4):
                            mm = pe.transpose(bank[4 + 2 * (pr % 2)][:, u * P:(u + 1) * P],
                                              xinvT(pr)[:, u * P:(u + 1) * P], ident[:])
                        mm.then_inc(x1_full, 1)
                    for i in range(1, 7):
                        for pr in prs:
                            n = jj * 12 + 2 * (i - 1) + pr % 2
                            pe.wait_ge(lm_ready, n + 1)
                            if i == 1:
                                pe.wait_ge(x1_ready, pr + 1)
                            else:
                                pe.wait_ge(xi_ready, xi(jj, i - 1, pr) + 1)
                            for u in range(4):
                                us = slice(u * P, (u + 1) * P)
                                mm = pe.matmul(bank[2 + pr % 2][:, us], lmask(pr, i)[:, us], xinv(pr)[:, us],
                                               start=True, stop=True)
                            mm.then_inc(tm_full, 1)
                        for pr in prs:
                            n = jj * 12 + 2 * (i - 1) + pr % 2
                            pe.wait_ge(tm_ready, n + 1)
                            if i > 1:
                                pe.wait_ge(xm_ready, n - 1)
                            if i < 6:
                                for u in range(4):
                                    us = slice(u * P, (u + 1) * P)
                                    mm = pe.matmul(bank[4 + 2 * (pr % 2)][:, us], xinvT(pr)[:, us],
                                                   tmid(pr)[:, us], start=True, stop=True)
                                mm.then_inc(xi_full, 1)
                            for u in range(4):
                                us = slice(u * P, (u + 1) * P)
                                mm = pe.matmul(bank[5 + 2 * (pr % 2)][:, us], tmid(pr)[:, us], xinvT(pr)[:, us],
                                               start=True, stop=True)
                            mm.then_inc(xm_full, 1)

                def solve_w(pr, tt):
                    bw = bank[2 + pr % 2]
                    for hh in range(2):
                        o = bw[:, hh * HEAD:(hh + 1) * HEAD]
                        h = 2 * pr + hh
                        mm = pe.matmul(o, sc(pr, 0, tt, hh), vN1[:, tt, h, :], start=True, stop=(tt == 0))
                        if tt:
                            pe.matmul(o, scro(pr, 0, hh), vN1[:, 0, h, :], start=False, stop=False)
                            mm = pe.matmul(o, scro(pr, 2, hh), uneg(pr, 0)[:, hh * HEAD:(hh + 1) * HEAD],
                                           start=False, stop=True)
                    mm.then_inc(w_full, 1)

                def solve_u(pr, tt):
                    for hh in range(2):
                        mm = pe.matmul(bank[2 + pr % 2][:, P + hh * HEAD:P + (hh + 1) * HEAD],
                                       xinvT(pr)[:, (2 * tt + hh) * P:(2 * tt + hh + 1) * P],
                                       tmid(pr)[:, (2 * tt + hh) * HEAD:(2 * tt + hh + 1) * HEAD],
                                       start=True, stop=True)
                    mm.then_inc(u_full, 1)

                def outputs(pr):
                    def step(cols, keys, scores, first, last):
                        for hh in range(2):
                            o = bank[4 + 2 * (pr % 2)][hh * HEAD:(hh + 1) * HEAD, :]
                            mm = pe.matmul(o[:, cols], keys(hh), scores(hh), start=first, stop=last)
                        return mm

                    v = lambda tt: lambda hh: vN1[:, tt, 2 * pr + hh, :]
                    un = lambda tt: lambda hh: uneg(pr, tt)[:, hh * HEAD:(hh + 1) * HEAD]
                    one, two = slice(0, P), slice(P, S)
                    step(one, v(0), lambda hh: sc(pr, 1, 0, hh), True, False)
                    step(one, un(0), lambda hh: sc(pr, 3, 0, hh), False, True)
                    step(two, v(1), lambda hh: sc(pr, 1, 1, hh), True, False)
                    step(two, un(1), lambda hh: sc(pr, 3, 1, hh), False, False)
                    step(two, v(0), lambda hh: scro(pr, 1, hh), False, False)
                    mm = step(two, un(0), lambda hh: scro(pr, 3, hh), False, True)
                    mm.then_inc(ry_full, 1)

                pe.wait_ge(proj_evac, 26 + 12 + 12)
                pe.wait_ge(bcast_used, 8)
                for pr in range(2):
                    for q in range(6):
                        score_fill(pr, q)
                for jj in range(KB // 2):
                    prs = (2 * jj, 2 * jj + 1)
                    fills = [(pr, q) for pr in (2 * jj + 2, 2 * jj + 3) for q in range(6) if pr < KB]
                    if jj > 0:
                        pe.wait_ge(ry_ready, 2 * jj)
                    invert(jj)
                    for pr in prs:
                        pe.wait_ge(xm_ready, jj * 12 + 10 + pr % 2 + 1)
                    for tt in range(NT):
                        for pr in prs:
                            if tt:
                                pe.wait_ge(u_ready, 4 * jj + pr % 2 + 1)
                            solve_w(pr, tt)
                        for pr, q in fills[6 * tt:6 * tt + 3]:
                            score_fill(pr, q)
                        for pr in prs:
                            pe.wait_ge(w_ready, 4 * jj + 2 * tt + pr % 2 + 1)
                            solve_u(pr, tt)
                        for pr, q in fills[6 * tt + 3:6 * tt + 6]:
                            score_fill(pr, q)
                    for pr in prs:
                        pe.wait_ge(u_ready, 4 * jj + 2 + pr % 2 + 1)
                        outputs(pr)

                pe.wait_ge(ry_ready, KB)

                head_sums(bank[4], oR).then_inc(head_sum, 1)
                pe.wait_ge(gn_mean, 1)
                head_rows_ring(gm_mean, 1)
                pe.wait_ge(squares_ready, 2)
                head_sums(bank[4], by_tile(3)).then_inc(head_sum, 1)
                pe.wait_ge(head_rstd, 4)
                pe.wait_ge(bcast_used, 12)
                head_rows_ring(rstd, 2)
                pe.wait_ge(bv_ready, 1)
                pe.wait_ge(ry_ready, KB)
                for pr in range(KB):
                    for tt in range(NT):
                        mm = pe.transpose(bank[pr // 2][:, (pr % 2) * S + tt * P:(pr % 2) * S + (tt + 1) * P],
                                          bvN[:, tt, 2 * pr:2 * pr + 2, :].rearrange("p h n -> p (h n)"), ident[:])
                mm.then_inc(bvT_full, 1)
                pe.wait_ge(og_ready, 1)
                og = blocks(4)
                out_projection(1, places[1, "wo"][0], 2, lambda i: og[:, i, :], lambda j: None)
            if NSUB >= 4:
                moe(1, 3)
            norm(NSUB)
            for u in range(8):
                q, tt = u // 2, u % 2
                pe.wait_ge(h_ready, 4 * NSUB + q + 1)
                for c in range(2):
                    mm = pe.transpose(bank[u][:, c * P:(c + 1) * P],
                                      hT[:, 2 * q + c, tt * P:(tt + 1) * P], ident[:])
                mm.then_inc(o_full, 1)

        @block.scalar
        def _(act):
            count = [0]

            def link(ins):
                count[0] += 1
                ins.then_inc(act_chain, 1)
                act.wait_ge(act_chain, count[0])

            act.wait_ge(vrows_zeroed, 1)
            for name, (g, r, n) in VEC.items():
                src = t[name]
                flat = src.rearrange({1: "a -> a", 2: "a b -> (a b)", 3: "a b c -> (a b c)"}[len(src.shape)])
                act.dma_start(vrows[r:r + n, g, :], flat.rearrange("(n p) -> n p", p=P)).then_inc(vec_landed, 16)
            act.dma_start(xN[:, :, :], t["x"][0].rearrange("(t p) d -> p t d", p=P)).then_inc(x_landed, 16)
            act.dma_start(dt_bias[:], t["ev_dt_bias"].rearrange("a h -> h a")).then_inc(small_landed, 16)
            act.dma_start(a_log[:], t["ev_a_log"].rearrange("a h -> h a")).then_inc(small_landed, 16)
            skip = t["ev_d_skip"].rearrange("a (j two) -> two (a j)", two=2)
            for hh in range(2):
                act.dma_start(dskip[hh * HEAD:(hh + 1) * HEAD, :],
                              skip[hh:hh + 1, :].to_broadcast([HEAD, KB])).then_inc(small_landed, 16)
            act.dma_start(w_dt[:], row_block(t["ev_w_in"][0])[:, :, IN_COLS - NH:IN_COLS]).then_inc(small_landed, 16)
            act.dma_start(router_w[:], row_block(t["router_w"])).then_inc(small_landed, 16)
            act.dma_start(router_b[:], t["router_b"].rearrange("(a e) -> a e", a=1).to_broadcast([P, NE])
                          ).then_inc(small_landed, 16)

            act.wait_ge(vec_cols, 1)
            act.activation(csilu[:], cols("c", 0, KB), ACT.Silu).then_inc(csilu_ready, 1)
            act.wait_ge(lb_max, 1)
            act.activation(lbe[:], lbe[:], ACT.Exp).then_inc(start_exp, 1)
            for u in range(4):
                act.wait_ge(xT_psum, u + 1)
                ins = act.activation(xT[:, 2 * u:2 * u + 2, :].rearrange("p k s -> p (k s)"), bank[u][:], ACT.Copy)
            ins.then_inc(xT_evac, 1)
            act.wait_ge(basics, 1)

            def mod_evac(m, row_banks):
                act.wait_ge(mod_full, m + 1)
                if m >= 2:
                    act.wait_ge(mod_cols, m - 1)
                act.activation(mod_rows[m // 12][:, m % 2, :], row_banks[m % len(row_banks)][:], ACT.Copy).then_inc(mod_row, 1)

            mod_next = [12]

            def modulation_step():
                if mod_next[0] < 24:
                    mod_evac(mod_next[0], (bank[0], bank[1]))
                    mod_next[0] += 1

            def norm_root(k):
                for u in range(4):
                    if k == 0:
                        act.wait_ge(xT_evac, 1)
                    else:
                        act.wait_ge(x_ready, 4 * (k - 1) + u + 1)
                    act.activation(squares[:, 2 * u:2 * u + 2, :], xT[:, 2 * u:2 * u + 2, :],
                                   ACT.Square).then_inc(sq_ready, 1)
                act.wait_ge(parts_full, k + 1)
                act.activation(norm_parts, bank[7][:, 0:S], ACT.Copy).then_inc(parts_evac, 1)
                act.wait_ge(total_full, k + 1)
                act.activation(norm_rstd, bank[6][:, 0:S], ACT.Sqrt, bias=eps_col[:, 0:1],
                               scale=1.0 / D).then_inc(root_ready, 1)

            def norm_shift(k):
                if k < NSUB:
                    l, f = k // 2, k % 2
                    for b in range(KB):
                        act.wait_ge(scaled, 4 * k + b // 2 + 1)
                        ins = act.activation(hT[:, b, :], hT[:, b, :], ACT.Identity,
                                             bias=modT[:, l, 3 * f * KB + b:3 * f * KB + b + 1])
                        if b % 2:
                            ins.then_inc(h_ready, 1)

            def norm(k):
                norm_root(k)
                norm_shift(k)

            norm_root(0)
            for m in range(MOD_FIRST):
                mod_evac(m, (bank[6], bank[7]))
            norm_shift(0)
            evac = [0]

            def evacuate(dst, func=ACT.Copy, **kw):
                n = evac[0]
                act.wait_ge(proj_full, n + 1)
                act.activation(dst, bank[n % 4][:], func, **kw).then_inc(proj_evac, 1)
                evac[0] += 1

            def evac_T(dst, first):
                for u in range(2):
                    b = first + 2 * u
                    evacuate(dst[:, b:b + 2, :].rearrange("p k s -> p (k s)"), ACT.Copy)

            act.wait_ge(small_landed, 16 * 7)
            act.activation(a_neg[:], a_log[:], ACT.Exp).then_inc(start_exp, 1)
            for u in range(4):
                n = evac[0]
                act.wait_ge(proj_full, n + 1)
                act.activation(fT[:, 2 * u:2 * u + 2, :].rearrange("p k s -> p (k s)"), bank[n % 4][:],
                               ACT.Sigmoid).then_inc(proj_evac, 1)
                evac[0] += 1
                if u % 2:
                    mod_evac(MOD_FIRST + u // 2, (bank[7],))
            act.wait_ge(k_ready, 1)
            act.activation(fT[:, :, :], fT[:, :, :], ACT.Ln).then_inc(logf_ready, 1)
            evac_T(qT, 0)
            mod_evac(MOD_FIRST + 2, (bank[7],))
            evac_T(qT, 4)
            mod_evac(MOD_FIRST + 3, (bank[7],))

            def level_exp(i):
                act.wait_ge(dl_ready, i + 1)
                act.wait_ge(dr_ready, i + 1)
                act.activation(buf(eT[i % 2]), buf(eT[i % 2]), ACT.Exp).then_inc(el_exp, 1)

            def evac_v(j):
                for tt in range(NT):
                    evacuate(vN[:, tt, j * W:(j + 1) * W])

            def evac_xbc(first):
                for u in range(2):
                    n = evac[0]
                    b = first + 2 * u
                    act.wait_ge(consts, 1)
                    act.wait_ge(proj_full, n + 1)
                    act.activation(xpad[:, b:b + 2, TAPS - 1:],
                                   bank[n % 4][:].rearrange("p (k s) -> p k s", k=2), ACT.Copy).then_inc(proj_evac, 1)
                    evac[0] += 1

            level_exp(0)
            evac_v(0)
            mod_evac(MOD_FIRST + 4, (bank[7],))
            level_exp(1)
            evac_v(1)
            mod_evac(MOD_FIRST + 5, (bank[7],))
            level_exp(2)
            evac_xbc(8)
            mod_evac(MOD_FIRST + 6, (bank[7],))
            level_exp(3)
            evac_xbc(0)
            mod_evac(MOD_FIRST + 7, (bank[7],))
            level_exp(4)
            evac_xbc(4)
            level_exp(5)
            act.wait_ge(dtz, 1)
            act.activation(dts[:, 1, :], dts[:, 0, :], ACT.Abs).then_inc(dtabs, 1)
            act.wait_ge(dtabs, 1)
            link(act.activation(dts[:, 1, :], dts[:, 1, :], ACT.Exp, scale=-1.0))
            act.activation(dts[:, 2, :], dts[:, 1, :], ACT.Ln, bias=1.0).then_inc(dtln, 1)
            evac_T(zT, 0)
            level_exp(6)
            evac_T(zT, 4)
            level_exp(7)
            evac_T(gT, 0)
            evac_T(gT, 4)
            act.wait_ge(proj_evac, 26)
            for u in range(4):
                act.wait_ge(o_full, u + 1)
                dst = lambda x: x[:, 2 * u:2 * u + 2, :].rearrange("p k s -> p (k s)")
                act.activation(dst(oa), bank[6 + u % 2][:], ACT.Copy)
                act.activation(dst(fT), bank[6 + u % 2][:], ACT.Square).then_inc(o_evac, 1)
                modulation_step()
            act.wait_ge(conv_done, XBLK)
            act.activation(xpad[:, :, TAPS - 1:], xpad[:, :, TAPS - 1:], ACT.Silu).then_inc(conv_silu, 1)
            act.activation(buf(10), buf(10), ACT.Silu)
            act.activation(buf(11), buf(11), ACT.Silu).then_inc(silu_g, 1)
            act.wait_ge(head_sum, 1)
            act.activation(rs_root[:, 0:2 * KB], bank[4][:, 0:2 * KB], ACT.Sqrt, bias=eps_col[:, 0:1],
                           scale=1.0 / P).then_inc(head_root, 1)
            for h in range(NH):
                act.wait_ge(dec_diff, h + 1)
                act.activation(dec[:, h % NDEC, :], dec[:, h % NDEC, :], ACT.Exp).then_inc(dec_exp, 1)
                modulation_step()
            act.wait_ge(y_ready, KB)
            act.wait_ge(head_sum, 1)
            act.activation(fT[:, :, :], yT[:, :, :], ACT.Square).then_inc(squares_ready, 1)
            act.wait_ge(head_sum, 2)
            act.activation(rs_root[:, 0:4], bank[4][:, 0:4], ACT.Sqrt, bias=eps_col[:, 0:1],
                           scale=1.0 / (4 * P)).then_inc(head_root, 1)

            def moe(l, k):
                m = M[l]
                norm(k)
                act.wait_ge(m["lmax"], l + 1)
                act.activation(small(1), small(1), ACT.Exp).then_inc(m["lexp"], 1)
                for u in range(4):
                    half, tt = u // 2, u % 2
                    act.wait_ge(m["hN_full"], 4 * l + u + 1)
                    act.activation(hN[:, tt, half * W:(half + 1) * W], bank[4 + u][:], ACT.Copy).then_inc(m["hN_evac"], 1)
                act.wait_ge(m["slot_full"], l + 1)
                for r in range(2):
                    ins = act.activation(rows4[:, 2 * r:2 * r + 2, :].rearrange("p r s -> p (r s)"),
                                         bank[2 + r][:], ACT.Copy)
                ins.then_inc(m["rows_ready"], 1)

                def take_a():
                    act.activation(hgT[:, 0:4, :].rearrange("p k c -> p (k c)"), bank[6][:],
                                   ACT.Copy).then_inc(m["hga_ready"], 1)

                act.wait_ge(m["gath_full"], 1)
                take_a()
                total = act.value_load(tab_i[0:1, NE:NE + 1], min_val=NE // 2, max_val=NE)
                with act.Fori(0, total) as g:
                    act.wait_ge(m["w1_done"], g + 1)
                    act.activation(hsil, bank[4][:], ACT.Silu).then_inc(m["silu_done"], 1)
                    act.wait_ge(m["gath_full"], g + 2)
                    take_a()
                    act.wait_ge(m["hidT_full"], g + 1)
                    act.activation(hidT[:, :, :].rearrange("p f c -> p (f c)"), bank[4][:],
                                   ACT.Copy).then_inc(m["hidT_ready"], 1)
                    act.wait_ge(m["down_half"], g * 2 + 1)
                    act.wait_ge(m["scat_done"], g + 2)
                    act.activation(ymoe[:, 0:W], bank[5][:], ACT.Copy).then_inc(m["y0_ready"], 1)

            if NSUB >= 2:
                moe(0, 1)
            if NSUB >= 3:
                norm(2)
                lora_func = [ACT.Tanh, ACT.Copy, ACT.Sigmoid]
                for i, (dst, bias) in enumerate(((sgT, "od_w_dec0"), (aT, "od_a0"), (ggT, None))):
                    r = P if i == 2 else 64
                    act.wait_ge(lora_full, i + 1)
                    act.activation(lora[i][0:r, :], bank[4][0:r, 0:S], lora_func[i]).then_inc(lora_evac, 1)
                    for u in range(4):
                        n = evac[0]
                        act.wait_ge(proj_full, n + 1)
                        if bias is None:
                            ins = act.activation(dst[:, 2 * u:2 * u + 2, :].rearrange("p k s -> p (k s)"),
                                                 bank[n % 4][:], ACT.Copy)
                        else:
                            for c in range(2):
                                b = 2 * u + c
                                ins = act.activation(dst[:, b, :], bank[n % 4][:, c * S:(c + 1) * S], ACT.Sigmoid,
                                                     bias=col(bias, b))
                        ins.then_inc(proj_evac, 1)
                        evac[0] += 1
                evac_T(k1T, 0)
                evac_T(k1T, 4)
                evac_T(rT, 0)
                evac_T(rT, 4)
                act.wait_ge(head_sum, 3)
                act.activation(rs_root[:], bank[4][:, 0:2 * NH], ACT.Sqrt).then_inc(head_root, 1)
                for j in range(2):
                    for tt in range(NT):
                        evacuate(vN1[:, tt, 8 * j:8 * j + 8, :].rearrange("p h n -> p (h n)"))
                    if j == 0:
                        act.wait_ge(rw_diff, 1)
                        act.activation(buf(10), buf(10), ACT.Exp, scale=-E05).then_inc(rw_exp, 1)
                        act.wait_ge(rw_diff, 2)
                        act.activation(kmid[:], kmid[:], ACT.Exp, scale=E05).then_inc(rw_exp, 1)
                        act.wait_ge(rw_diff, 3)
                        act.activation(buf(3), buf(3), ACT.Exp, scale=-E05).then_inc(rw_exp, 1)
                act.wait_ge(rw_diff, 4)
                act.activation(buf(10), buf(10), ACT.Exp, scale=E05).then_inc(rw_exp, 1)
                for i in range(KB // 2 * 12):
                    jj, r = i // 12, i % 12
                    pr = 2 * jj + r % 2
                    act.wait_ge(tm_full, i + 1)
                    act.activation(tmid(pr), bank[2 + pr % 2][:], ACT.Copy).then_inc(tm_ready, 1)
                    if r == 11:
                        for tt in range(NT):
                            for q in (2 * jj, 2 * jj + 1):
                                act.wait_ge(w_full, 4 * jj + 2 * tt + q % 2 + 1)
                                act.activation(tmid(q)[:, tt * P:(tt + 1) * P], bank[2 + q % 2][:, 0:P],
                                               ACT.Copy).then_inc(w_ready, 1)
                            for q in (2 * jj, 2 * jj + 1):
                                act.wait_ge(u_full, 4 * jj + 2 * tt + q % 2 + 1)
                                act.activation(uneg(q, tt), bank[2 + q % 2][:, P:2 * P], ACT.Copy,
                                               scale=-1.0).then_inc(u_ready, 1)
                act.wait_ge(bcast_used, 12)
                act.activation(buf(3).rearrange("p (k t s) -> p k t s", k=KB, t=NT), oR, ACT.Square).then_inc(squares_ready, 1)
                act.wait_ge(head_sum, 6)
                act.activation(rs_root[:], bank[4][:, 0:2 * NH], ACT.Sqrt, bias=eps_col[:, 1:2],
                               scale=1.0 / HEAD).then_inc(head_root, 1)
            if NSUB >= 4:
                moe(1, 3)
            norm(NSUB)
            for u in range(8):
                q, tt = u // 2, u % 2
                act.wait_ge(o_full, 4 + u + 1)
                act.activation(hN[:, tt, 2 * q * P:(2 * q + 2) * P], bank[u][:, 0:S],
                               ACT.Copy).then_inc(o_evac, 1)

        @block.vector
        def _(dve):
            count = [0]

            def link(ins):
                count[0] += 1
                ins.then_inc(dve_chain, 1)
                dve.wait_ge(dve_chain, count[0])

            tt_ = dve.tensor_tensor
            ts_ = dve.tensor_scalar
            stt = dve.scalar_tensor_tensor

            dve.memset(vrows[:], 0.0).then_inc(vrows_zeroed, 1)
            dve.wait_ge(vec_T, 1)
            dve.tensor_copy(vcols[:].rearrange("p g r -> p (g r)"), bank[4][:, 0:3 * P]).then_inc(vec_cols, 1)
            dve.wait_ge(vec_cols, 1)
            lg = cols("hg_lb_logits", 0, 3 * KB).rearrange("p (r k) -> p r k", r=3)
            link(tt_(lbm[:], lg[:, 0, :], lg[:, 1, :], ALU.max))
            link(tt_(lbm[:], lbm[:], lg[:, 2, :], ALU.max))
            tt_(lbe[:], lg, lbm[:].unsqueeze(1).to_broadcast([P, 3, KB]), ALU.subtract).then_inc(lb_max, 1)
            dve.wait_ge(start_exp, 1)
            link(tt_(lbm[:], lbe[:, 0, :], lbe[:, 1, :], ALU.add))
            link(tt_(lbm[:], lbm[:], lbe[:, 2, :], ALU.add))
            link(dve.reciprocal(lbm[:], lbm[:]))
            link(tt_(lb[:], lbe[:, 1, :], lbm[:], ALU.mult))
            link(ts_(oml[:], lb[:], -1.0, 1.0, ALU.mult, ALU.add))

            def modulation(l, a, b, cols_bank):
                return tt_(modT[:, l, a:b], cols_bank[:, 48 * l + a:48 * l + b],
                           cols("mod_b", 48 * l + a, 48 * l + b), ALU.add)

            def gains(l, f):
                link(ts_(gain[:, l, f, :], modT[:, l, (3 * f + 1) * KB:(3 * f + 2) * KB], 1.0, None, ALU.add))
                link(tt_(gain[:, l, f, :], gain[:, l, f, :], cols("norm_w", (2 * l + f) * KB, (2 * l + f + 1) * KB),
                         ALU.mult))

            def norm_rstd_step(k):
                dve.wait_ge(root_ready, k + 1)
                link(dve.reciprocal(norm_rstd, norm_rstd))

            def norm(k):
                if k:
                    norm_rstd_step(k)
                for b in range(KB):
                    g = col("final_norm_w", b) if k == NSUB else gain[:, k // 2, k % 2, b:b + 1]
                    ins = stt(hT[:, b, :], xT[:, b, :], g, norm_rstd, ALU.mult, ALU.mult)
                    if b % 2:
                        ins.then_inc(h_ready if k == NSUB else scaled, 1)

            def residual(k):
                l, f = k // 2, k % 2
                for b in range(KB):
                    gt = modT[:, l, (3 * f + 2) * KB + b:(3 * f + 2) * KB + b + 1]
                    ins = stt(xT[:, b, :], bank[b // 2][:, (b % 2) * S:(b % 2 + 1) * S], gt, xT[:, b, :],
                              ALU.mult, ALU.add)
                    if b % 2:
                        ins.then_inc(x_ready, 1)

            norm_rstd_step(0)
            dve.wait_ge(mod_cols, MOD_FIRST)
            modulation(0, 0, 4 * MOD_FIRST, bank[5]).then_inc(mod_taken, 1)
            dve.wait_ge(mod_taken, 1)
            gains(0, 0)
            dve.wait_ge(xT_evac, 1)
            norm(0)

            dve.wait_ge(proj_evac, 4)
            for b in range(KB):
                ins = ts_(fT[:, b, :], fT[:, b, :], oml[:, b:b + 1], lb[:, b:b + 1], ALU.mult, ALU.add)
            link(ins)
            ts_(kT[:, :, :], fT[:, :, :], -1.0, 1.0, ALU.mult, ALU.add).then_inc(k_ready, 1)
            dve.wait_ge(consts, 1)
            dve.wait_ge(logf_ready, 1)
            for b in range(KB):
                ins = dve.tensor_tensor_scan(bT[:, b, :], ones[:, 0:S], fT[:, b, :], 0.0, ALU.mult, ALU.add)
            ins.then_inc(b_ready, 1)
            dve.wait_ge(b_ready, 1)

            def level_diff(i):
                h = (HALVES + [P])[i]
                e = buf(eT[i % 2]).rearrange("p (b two h) -> p b two h", two=2, h=h)
                b = buf(5).rearrange("p (b two h) -> p b two h", two=2, h=h)
                if i >= 2:
                    dve.wait_ge(score_full, 4 + 2 * (i - 1))
                mid = b[:, :, 0, h - 1:h].to_broadcast([P, KB * S // (2 * h), h])
                tt_(e[:, :, 1, :], b[:, :, 1, :], mid, ALU.subtract).then_inc(dr_ready, 1)

            def level_mult(i):
                h = (HALVES + [P])[i]
                e = buf(eT[i % 2]).rearrange("p (b two h) -> p b two h", two=2, h=h)
                q = buf(2).rearrange("p (b two h) -> p b two h", two=2, h=h)
                dve.wait_ge(el_exp, i + 1)
                dve.wait_ge(proj_evac, 8)
                tt_(e[:, :, 1, :], e[:, :, 1, :], q[:, :, 1, :], ALU.mult).then_inc(eq_ready, 1)

            def level_take(i):
                h = HALVES[i]
                for tt in range(NT):
                    m = 4 + 2 * i + tt
                    dve.wait_ge(score_full, m + 1)
                    src = bank[4 + m % 2][:].rearrange("p (u s) -> p u s", s=64)
                    dst = scd[:, tt, :, :].rearrange("p u (b two h) -> p u b two h", two=2, h=h)[:, :, :, 1, :]
                    mk = level[:, i, :].rearrange("p (b two h) -> p b two h", two=2, h=h)[:, :, 1, :]
                    ins = dve.copy_predicated(dst, mk.unsqueeze(1).to_broadcast([P, KB, 64 // h, h]).bitcast(I32),
                                              src.rearrange("p u (b h) -> p u b h", h=h))
                    ins.then_inc(score_evac, 1)

            level_diff(0)
            level_diff(1)
            for r in range(2):
                for tt in range(NT):
                    m = 2 * r + tt
                    dve.wait_ge(score_full, m + 1)
                    tt_(scd[:, tt, 4 * r:4 * r + 4, :], bank[4 + m % 2][:].rearrange("p (u s) -> p u s", u=4),
                        ident[:].unsqueeze(1).to_broadcast([P, 4, P]), ALU.mult).then_inc(score_evac, 1)
            dve.wait_ge(score_evac, 4)
            for i in range(8):
                level_mult(i)
                if i < 7:
                    level_take(i)
                if i + 2 < 8:
                    level_diff(i + 2)
                if i == 5:
                    dve.wait_ge(dt_full, 1)
                    dve.wait_ge(small_landed, 16 * 7)
                    ts_(dts[:, 0, :], bank[7][0:NH, 0:S], dt_bias[:], None, ALU.add).then_inc(dtz, 1)
                if i == 6:
                    dve.wait_ge(start_exp, 2)
                    dve.wait_ge(dtln, 1)
                    link(stt(dts[:, 3, :], dts[:, 0, :], 0.0, dts[:, 2, :], ALU.max, ALU.add))
                    link(ts_(dts[:, 2, :], dts[:, 3, :], a_neg[:], -1.0, ALU.mult, ALU.mult))
                    dve.tensor_tensor_scan(dts[:, 4, :], ones[0:NH, 0:S], dts[:, 2, :], 0.0, ALU.mult,
                                           ALU.add).then_inc(dt_ready, 1)
            for r in range(2):
                m = 18 + r
                dve.wait_ge(score_full, m + 1)
                dve.tensor_copy(scx[:, 4 * r:4 * r + 4, :].rearrange("p u s -> p (u s)"),
                                bank[4 + m % 2][:]).then_inc(score_evac, 1)
            dve.wait_ge(mod_cols, 12)
            modulation(0, 4 * MOD_FIRST, 48, bank[6]).then_inc(mod_taken, 1)
            dve.wait_ge(mod_taken, 2)
            gains(0, 1)
            dve.wait_ge(proj_evac, 18)
            for b in range(XBLK):
                tmp = ctmp[:, b % 2, :]
                wt = lambda j: col("ev_conv_w", j * XBLK + b)
                link(ts_(tmp, xpad[:, b, 0:S], wt(0), col("ev_conv_b", b), ALU.mult, ALU.add))
                for j in range(1, TAPS - 1):
                    link(stt(tmp, xpad[:, b, j:j + S], wt(j), tmp, ALU.mult, ALU.add))
                stt(xpad[:, b, TAPS - 1:], xpad[:, b, TAPS - 1:], wt(TAPS - 1), tmp, ALU.mult,
                    ALU.add).then_inc(conv_done, 1)
            dve.wait_ge(dtN_full, 1)
            dve.tensor_copy(dtN[:].rearrange("p a t h -> p (a t h)"), bank[4][:, 0:4 * NH]).then_inc(dtN_ready, 1)
            dve.wait_ge(dtN_ready, 1)
            for u in range(4):
                tt, half = u // 2, u % 2
                dve.wait_ge(xs_full, u + 1)
                tt_(xdt[:, tt, half * W:(half + 1) * W].rearrange("p (h n) -> p h n", n=HEAD),
                    bank[[5, 6, 7, 5][u]][:].rearrange("p (h n) -> p h n", n=HEAD),
                    dtN[:, 0, tt, 8 * half:8 * half + 8].unsqueeze(2).to_broadcast([P, 8, HEAD]),
                    ALU.mult).then_inc(xdt_ready, 1)
            for g in range(GROUPS):
                dve.wait_ge(cb_full, g + 1)
                ps = bank[6 + g]
                tt_(cbm[:, g, 0:P], ps[:, 0:P], causal[:], ALU.mult)
                tt_(cbm[:, g, 2 * P:3 * P], ps[:, S:S + P], causal[:], ALU.mult)
                dve.tensor_copy(cbm[:, g, P:S], ps[:, P:S]).then_inc(cb_ready, 1)
            dve.wait_ge(head_root, 1)
            dve.reciprocal(rstd[:, 0:2 * KB], rs_root[:, 0:2 * KB]).then_inc(head_rstd, 1)
            dve.wait_ge(silu_g, 1)
            for u in range(4):
                dve.wait_ge(head_bcast, u + 1)
                o = oa[:, 2 * u:2 * u + 2, :].rearrange("p k s -> p (k s)")
                ins = tt_(o, o, bank[4 + u % 2][:], ALU.mult)
                ins.then_inc(bcast_used, 1)
            dve.wait_ge(bcast_used, 4)
            for h in range(KB):
                ins = stt(oa[:, h, :], oa[:, h, :], col("ev_hg_norm", h), gT[:, h, :], ALU.mult, ALU.mult)
            ins.then_inc(oa_ready, 1)

            def decay_diff(h):
                dve.wait_ge(row_full, h + 1)
                if h >= NDEC:
                    dve.wait_ge(y_full, h - NDEC + 1)
                row = bank[4 + h % 2]
                dd = dec[:, h % NDEC, :]
                ts_(dd[:, 0:S], row[:, 0:S], dtN[:, 1, 0, h:h + 1], 0.0, ALU.subtract, ALU.min)
                ts_(dd[:, S:S + P], row[:, P:S], dtN[:, 1, 1, h:h + 1], 0.0, ALU.subtract,
                    ALU.min).then_inc(dec_diff, 1)

            def decay_mult(h):
                dve.wait_ge(dec_exp, h + 1)
                dd = dec[:, h % NDEC, :]
                tt_(dd, dd, cbm[:, h // 8, :], ALU.mult).then_inc(dec_mat, 1)

            def ssd_out(pr):
                dve.wait_ge(y_full, 2 * pr + 2)
                link(stt(yT[:, pr, :], xpad[:, pr, TAPS - 1:], dskip[:, pr:pr + 1], bank[6 + pr % 2][:, 0:S],
                         ALU.mult, ALU.add))
                tt_(yT[:, pr, :], yT[:, pr, :], zT[:, pr, :], ALU.mult).then_inc(y_ready, 1)

            dve.wait_ge(cb_ready, 2)
            for h in range(NH + 4):
                if h < NH:
                    decay_diff(h)
                if 1 <= h <= NH:
                    decay_mult(h - 1)
                if h >= 4 and h % 2 == 1:
                    ssd_out((h - 4) // 2)
            dve.wait_ge(mod_cols, 24)
            modulation(1, 0, 48, bank[2]).then_inc(mod_taken, 1)
            dve.wait_ge(mod_taken, 3)
            gains(1, 0)
            gains(1, 1)
            dve.wait_ge(head_root, 2)
            dve.reciprocal(rstd[:, 0:4], rs_root[:, 0:4]).then_inc(head_rstd, 1)
            dve.wait_ge(yb_full, 1)
            for b in range(KB):
                g = b // 4
                ins = stt(yT[:, b, :], yT[:, b, :], col("ev_ssm_norm", b), bank[5][:, g * S:(g + 1) * S],
                          ALU.mult, ALU.mult)
            ins.then_inc(ob_ready, 1)
            dve.wait_ge(tile_used, USED[0])
            residual(0)

            def first_of(dst, vals, top, shape, scratch):
                link(tt_(dst, vals, top, ALU.is_equal))
                link(ts_(scratch[0], dst, -4.0, 4.0, ALU.mult, ALU.add))
                link(tt_(scratch[0], scratch[0], shape[0], ALU.add))
                link(dve.tensor_reduce(scratch[1], scratch[0], AX.X, ALU.min))
                link(tt_(dst, shape[0], scratch[1].unsqueeze(len(scratch[1].shape)).to_broadcast(shape[1]),
                         ALU.is_equal))

            def moe(l, k):
                m = M[l]
                norm(k)
                v3 = lambda i: small(i).rearrange("p (t e) -> p t e", t=NT)
                v8 = lambda i: small(i).rearrange("p (a e) -> p a e", e=4)
                dve.wait_ge(m["logit_full"], l + 1)
                dve.wait_ge(small_landed, 16 * 7)
                link(tt_(v3(0), bank[0][:, 0:2 * NE].rearrange("p (t e) -> p t e", t=NT),
                         router_b[:].unsqueeze(1).to_broadcast([P, NT, NE]), ALU.add))
                mx = small(20)[:, 0:2]
                link(dve.tensor_reduce(mx, v3(0), AX.X, ALU.max))
                tt_(v3(1), v3(0), mx.unsqueeze(2).to_broadcast([P, NT, NE]), ALU.subtract).then_inc(m["lmax"], 1)
                dve.wait_ge(m["lexp"], l + 1)
                sm = small(20)[:, 2:4]
                link(dve.tensor_reduce(sm, v3(1), AX.X, ALU.add))
                link(dve.reciprocal(sm, sm))
                link(tt_(v3(2), v3(1), sm.unsqueeze(2).to_broadcast([P, NT, NE]), ALU.mult))
                p8 = v8(2)
                pos = tie4[:].unsqueeze(1).to_broadcast([P, 8, 4])
                t1, t2 = small(20)[:, 8:16], small(20)[:, 16:24]
                scr = (v8(5), small(20)[:, 24:32])
                b8 = lambda x: x.unsqueeze(2).to_broadcast([P, 8, 4])
                link(dve.tensor_reduce(t1, p8, AX.X, ALU.max))
                first_of(v8(3), p8, b8(t1), (pos, [P, 8, 4]), scr)
                link(stt(v8(6), v8(3), -2.0, p8, ALU.mult, ALU.add))
                link(dve.tensor_reduce(t2, v8(6), AX.X, ALU.max))
                first_of(v8(4), v8(6), b8(t2), (pos, [P, 8, 4]), scr)
                gs = small(21)[:, 0:8].rearrange("p (t g) -> p t g", t=NT)
                gm = small(21)[:, 8:16].rearrange("p (t g) -> p t g", t=NT)
                gx = small(21)[:, 16:18]
                pos2 = tie4[:].unsqueeze(1).to_broadcast([P, NT, 4])
                scr2 = (small(21)[:, 20:28].rearrange("p (t g) -> p t g", t=NT), small(21)[:, 28:30])
                link(tt_(small(21)[:, 0:8], t1, t2, ALU.add))
                link(dve.tensor_reduce(gx, gs, AX.X, ALU.max))
                first_of(gm, gs, gx.unsqueeze(2).to_broadcast([P, NT, 4]), (pos2, [P, NT, 4]), scr2)
                gmb = b8(small(21)[:, 8:16])
                link(tt_(v8(3), v8(3), gmb, ALU.mult))
                link(tt_(v8(4), v8(4), gmb, ALU.mult))
                tt_(small(8), small(3), small(4), ALU.add).then_inc(m["sel_ready"], 1)
                ga, gb_ = small(22)[:, 0:2], small(22)[:, 2:4]
                link(tt_(small(6), small(3), small(2), ALU.mult))
                link(dve.tensor_reduce(ga, v3(6), AX.X, ALU.add))
                link(tt_(small(6), small(4), small(2), ALU.mult))
                link(dve.tensor_reduce(gb_, v3(6), AX.X, ALU.add))
                gsum = small(22)[:, 4:6]
                link(tt_(gsum, ga, gb_, ALU.add))
                link(dve.reciprocal(gsum, gsum))
                link(tt_(tok4[:, :, 2], ga, gsum, ALU.mult))
                link(tt_(tok4[:, :, 3], gb_, gsum, ALU.mult))
                dve.wait_ge(m["rank_full"], l + 1)
                cnt = bank[1][:, 2 * NE:3 * NE]
                need = small(22)[:, 8:8 + NE]
                link(ts_(need, cnt, float(C), 1.0, ALU.is_gt, ALU.add))
                for c in range(2, S // C):
                    link(stt(need, cnt, float(c * C), need, ALU.is_gt, ALU.add))
                nblk, base = tab_f[:, 0:NE // 2], tab_f[:, NE // 2:NE]
                base_odd = tab_f[:, 2 * NE:2 * NE + NE // 2]
                link(dve.tensor_reduce(nblk, need.rearrange("p (i e) -> p i e", e=2), AX.X, ALU.max))
                link(dve.tensor_tensor_scan(base, ones[:, 0:NE // 2], nblk, 0.0, ALU.mult, ALU.add))
                link(dve.tensor_copy(tab_f[:, NE:NE + 1], tab_f[:, NE - 1:NE]))
                link(tt_(base, base, nblk, ALU.subtract))
                dve.tensor_copy(tab_i[:, 0:NE + 1], tab_f[0:1, 0:NE + 1]).then_inc(m["tab_ready"], 1)
                rank = bank[1][:, 0:2 * NE]
                over = small(7)
                ts_(base_odd, base, 0.5, None, ALU.add)
                link(ts_(over, rank, C - 0.5, None, ALU.is_gt))
                for c in range(2, S // C):
                    link(stt(over, rank, c * C - 0.5, over, ALU.is_gt, ALU.add))
                link(stt(small(6), over, float(C), rank, ALU.mult, ALU.add))
                pairs = small(6).rearrange("p (t i e) -> p t i e", t=NT, e=2)
                for e in range(2):
                    ins = stt(pairs[:, :, :, e], (base, base_odd)[e].unsqueeze(1).to_broadcast([P, NT, NE // 2]),
                              float(P), pairs[:, :, :, e], ALU.mult, ALU.add)
                link(ins)
                for r in range(2):
                    link(tt_(small(7), small(3 + r), small(6), ALU.mult))
                    dve.tensor_reduce(tok4[:, :, r], v3(7), AX.X, ALU.add).then_inc(m["slots_ready"], 1)
                    dve.wait_ge(m["slots_ready"], 2 * l + r + 1)
                dve.memset(spread, 0.0).then_inc(m["spread_ready"], 1)
                dve.memset(ymoe[:, 0:W], 0.0).then_inc(m["y0_ready"], 1)
                dve.memset(ymoe[:, W:D], 0.0).then_inc(m["y1_ready"], 1)
                link(dve.tensor_copy(pcol[:], pcol0[:]))

                def pick_step(wait_for):
                    for tt in range(NT):
                        ts_(pick2[:, tt, :], iota[:], tok4[:, tt, 1:2], None, ALU.is_equal)
                        ins = ts_(pick[:, tt, :], iota[:], tok4[:, tt, 0:1], None, ALU.is_equal)
                    wait_for(ins)
                    return tt_(pick, pick, pick2, ALU.add)

                def take_b():
                    dve.tensor_copy(hgT[:, 4:8, :].rearrange("p k c -> p (k c)"), bank[7][:]).then_inc(m["hgb_ready"], 1)

                pick_step(link).then_inc(m["pick_ready"], 1)
                dve.wait_ge(m["slot_full"], l + 1)
                link(ts_(tok4[:, :, 0:2], tok4[:, :, 0:2], -float(P), None, ALU.add))
                dve.wait_ge(m["rows_ready"], l + 1)
                dve.wait_ge(m["tab_ready"], l + 1)
                total = dve.value_load(tab_i[0:1, NE:NE + 1], min_val=NE // 2, max_val=NE)
                dve.wait_ge(m["gath_full"], 1)
                take_b()
                pick_step(link).then_inc(m["pick_ready"], 1)
                link(ts_(tok4[:, :, 0:2], tok4[:, :, 0:2], -float(P), None, ALU.add))
                steps = 4
                with dve.Fori(0, total) as g:
                    def after(ins, n):
                        ins.then_inc(m["chain"], 1)
                        dve.wait_ge(m["chain"], g * steps + (n + 1))

                    dve.wait_ge(m["silu_done"], g + 1)
                    dve.wait_ge(m["w3_done"], g + 1)
                    tt_(hid, hsil, bank[5][:], ALU.mult).then_inc(m["hid_ready"], 1)
                    dve.wait_ge(m["gath_full"], g + 2)
                    take_b()
                    pick_step(lambda ins: after(ins, 0)).then_inc(m["pick_ready"], 1)
                    after(ts_(tok4[:, :, 0:2], tok4[:, :, 0:2], -float(P), None, ALU.add), 1)
                    stt(spread2, rows4[:, 1, :], pcol[:], rows4[:, 3, :], ALU.is_equal, ALU.mult)
                    dve.wait_ge(m["scat_done"], g + 2)
                    after(stt(spread, rows4[:, 0, :], pcol[:], rows4[:, 2, :], ALU.is_equal, ALU.mult), 2)
                    tt_(spread, spread, spread2, ALU.add).then_inc(m["spread_ready"], 1)
                    after(ts_(pcol[:], pcol[:], float(P), None, ALU.add), 3)
                    dve.wait_ge(m["down_half"], g * 2 + 2)
                    dve.tensor_copy(ymoe[:, W:D], bank[6][:]).then_inc(m["y1_ready"], 1)
                dve.wait_ge(m["scat_done"], total + 2)
                residual(k)

            if NSUB >= 2:
                moe(0, 1)
            if NSUB >= 3:
                norm(2)
                def mix_used(n):
                    return (lora_full, n + 1) if n < 3 else (proj_full, FULL_LORA + 4 * (n - 3) + 4)

                dve.wait_ge(h_ready, 12)
                for n, i in enumerate((3, 4, 5, 1, 0, 2)):
                    if n >= 2:
                        dve.wait_ge(*mix_used(n - 2))
                    for b in range(KB):
                        if n == 0 and b % 2 == 0:
                            tt_(xx[:, b:b + 2, 1:S], hT[:, b:b + 2, 0:S - 1], hT[:, b:b + 2, 1:S], ALU.subtract)
                            link(ts_(xx[:, b:b + 2, 0:1], hT[:, b:b + 2, 0:1], -1.0, None, ALU.mult))
                        ins = stt(mixed[n % 2][:, b, :], xx[:, b, :], col("od_mu", i * KB + b), hT[:, b, :],
                                  ALU.mult, ALU.add)
                        if n == 0 and b in (1, 3, 5):
                            ins.then_inc(mix_ready, 1)
                    ins.then_inc(mix_ready, 1)
                    if n == 3:
                        dve.wait_ge(proj_evac, 26 + 4)
                        dve.memset(cum[:, :, 0:1], 0.0)
                        for b in range(KB):
                            ins = dve.tensor_tensor_scan(cum[:, b, 1:], ones[:, 0:S], sgT[:, b, :], 0.0,
                                                         ALU.mult, ALU.add)
                        ins.then_inc(cum_ready, 1)
                def exponents(dst, shift, signal):
                    for tt in range(NT):
                        mid = cum[:, :, tt * P + MID:tt * P + MID + 1].to_broadcast([P, KB, P])
                        ins = tt_(by_tile(dst)[:, :, tt, :], cum[:, :, shift + tt * P:shift + (tt + 1) * P], mid,
                                  ALU.subtract)
                    ins.then_inc(signal, 1)

                dve.wait_ge(cum_ready, 1)
                exponents(10, 0, rw_diff)
                tt_(kmid[:], cum[:, :, MID], cum[:, :, P + MID], ALU.subtract).then_inc(rw_diff, 1)
                dve.wait_ge(proj_evac, 26 + 12 + 4)
                for b in range(KB):
                    ins = ts_(kkT[:, b, :], k1T[:, b, :], col("od_k_k", b), None, ALU.mult)
                link(ins)
                tt_(buf(1), buf(11), buf(11), ALU.mult).then_inc(sums_in, 1)
                for b in range(KB):
                    ins = ts_(xx[:, b, :], aT[:, b, :], -1.0, col("od_k_a", b), ALU.add, ALU.mult)
                link(ins)
                for b in range(KB):
                    ins = stt(k1T[:, b, :], xx[:, b, :], 1.0, k1T[:, b, :], ALU.add, ALU.mult)
                link(ins)
                dve.wait_ge(*mix_used(4))
                exponents(3, 1, rw_diff)
                dve.wait_ge(proj_evac, 26 + 12 + 8)
                for b in range(KB):
                    ins = stt(xx[:, b, :], rT[:, b, :], col("od_r_k", b), k1T[:, b, :], ALU.mult, ALU.mult)
                ins.then_inc(sums_in, 1)
                dve.wait_ge(head_root, 3)
                link(ts_(rs_root[:], rs_root[:], 1e-12, None, ALU.max))
                dve.reciprocal(rstd[:], rs_root[:]).then_inc(head_rstd, 1)

                def take_rows(n):
                    dve.wait_ge(hrow_full, n + 1)
                    dve.tensor_copy(hrows, bank[4][0:NH, P:P + S]).then_inc(hrow_evac, 1)

                take_rows(0)
                for u in range(4):
                    dve.wait_ge(head_bcast, u + 5)
                    v = kkT[:, 2 * u:2 * u + 2, :].rearrange("p k s -> p (k s)")
                    tt_(v, v, bank[6 + u % 2][:], ALU.mult).then_inc(bcast_used, 1)
                dve.wait_ge(head_sum, 4)
                dve.tensor_copy(beta[:], bank[5][:, 0:2 * NH])
                dve.wait_ge(bcast_used, 8)
                dve.wait_ge(rw_exp, 1)
                tt_(AR[:, :, :, 0, :], by_tile(11), by_tile(10), ALU.mult).then_inc(rw_ops, 1)
                link(tt_(buf(8), buf(8), buf(11), ALU.mult))
                dve.wait_ge(rw_ops, 1)
                exponents(10, 1, rw_diff)
                dve.wait_ge(rw_exp, 3)
                tt_(AR[:, :, :, 1, :], by_tile(5), by_tile(3), ALU.mult).then_inc(rw_ops, 1)
                dve.wait_ge(rw_exp, 4)
                tt_(buf(8), buf(8), buf(10), ALU.mult).then_inc(rw_ops, 1)
                tt_(buf(6), buf(6), buf(10), ALU.mult).then_inc(rw_ops, 1)
                dve.wait_ge(rw_ops, 4)

                def u4(x):
                    return x.rearrange("p (u s) -> p u s", s=P)

                def take_scores(pr):
                    n = 6 * pr
                    for which, keys in ((0, rwK), (1, rwB)):
                        ins = ts_(kcross(pr, which), keys[:, pr, 0, :], kmid[:, pr:pr + 1], None, ALU.mult)
                    ins.then_inc(kc_ready, 1)
                    for kind in range(2):
                        for hh in range(2):
                            dve.wait_ge(rsc_full, n + 2 * kind + hh + 1)
                            ps = bank[hh][:].rearrange("p (t a s) -> p t a s", t=2, a=2)
                            to_a, to_r = (part(pr, (2 * kind + a) * 4, 4).rearrange(
                                "p (t h s) -> p t h s", t=2, h=2)[:, :, hh, :] for a in range(2))
                            two = lambda mask: mask[:].unsqueeze(1).to_broadcast([P, 2, P])
                            ins = stt(to_a, ps[:, :, 0, :], -1.0 if kind else 1.0, two(strict), ALU.mult, ALU.mult)
                            if kind and hh:
                                ins.then_inc(lt_ready, 1)
                            tt_(to_r, ps[:, :, 1, :], two(causal), ALU.mult).then_inc(rsc_evac, 1)
                    dve.wait_ge(lt_ready, pr + 1)
                    link(tt_(u4(xinvT(pr)), u4(part(pr, 8, 4)), level[:, 0:1, :].to_broadcast([P, 4, P]), ALU.mult))
                    tt_(u4(xinvT(pr)), u4(xinvT(pr)), ident[:].unsqueeze(1).to_broadcast([P, 4, P]),
                        ALU.add).then_inc(xt1_ready, 1)
                    for hh in range(2):
                        dve.wait_ge(rsc_full, n + 4 + hh + 1)
                        dve.tensor_copy(part(pr, 16, 8).rearrange("p (q h s) -> p q h s", q=4, h=2)[:, :, hh, :],
                                        u4(bank[hh][:])).then_inc(rsc_evac, 1)

                for pr in range(2):
                    take_scores(pr)
                for jj in range(KB // 2):
                    prs = (2 * jj, 2 * jj + 1)
                    for pr in prs:
                        dve.wait_ge(x1_full, pr + 1)
                        dve.tensor_copy(xinv(pr), bank[4 + 2 * (pr % 2)][:]).then_inc(x1_ready, 1)
                    for i in range(1, 7):
                        for pr in prs:
                            n = jj * 12 + 2 * (i - 1) + pr % 2
                            if i < 6:
                                dve.wait_ge(xi_full, xi(jj, i, pr) + 1)
                                if i == 1:
                                    dve.wait_ge(x1_ready, pr + 1)
                                else:
                                    dve.wait_ge(xi_ready, xi(jj, i - 1, pr) + 1)
                                tt_(xinv(pr), xinv(pr), bank[4 + 2 * (pr % 2)][:], ALU.add).then_inc(xi_ready, 1)
                            dve.wait_ge(xm_full, n + 1)
                            if i == 1:
                                dve.wait_ge(xt1_ready, pr + 1)
                            else:
                                dve.wait_ge(xm_ready, n - 1)
                            tt_(xinvT(pr), xinvT(pr), bank[5 + 2 * (pr % 2)][:], ALU.add).then_inc(xm_ready, 1)
                    if jj < KB // 2 - 1:
                        for pr in (2 * jj + 2, 2 * jj + 3):
                            take_scores(pr)
                    for pr in prs:
                        dve.wait_ge(ry_full, pr + 1)
                        dve.tensor_copy(oR[:, pr, :, :], bank[4 + 2 * (pr % 2)][:, 0:S].rearrange(
                            "p (t s) -> p t s", t=NT)).then_inc(ry_ready, 1)

                dve.wait_ge(ry_ready, KB)
                tt_(bvN, vN1, beta[:].rearrange("p (t h) -> p t h", t=NT).unsqueeze(3).to_broadcast(
                    [P, NT, NH, HEAD]), ALU.mult).then_inc(bv_ready, 1)
                dve.wait_ge(head_sum, 5)
                ts_(gm_mean[:], bank[4][:, 0:2 * NH], 1.0 / HEAD, None, ALU.mult).then_inc(gn_mean, 1)
                take_rows(1)
                four = lambda x: x.rearrange("p (k t s) -> p k t s", k=2, t=NT)
                for u in range(4):
                    dve.wait_ge(head_bcast, u + 9)
                    v = oR[:, 2 * u:2 * u + 2, :, :]
                    tt_(v, v, four(bank[6 + u % 2][:]), ALU.subtract).then_inc(bcast_used, 1)
                dve.wait_ge(head_root, 4)
                dve.reciprocal(rstd[:], rs_root[:]).then_inc(head_rstd, 1)
                take_rows(2)
                for u in range(4):
                    dve.wait_ge(head_bcast, u + 13)
                    v = oR[:, 2 * u:2 * u + 2, :, :]
                    tt_(v, v, four(bank[6 + u % 2][:]), ALU.mult).then_inc(bcast_used, 1)
                dve.wait_ge(bcast_used, 16)
                og = by_tile(4)
                for b in range(KB):
                    ins = ts_(og[:, b, :, :], oR[:, b, :, :], col("od_ln_w", b), col("od_ln_b", b), ALU.mult, ALU.add)
                link(ins)
                dve.wait_ge(bvT_full, 1)
                for b in range(0, KB, 2):
                    v = blocks(4)[:, b:b + 2, :].rearrange("p k s -> p (k s)")
                    ins = tt_(v, v, bank[b // 2][:], ALU.add)
                link(ins)
                tt_(buf(4), buf(4), buf(9), ALU.mult).then_inc(og_ready, 1)
                dve.wait_ge(tile_used, USED[1])
                residual(2)
            if NSUB >= 4:
                moe(1, 3)
            norm(NSUB)


INPUTS = ["x", "c", "mod_w", "mod_b", "norm_w", "hg_lb_logits", "ev_w_in", "ev_hg_norm", "ev_conv_w", "ev_conv_b",
          "ev_dt_bias", "ev_a_log", "ev_d_skip", "ev_ssm_norm", "ev_w_out", "od_mu", "od_w_rkv", "od_w_dec0",
          "od_w_dec1", "od_w_dec2", "od_a0", "od_a1", "od_a2", "od_g1", "od_g2", "od_k_k", "od_k_a", "od_r_k",
          "od_ln_w", "od_ln_b", "od_w_o", "router_w", "router_b", "moe_w1", "moe_w3", "moe_w2", "final_norm_w"]


def kernel(**inputs):
    import numpy as np
    import concourse.bacc as bacc
    from concourse.bass_utils import run_bass_kernel_spmd as run

    nc = bacc.Bacc("TRN2", target_bir_lowering=False, num_devices=1, dynamic_dma_scratch_size=1024)
    arrays, args = {}, {}
    for name in INPUTS:
        a = np.ascontiguousarray(inputs[name])
        arrays[f"in_{name}"] = a
        args[name] = nc.dram_tensor(f"in_{name}", a.shape, mybir.dt.from_np(a.dtype), kind="ExternalInput").ap()
    out = nc.dram_tensor("out_0", (1, S, D), F32, kind="ExternalOutput").ap()
    trunk(nc, args, out)
    r = run(nc, [arrays], core_ids=[0])
    return r.results[0]["out_0"]
```
